# Optimizing a Trainium2 kernel written in Bass

```python
import jax, jax.numpy as jnp
from jax import lax
import numpy as np

D_MODEL = 1024
BATCH = 1
SEQ = 1024
DEPTH = 2
DEC_BATCH = 1
DEC_SEQ = 32
PAST_LEN = 512

CHUNK = 64
N_META = 16
Q_BLOCK = 128
N_A = DEPTH // 2
N_B = DEPTH - N_A
A_HEADS = 8
A_HEAD_DIM = 128
A_WIDTH = A_HEADS * A_HEAD_DIM
A_IN = 4 * A_WIDTH + A_HEADS
FORGET_BIAS_INIT = 3.0
B_HEADS = 8
QK_NOPE = 128
QK_ROPE = 64
V_HEAD = 128
KV_LORA = 256
Q_LORA = 384
B_WIDTH = B_HEADS * V_HEAD
B_IN = Q_LORA + B_WIDTH
MLA_SCALE = (QK_NOPE + QK_ROPE) ** -0.5
ROPE_BASE = 10000.0
EPS = 1e-6
NEG = -1e30

kernel_name = 'yoco_fox_mla_streaming_encoder'

def rmsnorm(x, g):
    xf = x.astype(jnp.float32)
    y = xf * lax.rsqrt(jnp.mean(xf * xf, axis=-1, keepdims=True) + EPS)
    return (y * g.astype(jnp.float32)).astype(x.dtype)

def rope(x, pos):
    half = QK_ROPE // 2
    inv = ROPE_BASE ** (-jnp.arange(half, dtype=jnp.float32) / half)
    ang = pos.astype(jnp.float32)[:, None] * inv[None, :]
    cos = jnp.cos(ang)[None, :, None, :]
    sin = jnp.sin(ang)[None, :, None, :]
    xf = x.astype(jnp.float32)
    x1, x2 = xf[..., :half], xf[..., half:]
    return jnp.concatenate([x1 * cos - x2 * sin, x1 * sin + x2 * cos], axis=-1).astype(x.dtype)

def to_blocks(a):
    b, lp = a.shape[:2]
    return jnp.moveaxis(a.reshape((b, lp // Q_BLOCK, Q_BLOCK) + a.shape[2:]), 1, 0)

def from_blocks(o, width):
    o = jnp.moveaxis(o, 0, 1)
    return o.reshape(o.shape[0], o.shape[1] * o.shape[2], width)

def fox_project(h, w_in, b_f):
    p = h @ w_in
    q, k, v, f, g = jnp.split(p, [A_WIDTH, 2 * A_WIDTH, 3 * A_WIDTH, 3 * A_WIDTH + A_HEADS], axis=-1)
    shp = h.shape[:2] + (A_HEADS, A_HEAD_DIM)
    logf = jax.nn.log_sigmoid(f.astype(jnp.float32) + b_f.astype(jnp.float32))
    return q.reshape(shp), k.reshape(shp), v.reshape(shp), logf, g

def fox_core(q, k, v, fq, fk, mask):
    decay = jnp.swapaxes(fq, 1, 2)[:, :, :, None] - jnp.swapaxes(fk, 1, 2)[:, :, None, :]
    logits = jnp.einsum('bqhd,bkhd->bhqk', q, k).astype(jnp.float32) * (A_HEAD_DIM ** -0.5) + decay
    logits = jnp.where(mask, logits, NEG)
    p = jax.nn.softmax(logits, axis=-1).astype(v.dtype)
    return jnp.einsum('bhqk,bkhd->bqhd', p, v)

def mla_shared_latent(x, kv_norm, w_dkv, kv_lat_norm, pos):
    ckr = rmsnorm(x, kv_norm) @ w_dkv
    c = rmsnorm(ckr[..., :KV_LORA], kv_lat_norm)
    kr = rope(ckr[..., KV_LORA:][:, :, None, :], pos)[:, :, 0, :]
    return c, kr

def mla_expand(c, w_ukv):
    kv = (c @ w_ukv).reshape(c.shape[:2] + (B_HEADS, QK_NOPE + V_HEAD))
    return kv[..., :QK_NOPE], kv[..., QK_NOPE:]

def mla_core(q_nope, q_rope, k_nope, k_rope, v, mask):
    logits = (jnp.einsum('bqhn,bkhn->bhqk', q_nope, k_nope)
              + jnp.einsum('bqhr,bkr->bhqk', q_rope, k_rope)).astype(jnp.float32) * MLA_SCALE
    if mask is not None:
        logits = jnp.where(mask, logits, NEG)
    p = jax.nn.softmax(logits, axis=-1).astype(v.dtype)
    return jnp.einsum('bhqk,bkhv->bqhv', p, v)

def setup_inputs(seed: int = 0) -> dict:
    key = jax.random.key(seed)
    ks = jax.random.split(key, 22)

    def nrm(k, shape, scale=1.0):
        return scale * jax.random.normal(k, shape, jnp.float32)

    return {
        'x_prompt': nrm(ks[0], (BATCH, SEQ, D_MODEL)),
        'x_sample': nrm(ks[1], (DEC_BATCH, DEC_SEQ, D_MODEL)),
        'cache_fox_k': nrm(ks[2], (N_A, DEC_BATCH, PAST_LEN, A_HEADS, A_HEAD_DIM)),
        'cache_fox_v': nrm(ks[3], (N_A, DEC_BATCH, PAST_LEN, A_HEADS, A_HEAD_DIM)),
        'cache_fox_logf': jax.nn.log_sigmoid(FORGET_BIAS_INIT + nrm(ks[4], (N_A, DEC_BATCH, PAST_LEN, A_HEADS))),
        'cache_mla_ckv': nrm(ks[5], (DEC_BATCH, PAST_LEN, KV_LORA)),
        'cache_mla_krope': nrm(ks[6], (DEC_BATCH, PAST_LEN, QK_ROPE)),
        'meta': nrm(ks[7], (N_META, D_MODEL)),
        'a_norm': 1.0 + nrm(ks[8], (N_A, D_MODEL), 0.02),
        'a_w_in': nrm(ks[9], (N_A, D_MODEL, A_IN), D_MODEL ** -0.5),
        'a_b_forget': FORGET_BIAS_INIT + nrm(ks[10], (N_A, A_HEADS), 0.5),
        'a_w_out': nrm(ks[11], (N_A, A_WIDTH, D_MODEL), A_WIDTH ** -0.5),
        'kv_norm': 1.0 + nrm(ks[12], (D_MODEL,), 0.02),
        'w_dkv': nrm(ks[13], (D_MODEL, KV_LORA + QK_ROPE), D_MODEL ** -0.5),
        'kv_lat_norm': 1.0 + nrm(ks[14], (KV_LORA,), 0.02),
        'w_ukv': nrm(ks[15], (KV_LORA, B_HEADS * (QK_NOPE + V_HEAD)), KV_LORA ** -0.5),
        'b_norm': 1.0 + nrm(ks[16], (N_B, D_MODEL), 0.02),
        'b_w_in': nrm(ks[17], (N_B, D_MODEL, B_IN), D_MODEL ** -0.5),
        'b_q_norm': 1.0 + nrm(ks[18], (N_B, Q_LORA), 0.02),
        'b_w_uq': nrm(ks[19], (N_B, Q_LORA, B_HEADS * (QK_NOPE + QK_ROPE)), Q_LORA ** -0.5),
        'b_w_out': nrm(ks[20], (N_B, B_WIDTH, D_MODEL), B_WIDTH ** -0.5),
        'final_norm': 1.0 + nrm(ks[21], (D_MODEL,), 0.02),
    }

def reference(x_prompt, x_sample, cache_fox_k, cache_fox_v, cache_fox_logf, cache_mla_ckv, cache_mla_krope,
              meta, a_norm, a_w_in, a_b_forget, a_w_out, kv_norm, w_dkv, kv_lat_norm, w_ukv,
              b_norm, b_w_in, b_q_norm, b_w_uq, b_w_out, final_norm):

    def trunk(x, pos, fox_attend, mla_context):
        fox_k, fox_v, fox_lf = [], [], []
        for l in range(DEPTH):
            if l < N_A:
                h = rmsnorm(x, a_norm[l])
                q, k, v, logf, g = fox_project(h, a_w_in[l], a_b_forget[l])
                o = fox_attend(l, q, k, v, logf)
                x = x + (o * jax.nn.silu(g)) @ a_w_out[l]
                fox_k.append(k)
                fox_v.append(v)
                fox_lf.append(logf)
            else:
                if l == N_A:
                    c_new, kr_new = mla_shared_latent(x, kv_norm, w_dkv, kv_lat_norm, pos)
                    mla_attend = mla_context(c_new, kr_new)
                i = l - N_A
                p = rmsnorm(x, b_norm[i]) @ b_w_in[i]
                q = (rmsnorm(p[..., :Q_LORA], b_q_norm[i]) @ b_w_uq[i]).reshape(
                    x.shape[:2] + (B_HEADS, QK_NOPE + QK_ROPE))
                o = mla_attend(q[..., :QK_NOPE], rope(q[..., QK_NOPE:], pos))
                x = x + (o * jax.nn.silu(p[..., Q_LORA:])) @ b_w_out[i]
        return rmsnorm(x, final_norm), jnp.stack(fox_k), jnp.stack(fox_v), jnp.stack(fox_lf), c_new, kr_new

    bsz, seq = x_prompt.shape[:2]
    L = N_META + seq
    Lp = -(-L // Q_BLOCK) * Q_BLOCK
    nb = Lp // Q_BLOCK
    xp = jnp.concatenate([
        jnp.broadcast_to(meta.astype(x_prompt.dtype)[None], (bsz, N_META, D_MODEL)),
        x_prompt,
        jnp.zeros((bsz, Lp - L, D_MODEL), x_prompt.dtype)], axis=1)
    pos_p = jnp.arange(Lp)
    cid_p = (pos_p - N_META) // CHUNK

    def fox_attend_prompt(l, q, k, v, logf):
        fcum = jnp.cumsum(logf, axis=1)

        def blk(a):
            qb, fqb, qpos = a
            return fox_core(qb, k, v, fqb, fcum, pos_p[None, :] <= qpos[:, None])

        o = lax.map(blk, (to_blocks(q), to_blocks(fcum), pos_p.reshape(nb, Q_BLOCK)))
        return from_blocks(o, A_WIDTH)

    def mla_context_prompt(c, kr):
        k_nope, v = mla_expand(c, w_ukv)

        def attend(q_nope, q_rope):
            def blk(a):
                qn, qr, cq = a
                return mla_core(qn, qr, k_nope, kr, v, cid_p[None, :] <= cq[:, None])

            o = lax.map(blk, (to_blocks(q_nope), to_blocks(q_rope), cid_p.reshape(nb, Q_BLOCK)))
            return from_blocks(o, B_WIDTH)
        return attend

    yp, fk_p, fv_p, flf_p, ckv_p, kr_p = trunk(xp, pos_p, fox_attend_prompt, mla_context_prompt)

    dbsz, dseq = x_sample.shape[:2]
    past = cache_mla_ckv.shape[1]
    pos_s = past + jnp.arange(dseq)
    fox_mask_s = jnp.arange(past + dseq)[None, :] <= pos_s[:, None]

    def fox_attend_sample(l, q, k, v, logf):
        k_all = jnp.concatenate([cache_fox_k[l].astype(k.dtype), k], axis=1)
        v_all = jnp.concatenate([cache_fox_v[l].astype(v.dtype), v], axis=1)
        fcum = jnp.cumsum(jnp.concatenate([cache_fox_logf[l].astype(jnp.float32), logf], axis=1), axis=1)
        o = fox_core(q, k_all, v_all, fcum[:, past:], fcum, fox_mask_s)
        return o.reshape(dbsz, dseq, A_WIDTH)

    def mla_context_sample(c, kr):
        k_nope, v = mla_expand(jnp.concatenate([cache_mla_ckv.astype(c.dtype), c], axis=1), w_ukv)
        kr_all = jnp.concatenate([cache_mla_krope.astype(kr.dtype), kr], axis=1)

        def attend(q_nope, q_rope):
            return mla_core(q_nope, q_rope, k_nope, kr_all, v, None).reshape(dbsz, dseq, B_WIDTH)
        return attend

    ys, fk_s, fv_s, flf_s, ckv_s, kr_s = trunk(x_sample, pos_s, fox_attend_sample, mla_context_sample)

    y_prompt = yp[:, N_META:L]
    return (y_prompt, ys,
            fk_p[:, :, :L], fv_p[:, :, :L], flf_p[:, :, :L], ckv_p[:, :L], kr_p[:, :L],
            fk_s, fv_s, flf_s, ckv_s, kr_s)


_drawn_inputs = setup_inputs


def setup_inputs(seed=0):
    import zlib

    import numpy as np

    out = dict(_drawn_inputs(seed))
    spreads = {}
    factors = {'cache_fox_logf': 3.225,
     'a_norm': 2.97,
     'kv_norm': 2.875,
     'kv_lat_norm': 2.928,
     'b_norm': 8.0,
     'b_q_norm': 8.0,
     'final_norm': 2.748}
    for name, (base, spread) in spreads.items():
        noise = np.random.default_rng([zlib.crc32(name.encode()), seed]).standard_normal(out[name].shape)
        drawn = base * np.exp(spread * noise) if base else spread * noise
        out[name] = __import__('jax').numpy.asarray(drawn.astype(out[name].dtype))
    for name, factor in factors.items():
        out[name] = (out[name] * factor).astype(out[name].dtype)
    return out
```

```python
from contextlib import ExitStack

import numpy as np

import concourse.bass as bass
from concourse import mybir

F32 = mybir.dt.float32
F32R = mybir.dt.float32r
BF16 = mybir.dt.bfloat16
ALU = mybir.AluOpType
ACT = mybir.ActivationFunctionType
AX_X = mybir.AxisListType.X

P = 128
D = 1024
KT = D // P
HEADS = 8
DH = 128
N_SAMPLE, N_META, SEQ, PAST = 32, 16, 1024, 512
L = N_META + SEQ
SMALL = N_SAMPLE + N_META
T = SMALL + SEQ
NT = 1 + SEQ // P
NC = PAST // P
ROPE, KV_LORA, Q_LORA = 64, 256, 384
QK_HEAD = DH + ROPE
QW = Q_LORA // P * 2 * QK_HEAD
FOX_SCALE = DH ** -0.5
MLA_SCALE = QK_HEAD ** -0.5
EPS = 1e-6
BIG = 1e30
FMAX = 3.0e38

CHUNK_W = 358
CHUNKS = [(0, CHUNK_W), (CHUNK_W, CHUNK_W), (2 * CHUNK_W, T - 2 * CHUNK_W)]
GROUPS = [(range(0, 4), 0, SMALL + 3 * P), (range(4, 8), SMALL + 3 * P, 4 * P), (range(8, 9), SMALL + 7 * P, P)]
S9W = (PAST + SMALL) // 2


def tile_cols(t):
    return (0, SMALL) if t == 0 else (SMALL + P * (t - 1), P)


def score_pieces(i):
    end = SMALL + P * (i + 1)
    used = end - N_SAMPLE
    if i == 0:
        return N_SAMPLE, 1, 256, used
    if i < 3:
        return N_SAMPLE, 1, used, used
    if i < 7:
        return N_SAMPLE, 2, used // 2, used
    return end - 3 * 348, 3, 348, 3 * 348


def prob_groups(i):
    blocks = list(range(i + 2))
    return [blocks[n:n + 4] for n in range(0, len(blocks), 4)]


TURNS = [("K", g) for g in range(3)] + [("C", 0), ("S", 0)] + [
    (i, g) for i in range(8) for g in range(len(prob_groups(i)))]
TURNS_PER_BANK = [(len(TURNS) + 1) // 2, len(TURNS) // 2]
SPLIT_TURNS = [u for u in TURNS if u[0] not in ("C", "S")]


def head_steps(fox, last):
    if fox:
        fill = {"start": "g1", 0: "", 1: "g2", 2: "k0", 3: "k1 k2", 4: "k3 k4", 5: "k5", 6: "k6 k7", "end": "k8 q0", "after": "q1 q2"}
    else:
        fill = {"start": "g1", 0: "", 1: "k0", 2: "g2", 3: "k1", 4: "k2 k3 k4 k5", 5: "k6 k7", 6: "k8 k9 k10", "end": "k11 k12", "after": ""}
    kinds = {"g": "gate", "k": "next_kv", "q": "next_q"}

    def filled(slot):
        return [(kinds[f[0]], int(f[1:])) for f in fill[slot].split() if not (last and f[0] in "kq")]

    def gate_done(c):
        return [("gate_tanh", c), ("gate_mul", c)]

    steps = [("turn_keys", 0), ("turn_keys", 1), ("gate", 0), ("split_query", 0), ("turn_keys", 2), ("turn_cache", 0),
             ("small_scores", 0), ("scores", 0), ("small_max", 0), ("max", 0), ("small_exp", 0), ("exp", 0),
             ("small_rescale", 0), ("rescale", 0)]
    steps += gate_done(0) + [("split_values", 0)] + filled("start") + [("turn_small", 0)]
    for i in range(8):
        groups = len(prob_groups(i))
        steps += [("turn_probs", (i, g)) for g in range(min(groups, 2))]
        if i < 7:
            steps += [("scores", i + 1), ("max", i + 1)]
        if i == 1:
            steps += gate_done(1) + [("gated", 0)]
        if i in (2, 4, 6):
            steps += [("gated", i // 2)]
        if i == 4:
            steps += gate_done(2)
        steps += [("turn_probs", (i, g)) for g in range(2, groups)]
        if i < 7:
            steps += [("exp", i + 1), ("rescale", i + 1)]
        if i == 0:
            steps += [("small_values", 0)]
        steps += filled(i if i < 7 else "end")
        if i % 2:
            steps += [("values", i // 2)]
    return steps + filled("after") + [("gated", 4)]


class Turns:

    def __init__(self, fox):
        self.tables = {}
        for last in (False, True):
            banks, seen = {}, [0, 0]
            for n, s in enumerate(s for s in head_steps(fox, last) if s[0] in ("gate", "next_kv", "next_q")):
                banks[s] = (n % 2, seen[n % 2])
                seen[n % 2] += 1
            self.tables[last] = banks
            if not last:
                self.proj_per_head = seen

    def proj(self, step, h):
        b, nth = self.tables[isinstance(h, int) and h == HEADS - 1][step]
        return b, self.proj_per_head[b] * h + nth

    def after_next_kv(self, h):
        return [(b, 1 + max(nth for s, (bank, nth) in self.tables[False].items() if s[0] == "next_kv" and bank == b)
                 + self.proj_per_head[b] * h) for b in range(2)]

    @staticmethod
    def turn(use, h):
        n = TURNS.index(use)
        return n % 2, TURNS_PER_BANK[n % 2] * h + n // 2

    @staticmethod
    def split(use, h):
        return len(SPLIT_TURNS) * h + SPLIT_TURNS.index(use)


def three_pass(pe, out, terms, start=True, stop=True):
    n = len(terms)
    for k, (lh, ll, rh, rl) in enumerate(terms):
        pe.matmul(out, lh, rh, start=start and k == 0, stop=False)
        pe.matmul(out, lh, rl, start=False, stop=False)
        last = pe.matmul(out, ll, rh, start=False, stop=stop and k == n - 1)
    return last


def wait_apart(eng, sem, value, waited):
    eng.wait_ge(sem, value)
    eng.sem_inc(waited, 1)


class Memory:

    def __init__(self, nc):
        self.nc = nc
        self.prefix = ""

    def sbuf(self, stack, name, shape, dtype=F32, side=None):
        return stack.enter_context(self.nc.sbuf_tensor(self.prefix + name, shape, dtype, side=side))


def attention(nc, m, fox, dram):
    pre = "fox_" if fox else "mla_"
    turns = Turns(fox)
    NKV = NT if fox else NT + NC
    bank = m.bank
    S, PT, O, PJ = bank[0:3], bank[3:5], bank[5], bank[6:8]
    ident = m.ident

    with ExitStack() as st:
        sems = []
        st.callback(nc.all_engine_barrier)
        st.callback(nc.clear_and_free_semaphores, sems)

        def sb(name, shape, dtype=F32):
            return st.enter_context(nc.sbuf_tensor(pre + name, shape, dtype))

        def sem(name):
            sems.append(nc.alloc_semaphore(pre + name))
            return sems[-1]

        key_hi, key_lo = sb("key_hi", [P, T], F32R), sb("key_lo", [P, T], F32R)
        key_32 = sb("key_32", [P, P])
        query_hi, query_lo = sb("query_hi", [P, T], F32R), sb("query_lo", [P, T], F32R)
        value_hi, value_lo = sb("value_hi", [P, NT, DH], F32R), sb("value_lo", [P, NT, DH], F32R)
        gate = sb("gate", [P, T])
        gate_tanh = sb("gate_tanh", [P, CHUNK_W])
        probs = sb("probs", [P, T])
        probs_s = sb("probs_s", [SMALL, PAST + SMALL])
        pT_hi, pT_lo = sb("pT_hi", [P, NT, 2 * P], F32R), sb("pT_lo", [P, NT, 2 * P], F32R)
        pT_s = sb("pT_s", [P, NC + 1, P])
        out_buf = sb("out_buf", [P, 2, 2 * P])
        cache_keyT = out_buf[:, :, :].rearrange("p a b -> p (a b)")
        neg_max, row_sum, row_inv = sb("neg_max", [P, NT]), sb("row_sum", [P, NT]), sb("row_inv", [P, NT])
        kv_nat, query_32 = m.kv_nat, m.query_32
        if fox:
            cache_k, cache_v = sb("cache_k", [P, NC, DH]), sb("cache_v", [P, NC, DH])
            f_keys = sb("f_keys", [P, T + PAST])
            f_query = sb("f_query", [P, NT])
            decay = [sb("decay0", [P, T]), sb("decay1", [P, T])]
            decay_s = probs_s
            value_small = sb("value_small", [P, DH])
        else:
            rope_q = sb("rope_q", [P, T], F32R)
            rope_qs = sb("rope_qs", [ROPE, SMALL])
            value_small = m.kv_nat[:, 0, DH:2 * DH]

        proj_full, proj_free = [sem("proj_full0"), sem("proj_full1")], [sem("proj_free0"), sem("proj_free1")]
        turn_full, turn_free = [sem("turn_full0"), sem("turn_full1")], [sem("turn_free0"), sem("turn_free1")]
        turn_rounded = sem("turn_rounded")
        scores_full, max_done, exp_done, probs_ready = sem("scores_full"), sem("max_done"), sem("exp_done"), sem("probs_ready")
        out_full, out_ready, out_stored = sem("out_full"), sem("out_ready"), [sem("out_stored0"), sem("out_stored1")]
        gate_tanhed, gate_ready = sem("gate_tanhed"), sem("gate_ready")
        query_rounded, value_rounded = sem("query_rounded"), sem("value_rounded")
        query_split, value_split = sem("query_split"), sem("value_split")
        kv_stored = sem("kv_stored")
        zeroed, vec_step, pool_step = sem("zeroed"), sem("vec_step"), sem("pool_step")
        kv_w_loaded, kv_w_split, qg_w_loaded, qg_w_split = sem("kv_w_loaded"), sem("kv_w_split"), sem("qg_w_loaded"), sem("qg_w_split")
        cache_loaded, f_loaded, f_query_ready = sem("cache_loaded"), sem("f_loaded"), sem("f_query_ready")
        decay_ready = sem("decay_ready")
        pe_waited, dve_waited, pool_waited = sem("pe_waited"), sem("dve_waited"), sem("pool_waited")
        q_loaded, rope_loaded, rope_split_loaded = sem("q_loaded"), sem("rope_loaded"), sem("rope_split_loaded")

        block = st.enter_context(nc.Block())
        KC = KT if fox else KV_LORA // P
        kv_w_hi, kv_w_lo = m.kv_w_hi, m.kv_w_lo
        g_w_hi, g_w_lo = m.g_w_hi, m.g_w_lo
        GCOL = DH if fox else 0

        def heads(eng, body):
            with eng.Fori(0, HEADS - 1) as h:
                body(h, False)
            body(HEADS - 1, True)

        FIRST = 1
        started = turn_free + proj_free + out_stored + [exp_done, max_done, out_ready, gate_ready, qg_w_split, out_full]

        @block.tensor
        def _(pe):
            for first in started:
                pe.sem_inc(first, FIRST)

            def turn_keys(h, g):
                tiles, col, width = GROUPS[g]
                b, nth = turns.turn(("K", g), h)
                wait_apart(pe, turn_free[b], FIRST + nth, pe_waited)
                for t in tiles:
                    c, n = tile_cols(t)
                    last = pe.transpose(PT[b][:, c - col:c - col + n], kv_nat[0:n, t, 0:DH], ident[0:n, 0:n])
                last.then_inc(turn_full[b], 1)

            def turn_cache(h):
                b, nth = turns.turn(("C", 0), h)
                if fox:
                    pe.wait_ge(cache_loaded, 32 * h + 32)
                pe.wait_ge(turn_free[b], FIRST + nth)
                for t in range(NC):
                    src = cache_k[:, t, :] if fox else kv_nat[:, NT + t, 0:DH]
                    last = pe.transpose(PT[b][:, P * t:P * t + P], src, ident[:, :])
                last.then_inc(turn_full[b], 1)

            def gate_chunk(h, c):
                b, nth = turns.proj(("gate", c), h)
                col, w = CHUNKS[c]
                if c == 0:
                    pe.wait_ge(qg_w_split, FIRST + h)
                pe.wait_ge(proj_free[b], FIRST + nth)
                three_pass(pe, PJ[b][:, 0:w],
                           [(g_w_hi[:, k, GCOL:GCOL + DH], g_w_lo[:, k, GCOL:GCOL + DH],
                             m.act_hi[:, k, col:col + w], m.act_lo[:, k, col:col + w]) for k in range(KT)]
                           ).then_inc(proj_full[b], 1)

            def small_scores(h):
                pe.wait_ge(exp_done if not fox else max_done, FIRST + NT * h)
                b, nth = turns.turn(("C", 0), h)
                pe.wait_ge(turn_free[b], FIRST + nth + 1)
                pe.wait_ge(query_split, h + 1)
                if not fox:
                    pe.wait_ge(rope_loaded, 16 * h + 16)
                q = query_32[:, 0:SMALL]
                pieces = [(0, 0, S9W, cache_keyT, 0), (1, 0, PAST - S9W, cache_keyT, S9W), (1, PAST - S9W, P, key_32, 0)]
                for b, c, n, keys, kc in pieces:
                    last = pe.matmul(S[b][0:SMALL, c:c + n], q, keys[:, kc:kc + n], start=True, stop=fox)
                    if not fox:
                        hidden = N_SAMPLE if keys is key_32 else n
                        half = hidden // 2
                        for e in (c, c + half):
                            pe.matmul(S[b][0:SMALL, e:e + half], m.mask_meta[0:1, :], m.mask_big[0:1, 0:half], start=False, stop=False)
                        if keys is key_32:
                            pe.matmul(S[b][0:SMALL, c + N_SAMPLE:c + SMALL], m.mask_sample[0:1, :], m.mask_big[0:1, 0:N_META],
                                      start=False, stop=False)
                        rc = kc if keys is key_32 else P + kc
                        last = pe.matmul(S[b][0:SMALL, c:c + n], rope_qs[:, :],
                                         m.rope_k32[0:ROPE, rc:rc + n], start=False, stop=True)
                last.then_inc(scores_full, 1)

            def scores(h, i):
                first, pieces, w, used = score_pieces(i)
                if i == 0:
                    first_bank = 2
                    pe.wait_ge(query_split, h + 1)
                    for g in range(3):
                        b, nth = turns.turn(("K", g), h)
                        pe.wait_ge(turn_free[b], FIRST + nth + 1)
                    if not fox:
                        pe.wait_ge(rope_split_loaded, 16 * h + 16)
                else:
                    first_bank = 0
                    pe.wait_ge(exp_done if not fox else max_done, FIRST + NT * h + i + 1)
                qc, _ = tile_cols(i + 1)
                for p in range(pieces):
                    out = S[first_bank + p][:, 0:w]
                    k0 = first + p * w
                    last = three_pass(pe, out, [(query_hi[:, qc:qc + P], query_lo[:, qc:qc + P],
                                                 key_hi[:, k0:k0 + w], key_lo[:, k0:k0 + w])], stop=fox)
                    if fox:
                        continue
                    if i == 7 and p == 0:
                        pe.matmul(out[:, 0:4], m.mask_all[0:1, :], m.mask_big[0:1, 0:4], start=False, stop=False)
                    if p == pieces - 1:
                        e = first + used - k0 - 64
                        pe.matmul(out[:, e:e + 64], m.mask_first[0:1, :], m.mask_big[0:1, 0:64], start=False, stop=False)
                    pe.matmul(out, rope_q[:, qc:qc + P], m.rope_k_hi[:, k0:k0 + w], start=False, stop=False)
                    last = pe.matmul(out, rope_q[0:ROPE, qc:qc + P], m.rope_k_lo[0:ROPE, k0:k0 + w], start=False, stop=True)
                last.then_inc(scores_full, 1)

            def turn_small(h):
                b, nth = turns.turn(("S", 0), h)
                pe.wait_ge(probs_ready, NT * h + 1)
                wait_apart(pe, turn_free[b], FIRST + nth, pe_waited)
                for k in range(NC + 1):
                    n = P if k < NC else SMALL
                    last = pe.transpose(PT[b][0:n, SMALL * k:SMALL * k + SMALL], probs_s[:, P * k:P * k + n],
                                        ident[0:SMALL, 0:SMALL])
                last.then_inc(turn_full[b], 1)

            def turn_probs(h, i, g):
                b, nth = turns.turn((i, g), h)
                if g == 0:
                    pe.wait_ge(probs_ready, NT * h + i + 2)
                    wait_apart(pe, turn_free[b], FIRST + nth, pe_waited)
                else:
                    pe.wait_ge(turn_free[b], FIRST + nth)
                for s, k in enumerate(prob_groups(i)[g]):
                    c, n = tile_cols(k)
                    last = pe.transpose(PT[b][0:n, P * s:P * s + P], probs[:, c:c + n], ident[:, :])
                last.then_inc(turn_full[b], 1)

            def small_values(h):
                b, nth = turns.turn(("S", 0), h)
                pe.wait_ge(turn_free[b], FIRST + nth + 1)
                pe.wait_ge(value_split, h + 1)
                pe.wait_ge(out_ready, FIRST + 5 * h)
                for k in range(NC):
                    v = cache_v[:, k, :] if fox else kv_nat[:, NT + k, DH:2 * DH]
                    pe.matmul(O[:, 0:P], v, pT_s[:, k, :], start=k == 0, stop=False)
                pe.matmul(O[:, 0:P], value_small[0:SMALL, :], pT_s[0:SMALL, NC, :], start=False, stop=True).then_inc(out_full, 1)

            def values(h, j):
                for g in range(len(prob_groups(2 * j + 1))):
                    b, nth = turns.turn((2 * j + 1, g), h)
                    pe.wait_ge(turn_free[b], FIRST + nth + 1)
                pe.wait_ge(zeroed, h + 1)
                pe.wait_ge(out_ready, FIRST + 5 * h + 1 + j)
                terms = []
                for k in range(2 * j + 3):
                    n = tile_cols(k)[1]
                    terms.append((value_hi[0:n, k, :], value_lo[0:n, k, :], pT_hi[0:n, k, :], pT_lo[0:n, k, :]))
                three_pass(pe, O[:, 0:2 * P], terms).then_inc(out_full, 1)

            def next_kv(h, t):
                b, nth = turns.proj(("next_kv", t), h)
                if t == 0:
                    pe.wait_ge(kv_w_split, h + 1)
                pe.wait_ge(proj_free[b], FIRST + nth)
                if t < NT:
                    c, n = tile_cols(t)
                else:
                    c, n = T + P * (t - NT), P
                last = three_pass(pe, PJ[b][0:n, 0:2 * DH],
                                  [(m.kv_act_hi[:, k, c:c + n], m.kv_act_lo[:, k, c:c + n], kv_w_hi[:, k, :], kv_w_lo[:, k, :])
                                   for k in range(KC)])
                last.then_inc(proj_full[b], 1)

            def next_q(h, c):
                b, nth = turns.proj(("next_q", c), h)
                col, w = CHUNKS[c]
                if c == 0:
                    pe.wait_ge(qg_w_split, FIRST + h + 1)
                pe.wait_ge(proj_free[b], FIRST + nth)
                three_pass(pe, PJ[b][:, 0:w],
                           [(g_w_hi[:, k, 0:DH], g_w_lo[:, k, 0:DH], m.act_hi[:, k, col:col + w], m.act_lo[:, k, col:col + w])
                            for k in range(KT)]).then_inc(proj_full[b], 1)

            def head(h, last):
                for step, n in head_steps(fox, last):
                    if step == "turn_keys":
                        turn_keys(h, n)
                    elif step == "turn_cache":
                        turn_cache(h)
                    elif step == "gate":
                        gate_chunk(h, n)
                    elif step == "small_scores":
                        small_scores(h)
                    elif step == "scores":
                        scores(h, n)
                    elif step == "turn_small":
                        turn_small(h)
                    elif step == "turn_probs":
                        turn_probs(h, *n)
                    elif step == "small_values":
                        small_values(h)
                    elif step == "values":
                        values(h, n)
                    elif step == "next_kv":
                        next_kv(h, n)
                    elif step == "next_q":
                        next_q(h, n)
                if not last:
                    for b, count in turns.after_next_kv(h):
                        pe.wait_ge(proj_free[b], FIRST + count)

            heads(pe, head)

        @block.scalar
        def _(act):
            def turn_keys(h, g):
                if g == 0:
                    for b in range(2):
                        act.wait_ge(proj_free[b], FIRST + turns.proj_per_head[b] * h)
                tiles, col, width = GROUPS[g]
                b, nth = turns.turn(("K", g), h)
                act.wait_ge(turn_full[b], nth + 1)
                act.activation(key_hi[:, col:col + width], PT[b][:, 0:width], ACT.Copy).then_inc(turn_rounded, 1)

            def split_query(h):
                if not fox:
                    act.wait_ge(q_loaded, 16 * h + 16)
                act.activation(query_hi[:, :], query_32[:, :], ACT.Copy).then_inc(query_rounded, 1)

            def split_values(h):
                act.activation(value_hi[:, :, :], kv_nat[:, 0:NT, DH:2 * DH], ACT.Copy).then_inc(value_rounded, 1)

            def turn_cache(h):
                b, nth = turns.turn(("C", 0), h)
                act.wait_ge(turn_full[b], nth + 1)
                act.wait_ge(out_stored[0], FIRST + 16 * 3 * h)
                act.wait_ge(out_stored[1], FIRST + 16 * 2 * h)
                act.activation(cache_keyT[:, :], PT[b][:, :], ACT.Copy).then_inc(turn_free[b], 1)

            def gate_tanh_chunk(h, c):
                col, w = CHUNKS[c]
                b, nth = turns.proj(("gate", c), h)
                act.wait_ge(proj_free[b], FIRST + nth + 1)
                act.wait_ge(gate_ready, FIRST + 3 * h + c)
                act.activation(gate_tanh[:, 0:w], gate[:, col:col + w], ACT.Tanh, scale=0.5).then_inc(gate_tanhed, 1)

            def small_exp(h):
                act.wait_ge(max_done, FIRST + NT * h + 1)
                if fox:
                    act.activation(probs_s[:, :], decay_s[:, :], ACT.Exp, scale=-1.0,
                                   bias=neg_max[0:SMALL, 0:1], accum_out=row_sum[0:SMALL, 0:1]).then_inc(exp_done, 1)
                else:
                    src = m.score_banks(0, 2)[0:SMALL, :, 0:S9W]
                    act.activation(probs_s[:, :].rearrange("p (a b) -> p a b", a=2), src, ACT.Exp,
                                   bias=neg_max[0:SMALL, 0:1], accum_out=row_sum[0:SMALL, 0:1]).then_inc(exp_done, 1)

            def exp(h, i):
                first, pieces, w, used = score_pieces(i)
                act.wait_ge(max_done, FIRST + NT * h + i + 2)
                bias, total = neg_max[:, i + 1:i + 2], row_sum[:, i + 1:i + 2]
                if fox:
                    act.activation(probs[:, first:first + used], decay[i % 2][:, first:first + used], ACT.Exp, scale=-1.0,
                                   bias=bias, accum_out=total).then_inc(exp_done, 1)
                else:
                    w = min(w, used)
                    act.activation(probs[:, first:first + used].rearrange("p (a b) -> p a b", a=pieces),
                                   m.score_banks(2 if i == 0 else 0, pieces)[:, :, 0:w], ACT.Exp,
                                   bias=bias, accum_out=total).then_inc(exp_done, 1)

            def turn_small(h):
                b, nth = turns.turn(("S", 0), h)
                act.wait_ge(turn_full[b], nth + 1)
                act.activation(pT_s[:, :, 0:SMALL], PT[b][:, 0:SMALL * (NC + 1)].rearrange("p (a b) -> p a b", b=SMALL),
                               ACT.Copy).then_inc(turn_free[b], 1)

            def turn_probs(h, i, g):
                q, blocks = P * (i % 2), prob_groups(i)[g]
                b, nth = turns.turn((i, g), h)
                n = len(blocks)
                act.wait_ge(turn_full[b], nth + 1)
                act.activation(pT_hi[:, blocks[0]:blocks[0] + n, q:q + P],
                               PT[b][:, 0:P * n].rearrange("p (a b) -> p a b", b=P), ACT.Copy).then_inc(turn_rounded, 1)

            def next_kv(h, t):
                b, nth = turns.proj(("next_kv", t), h)
                if t == 0:
                    act.wait_ge(value_split, h + 1)
                    if fox:
                        act.wait_ge(kv_stored, 96 * h + 96)
                    else:
                        act.wait_ge(out_full, FIRST + 5 * h + 1)
                act.wait_ge(proj_full[b], nth + 1)
                n = P if t >= NT else tile_cols(t)[1]
                if fox:
                    act.activation(kv_nat[0:n, t, :], PJ[b][0:n, 0:2 * DH], ACT.Copy, scale=m.rms_rows[0:n, t:t + 1]).then_inc(proj_free[b], 1)
                else:
                    act.activation(kv_nat[0:n, t, :], PJ[b][0:n, 0:2 * DH], ACT.Copy).then_inc(proj_free[b], 1)

            def head(h, last):
                for step, n in head_steps(fox, last):
                    if step == "turn_keys":
                        turn_keys(h, n)
                    elif step == "split_query":
                        split_query(h)
                    elif step == "split_values":
                        split_values(h)
                    elif step == "turn_cache":
                        turn_cache(h)
                    elif step == "gate_tanh":
                        gate_tanh_chunk(h, n)
                    elif step == "small_exp":
                        small_exp(h)
                    elif step == "exp":
                        exp(h, n)
                    elif step == "turn_small":
                        turn_small(h)
                    elif step == "turn_probs":
                        turn_probs(h, *n)
                    elif step == "next_kv":
                        next_kv(h, n)

            heads(act, head)

        @block.vector
        def _(dve):
            steps_done = [0]

            def chain(ins, h):
                ins.then_inc(vec_step, 1)
                steps_done[0] += 1
                dve.wait_ge(vec_step, STEPS * h + steps_done[0])

            def turn_keys(h, g):
                tiles, col, width = GROUPS[g]
                b, nth = turns.turn(("K", g), h)
                dve.wait_ge(turn_rounded, turns.split(("K", g), h) + 1)
                if g == 0:
                    dve.tensor_copy(key_32[:, :], PT[b][:, 0:P])
                dve.tensor_tensor(key_lo[:, col:col + width], PT[b][:, 0:width],
                                  key_hi[:, col:col + width].bitcast(F32), ALU.subtract).then_inc(turn_free[b], 1)

            def split_query(h):
                dve.wait_ge(query_rounded, h + 1)
                dve.tensor_tensor(query_lo[:, :], query_32[:, :], query_hi[:, :].bitcast(F32), ALU.subtract).then_inc(query_split, 1)

            def split_values(h):
                dve.wait_ge(value_rounded, h + 1)
                if fox:
                    dve.tensor_copy(value_small[0:SMALL, :], kv_nat[0:SMALL, 0, DH:2 * DH])
                dve.tensor_tensor(value_lo[:, :, :], kv_nat[:, 0:NT, DH:2 * DH], value_hi[:, :, :].bitcast(F32),
                                  ALU.subtract).then_inc(value_split, 1)

            def gate_chunk(h, c):
                b, nth = turns.proj(("gate", c), h)
                col, w = CHUNKS[c]
                dve.wait_ge(proj_full[b], nth + 1)
                dve.tensor_tensor(gate[:, col:col + w], PJ[b][:, 0:w], m.rms_cols[:, col:col + w], ALU.mult).then_inc(proj_free[b], 1)

            def gate_mul(h, c):
                col, w = CHUNKS[c]
                dve.wait_ge(gate_tanhed, 3 * h + c + 1)
                dve.scalar_tensor_tensor(out=gate[:, col:col + w], in0=gate_tanh[:, 0:w], scalar=1.0, in1=gate[:, col:col + w],
                                         op0=ALU.add, op1=ALU.mult).then_inc(gate_ready, 1)

            def rescale(h, n):
                rows, prob = SMALL, probs_s[:, :]
                if n:
                    first, _, _, used = score_pieces(n - 1)
                    rows, prob = P, probs[:, first:first + used]
                dve.wait_ge(exp_done, FIRST + NT * h + n + 1)
                chain(dve.reciprocal(row_inv[0:rows, n:n + 1], row_sum[0:rows, n:n + 1]), h)
                dve.tensor_scalar(prob, prob, row_inv[0:rows, n:n + 1], None, ALU.mult).then_inc(probs_ready, 1)

            def small_max(h):
                dve.wait_ge(scores_full, NT * h + 1)
                src = m.score_banks(0, 2)[0:SMALL, :, 0:S9W]
                if fox:
                    wait_apart(dve, decay_ready, NT * h + 1, dve_waited)
                    halves = lambda x: x.rearrange("p (a b) -> p a b", a=2)
                    dve.tensor_tensor_reduce(halves(decay_s[:, :]), src, halves(decay_s[:, :]), 1.0, FMAX,
                                             ALU.add, ALU.min, neg_max[0:SMALL, 0:1]).then_inc(max_done, 1)
                else:
                    dve.tensor_reduce(neg_max[0:SMALL, 0:1], src, mybir.AxisListType.XY, ALU.max, negate=True).then_inc(max_done, 1)

            def row_max(h, i):
                first, pieces, w, used = score_pieces(i)
                w = min(w, used)
                dve.wait_ge(scores_full, NT * h + i + 2)
                src = m.score_banks(2 if i == 0 else 0, pieces)[:, :, 0:w]
                if fox:
                    wait_apart(dve, decay_ready, NT * h + i + 2, dve_waited)
                    cut = lambda x: x[:, first:first + used].rearrange("p (a b) -> p a b", a=pieces)
                    dve.tensor_tensor_reduce(cut(decay[i % 2]), src, cut(decay[i % 2]), 1.0, FMAX,
                                             ALU.add, ALU.min, neg_max[:, i + 1:i + 2]).then_inc(max_done, 1)
                else:
                    dve.tensor_reduce(neg_max[:, i + 1:i + 2], src, mybir.AxisListType.XY, ALU.max, negate=True).then_inc(max_done, 1)

            def turn_probs(h, i, g):
                q, blocks = P * (i % 2), prob_groups(i)[g]
                b, nth = turns.turn((i, g), h)
                k, n = blocks[0], len(blocks)
                dve.wait_ge(turn_rounded, turns.split((i, g), h) + 1)
                dve.tensor_tensor(pT_lo[:, k:k + n, q:q + P], PT[b][:, 0:P * n].rearrange("p (a b) -> p a b", b=P),
                                  pT_hi[:, k:k + n, q:q + P].bitcast(F32), ALU.subtract).then_inc(turn_free[b], 1)

            def gated(h, n):
                col, w = (0, SMALL) if n == 0 else (SMALL + 2 * P * (n - 1), 2 * P)
                dve.wait_ge(out_full, FIRST + 5 * h + n + 1)
                dve.wait_ge(gate_ready, FIRST + 3 * h + (1, 1, 2, 3, 3)[n])
                dve.wait_ge(out_stored[n % 2], FIRST + 16 * ((3, 2)[n % 2] * h + n // 2))
                dve.scalar_tensor_tensor(out=out_buf[:, n % 2, 0:w], in0=O[:, 0:w], scalar=0.5, in1=gate[:, col:col + w],
                                         op0=ALU.mult, op1=ALU.mult).then_inc(out_ready, 1)

            def next_q(h, c):
                b, nth = turns.proj(("next_q", c), h)
                col, w = CHUNKS[c]
                dve.wait_ge(proj_full[b], nth + 1)
                dve.scalar_tensor_tensor(out=query_32[:, col:col + w], in0=PJ[b][:, 0:w], scalar=-FOX_SCALE,
                                         in1=m.rms_cols[:, col:col + w], op0=ALU.mult, op1=ALU.mult).then_inc(proj_free[b], 1)

            def head(h, last):
                steps_done[0] = 0
                for step, n in head_steps(fox, last):
                    if step == "turn_keys":
                        turn_keys(h, n)
                    elif step == "split_query":
                        split_query(h)
                    elif step == "split_values":
                        split_values(h)
                    elif step == "gate":
                        gate_chunk(h, n)
                    elif step == "gate_mul":
                        gate_mul(h, n)
                    elif step == "small_max":
                        small_max(h)
                    elif step == "max":
                        row_max(h, n)
                    elif step == "small_rescale":
                        rescale(h, 0)
                    elif step == "rescale":
                        rescale(h, n + 1)
                    elif step == "turn_probs":
                        turn_probs(h, *n)
                    elif step == "gated":
                        gated(h, n)
                    elif step == "next_q":
                        next_q(h, n)
                assert steps_done[0] == STEPS

            STEPS = NT
            heads(dve, head)

        @block.gpsimd
        def _(pool):
            pool.memset(pT_hi[:, :, :].bitcast(F32), 0.0)
            pool.memset(pT_lo[:, :, :].bitcast(F32), 0.0)
            pool.memset(pT_s[:, :, :], 0.0)
            if fox:
                pool.memset(decay[0][:, 0:N_SAMPLE], BIG)
                pool.memset(decay[1][:, 0:N_SAMPLE], BIG)
            pool.memset(probs[:, 0:N_SAMPLE], 0.0).then_inc(pool_step, 1)
            pool.wait_ge(pool_step, 1)
            DECAY_AFTER = [None, 2, None, 3, 4, 5, 6, 7]
            PSTEPS = 20 if fox else 3
            kv_stage = None if fox else m.stage[:, 0:4, :].rearrange("p (k a) n -> p k (a n)", a=2)
            taken = [0]

            def chain(ins, h):
                ins.then_inc(pool_step, 1)
                taken[0] += 1
                wait_apart(pool, pool_step, 1 + PSTEPS * h + taken[0], pool_waited)

            def zero_upper(h):
                wait_apart(pool, out_full, FIRST + 5 * h, pool_waited)
                pool.memset(pT_hi[:, 2:7:2, 0:P].bitcast(F32), 0.0)
                pool.memset(pT_lo[:, 2:7:2, 0:P].bitcast(F32), 0.0).then_inc(zeroed, 1)

            def split_piece(h, stage, hi, lo):
                chain(pool.tensor_scalar(hi, stage, 1.0, 0.0, ALU.mult, ALU.add), h)
                return pool.tensor_tensor(lo, stage, hi.bitcast(F32), ALU.subtract)

            def split_weights(h, stage, hi, lo, done):
                split_piece(h, stage, hi, lo).then_inc(done, 1)

            def decay_tile(h, i):
                n = SMALL + P * (i + 1) - N_SAMPLE
                d = decay[i % 2]
                wait_apart(pool, exp_done, FIRST + NT * h + (i if i >= 2 else 0), pool_waited)
                chain(pool.tensor_scalar(d[:, N_SAMPLE:N_SAMPLE + n], f_keys[:, N_SAMPLE:N_SAMPLE + n], 1.0,
                                         f_query[:, i + 1:i + 2], ALU.mult, ALU.add), h)
                e = N_SAMPLE + n - P
                pool.affine_select(out=d[:, e:e + P], in_=d[:, e:e + P], compare_op=ALU.is_ge, fill=BIG, base=0,
                                   pattern=[[-1, P]], channel_multiplier=1).then_inc(decay_ready, 1)

            def decay_small(h):
                own = decay_s[:, PAST:PAST + SMALL]
                chain(pool.tensor_scalar(decay_s[:, 0:PAST], f_keys[0:SMALL, T:T + PAST], 1.0, f_query[0:SMALL, 0:1],
                                         ALU.mult, ALU.add), h)
                chain(pool.tensor_scalar(own, f_keys[0:SMALL, 0:SMALL], 1.0, f_query[0:SMALL, 0:1], ALU.mult, ALU.add), h)
                chain(pool.affine_select(out=own, in_=own, compare_op=ALU.is_ge, fill=BIG, base=0,
                                         pattern=[[-1, SMALL]], channel_multiplier=1), h)
                pool.memset(decay_s[N_SAMPLE:SMALL, 0:PAST + N_SAMPLE], BIG).then_inc(decay_ready, 1)
                wait_apart(pool, decay_ready, NT * h + 1, pool_waited)

            def load_rope(h):
                pool.dma_start(rope_q[:, :], dram.q_rope[bass.ds(h * DH, DH), :]).then_inc(rope_split_loaded, 16)

            def head(h, last):
                taken[0] = 0
                zero_upper(h)
                if fox:
                    wait_apart(pool, f_loaded, 16 * h + 16, pool_waited)
                    wait_apart(pool, exp_done, FIRST + NT * h, pool_waited)
                    chain(pool.tensor_copy(f_query[:, :], m.f_query_all[:, h, :] if isinstance(h, int) else
                                           m.f_query_all[:, bass.ds(h, 1), :].rearrange("p a t -> p (a t)")), h)
                    decay_small(h)
                    decay_tile(h, 0)
                    decay_tile(h, 1)
                    for i in range(8):
                        if not last:
                            if i == 0:
                                wait_apart(pool, kv_w_loaded, 32 * h + 32, pool_waited)
                            if i == 4:
                                b, nth = turns.proj(("gate", 2), h)
                                wait_apart(pool, proj_full[b], nth + 1, pool_waited)
                                wait_apart(pool, qg_w_loaded, 32 * h + 32, pool_waited)
                            k = slice(2 * (i % 4), 2 * (i % 4) + 2)
                            hi, lo = (kv_w_hi, kv_w_lo) if i < 4 else (g_w_hi, g_w_lo)
                            last_split = split_piece(h, m.stage[:, k, :], hi[:, k, :], lo[:, k, :])
                            if i % 4 == 3:
                                last_split.then_inc(kv_w_split if i < 4 else qg_w_split, 1)
                        if DECAY_AFTER[i] is not None:
                            decay_tile(h, DECAY_AFTER[i])
                else:
                    if not last:
                        wait_apart(pool, kv_w_loaded, 16 * h + 16, pool_waited)
                        split_weights(h, kv_stage, kv_w_hi[:, :, :], kv_w_lo[:, :, :], kv_w_split)
                        b, nth = turns.proj(("gate", 2), h)
                        wait_apart(pool, proj_full[b], nth + 1, pool_waited)
                        wait_apart(pool, qg_w_loaded, 16 * h + 16, pool_waited)
                        for k in range(KT):
                            last_scaled = pool.tensor_scalar(m.stage[:, k, :], m.stage[:, k, :], m.b_gain[:, k:k + 1], 1.0,
                                                             ALU.mult, ALU.mult)
                        chain(last_scaled, h)
                        split_weights(h, m.stage[:, :, :], g_w_hi[:, :, :], g_w_lo[:, :, :], qg_w_split)
                        wait_apart(pool, scores_full, NT * h + NT, pool_waited)
                        load_rope(h + 1)

            if not fox:
                load_rope(0)
            heads(pool, head)

        @block.sync
        def _(sp):
            def store_out(h, n, col, w):
                sp.wait_ge(out_ready, FIRST + 5 * h + n + 1)
                sp.dma_start((dram.gated if fox else dram.gated_b)[bass.ds(h * DH, DH), col:col + w], out_buf[:, n % 2, 0:w]).then_inc(out_stored[n % 2], 16)

            def load_cache(h):
                sp.dma_start(cache_k[:, :, :], dram.cache_k[:, bass.ds(h * DH, DH)].rearrange("(t p) d -> p t d", p=P)).then_inc(cache_loaded, 16)
                sp.dma_start(cache_v[:, :, :], dram.cache_v[:, bass.ds(h * DH, DH)].rearrange("(t p) d -> p t d", p=P)).then_inc(cache_loaded, 16)

            def load_f_keys(h):
                sp.dma_start(f_keys[:, :], dram.f_cum[bass.ds(h, 1), :].to_broadcast([P, T + PAST])).then_inc(f_loaded, 16)

            def load_queries(h):
                sp.dma_start(query_32[:, :], dram.q_nope[bass.ds(h * DH, DH), :]).then_inc(q_loaded, 16)

            def load_rope(h):
                sp.dma_start(rope_qs[:, :], dram.q_rope_small[bass.ds(h * ROPE, ROPE), :]).then_inc(rope_loaded, 16)

            kv_stage = None if fox else m.stage[:, 0:4, :].rearrange("p (k a) n -> p k (a n)", a=2)
            if fox:
                load_cache(0)
                load_f_keys(0)
            else:
                load_queries(0)
                load_rope(0)

            def head(h, last):
                if fox and not last:
                    sp.wait_ge(qg_w_split, FIRST + h)
                    for n, sec in enumerate((1, 2)):
                        sp.dma_start(m.stage[:, :, DH * n:DH * n + DH], dram.fox_w(sec, h + 1)).then_inc(kv_w_loaded, 16)
                if fox:
                    for b in range(2):
                        sp.wait_ge(proj_free[b], FIRST + turns.proj_per_head[b] * h)
                    for dst_p, dst_s, col in ((dram.new_k_prompt, dram.new_k_sample, 0), (dram.new_v_prompt, dram.new_v_sample, DH)):
                        sp.dma_start(dst_s[:, bass.ds(h * DH, DH)], kv_nat[0:N_SAMPLE, 0, col:col + DH]).then_inc(kv_stored, 16)
                        sp.dma_start(dst_p[0:N_META, bass.ds(h * DH, DH)], kv_nat[N_SAMPLE:SMALL, 0, col:col + DH]).then_inc(kv_stored, 16)
                        sp.dma_start(dst_p[N_META:L, bass.ds(h * DH, DH)].rearrange("(t p) d -> p t d", p=P),
                                     kv_nat[:, 1:NT, col:col + DH]).then_inc(kv_stored, 16)
                if not fox and not last:
                    sp.wait_ge(qg_w_split, FIRST + h)
                    sp.dma_start(kv_stage, dram.w_ukv(h + 1)).then_inc(kv_w_loaded, 16)
                store_out(h, 0, 0, SMALL)
                if not last:
                    if fox:
                        load_cache(h + 1)
                    else:
                        sp.wait_ge(value_split, h + 1)
                        sp.wait_ge(scores_full, NT * h + 1)
                        load_queries(h + 1)
                        load_rope(h + 1)
                store_out(h, 1, SMALL, 2 * P)
                if not fox and not last:
                    sp.wait_ge(kv_w_split, h + 1)
                    sp.dma_start(m.stage[:, :, :], dram.w_gate(h + 1)).then_inc(qg_w_loaded, 16)
                if fox and not last:
                    sp.wait_ge(kv_w_split, h + 1)
                    for n, sec in enumerate((0, 3)):
                        sp.dma_start(m.stage[:, :, DH * n:DH * n + DH], dram.fox_w(sec, h + 1)).then_inc(qg_w_loaded, 16)
                store_out(h, 2, SMALL + 2 * P, 2 * P)
                store_out(h, 3, SMALL + 4 * P, 2 * P)
                if fox and not last:
                    sp.wait_ge(decay_ready, NT * h + NT)
                    load_f_keys(h + 1)
                store_out(h, 4, SMALL + 6 * P, 2 * P)

            heads(sp, head)
            sp.wait_ge(out_stored[0], FIRST + 16 * 3 * HEADS)
            sp.wait_ge(out_stored[1], FIRST + 16 * 2 * HEADS)
            if fox:
                sp.wait_ge(kv_stored, 96 * HEADS)


def embed(nc, m, dram):
    bank = m.bank
    ident = m.ident
    with ExitStack() as st:
        sems = []
        st.callback(nc.all_engine_barrier)
        st.callback(nc.clear_and_free_semaphores, sems)

        def sb(name, shape, dtype=F32):
            return st.enter_context(nc.sbuf_tensor("embed_" + name, shape, dtype))

        def sem(name):
            sems.append(nc.alloc_semaphore("embed_" + name))
            return sems[-1]

        x_nat = sb("x_nat", [P, NT, D])
        square = sb("square", [P, D])
        xt = sb("xt", [P, 3, 512])
        ones = sb("ones", [P, P])
        diag = sb("diag", [P, NT, P])
        a_gain = sb("a_gain", [P, KT])
        ssq, rms_ln, rms_t = sb("ssq", [P, NT]), sb("rms_ln", [P, NT]), sb("rms_t", [P, NT])
        wf, wf_hi, wf_lo = sb("wf", [P, KT, HEADS]), sb("wf_hi", [P, KT, HEADS], F32R), sb("wf_lo", [P, KT, HEADS], F32R)
        b_f = sb("b_f", [HEADS, 1])
        cache_f = sb("cache_f", [P, NC, HEADS])
        f = sb("f", [HEADS, T])
        f_abs, f_exp = sb("f_abs", [HEADS, T]), sb("f_exp", [HEADS, T])
        log_f = sb("log_f", [HEADS, T + PAST])
        f_cum = sb("f_cum", [HEADS, T + PAST])
        row_ones = sb("row_ones", [HEADS, T])
        log_f_nat = sb("log_f_nat", [P, NT, HEADS])

        x_loaded = [sem(f"x_loaded{t}") for t in range(NT)]
        const_loaded, f_in_loaded, kv_w_loaded, q_w_loaded, w_split = sem("const_loaded"), sem("f_in_loaded"), sem("kv_w_loaded"), sem("q_w_loaded"), sem("w_split")
        part_full, part_rounded, part_free = sem("part_full"), sem("part_rounded"), sem("part_free")
        xt_ready, xt_stored = sem("xt_ready"), [sem(f"xt_stored{n}") for n in range(3)]
        squared, rms_step_v, rms_step_a = sem("squared"), sem("rms_step_v"), sem("rms_step_a")
        ones_ready, diag_ready = sem("ones_ready"), sem("diag_ready")
        rms_full, rms_ready = sem("rms_full"), sem("rms_ready")
        f_full, f_step, f_act = sem("f_full"), sem("f_step"), sem("f_act")
        f_cache_full, f_nat_full, f_stored = sem("f_cache_full"), sem("f_nat_full"), sem("f_stored")
        proj_full, proj_free = [sem("proj_full0"), sem("proj_full1")], [sem("proj_free0"), sem("proj_free1")]
        wf_split = sem("wf_split")
        block = st.enter_context(nc.Block())

        parts = [(g, k) for g in range(3) for k in range(KT)]

        @block.sync
        def _(sp):
            for t in range(NT):
                if t == 0:
                    sp.dma_start(x_nat[0:N_SAMPLE, 0, :], dram.x_sample).then_inc(x_loaded[0], 16)
                    sp.dma_start(x_nat[N_SAMPLE:SMALL, 0, :], dram.meta).then_inc(x_loaded[0], 16)
                    sp.dma_start(ident[:, :], dram.ident).then_inc(const_loaded, 16)
                    sp.dma_start(a_gain[:, :], dram.a_norm).then_inc(const_loaded, 16)
                else:
                    sp.dma_start(x_nat[:, t, :], dram.x_prompt[P * (t - 1):P * t, :]).then_inc(x_loaded[t], 16)
                if t == 3:
                    sp.dma_start(wf[:, :, :], dram.a_w_in[:, 3 * D:3 * D + HEADS].rearrange("(k p) n -> p k n", p=P)).then_inc(f_in_loaded, 16)
                    sp.dma_start(b_f[:, :], dram.a_b_forget).then_inc(f_in_loaded, 16)
                    sp.dma_start(cache_f[:, :, :], dram.cache_f.rearrange("(t p) h -> p t h", p=P)).then_inc(f_in_loaded, 16)
                    for n, sec in enumerate((1, 2)):
                        sp.dma_start(m.stage[:, :, DH * n:DH * n + DH], dram.fox_w(sec, 0)).then_inc(kv_w_loaded, 16)
            for n, (g, k) in enumerate(parts):
                sp.wait_ge(xt_ready, n + 1)
                _, col, width = GROUPS[g]
                sp.dma_start(dram.resid[P * k:P * k + P, col:col + width], xt[:, n % 3, 0:width]).then_inc(xt_stored[n % 3], 16)
                if n == 4:
                    sp.wait_ge(w_split, 1)
                    for i, sec in enumerate((0, 3)):
                        sp.dma_start(m.stage[:, :, DH * i:DH * i + DH], dram.fox_w(sec, 0)).then_inc(q_w_loaded, 16)
            sp.wait_ge(f_step, 12)
            sp.dma_start(dram.f_cum, f_cum[:, :]).then_inc(f_stored, 16)
            sp.wait_ge(f_step, 13)
            sp.dma_start(dram.new_f_sample, log_f_nat[0:N_SAMPLE, 0, :]).then_inc(f_stored, 16)
            sp.dma_start(dram.new_f_prompt[0:N_META, :], log_f_nat[N_SAMPLE:SMALL, 0, :]).then_inc(f_stored, 16)
            sp.dma_start(dram.new_f_prompt[N_META:L, :].rearrange("(t p) h -> p t h", p=P), log_f_nat[:, 1:NT, :]).then_inc(f_stored, 16)
            sp.wait_ge(f_stored, 64)
            for n in range(3):
                sp.wait_ge(xt_stored[n], 16 * (len(parts) // 3))

        @block.gpsimd
        def _(pool):
            pool.memset(ones[:, :], 1.0)
            pool.memset(row_ones[:, :], 1.0)
            pool.memset(m.kv_nat[:, 0, :], 0.0)
            pool.memset(m.f_query_all[:, :, :], 0.0)
            pool.memset(ssq[:, :], float(D)).then_inc(ones_ready, 1)
            pool.wait_ge(f_in_loaded, 48)
            pool.tensor_scalar(wf_hi[:, :, :], wf[:, :, :], 1.0, 0.0, ALU.mult, ALU.add).then_inc(wf_split, 1)
            pool.wait_ge(wf_split, 1)
            pool.tensor_tensor(wf_lo[:, :, :], wf[:, :, :], wf_hi[:, :, :].bitcast(F32), ALU.subtract).then_inc(wf_split, 1)
            for n, (loaded, hi, lo) in enumerate(((kv_w_loaded, m.kv_w_hi, m.kv_w_lo), (q_w_loaded, m.g_w_hi, m.g_w_lo))):
                pool.wait_ge(loaded, 32)
                pool.tensor_scalar(hi[:, :, :], m.stage[:, :, :], 1.0, 0.0, ALU.mult, ALU.add).then_inc(wf_split, 1)
                pool.wait_ge(wf_split, n + 3)
                pool.tensor_tensor(lo[:, :, :], m.stage[:, :, :], hi[:, :, :].bitcast(F32), ALU.subtract).then_inc(w_split, 1)

        @block.tensor
        def _(pe):
            pe.wait_ge(const_loaded, 32)
            for n, (g, k) in enumerate(parts):
                tiles, col, width = GROUPS[g]
                if n >= 4:
                    pe.wait_ge(part_free, n - 3)
                for t in tiles:
                    c, w = tile_cols(t)
                    if k == 0:
                        pe.wait_ge(x_loaded[t], 32 if t == 0 else 16)
                    last = pe.transpose(bank[n % 4][:, c - col:c - col + w], x_nat[0:w, t, P * k:P * k + P], ident[0:w, 0:w])
                last.then_inc(part_full, 1)
            pe.wait_ge(part_free, len(parts))
            pe.wait_ge(wf_split, 2)
            for c, (col, w) in enumerate(CHUNKS):
                three_pass(pe, bank[c][0:HEADS, 0:w],
                           [(wf_hi[:, k, :], wf_lo[:, k, :], m.act_hi[:, k, col:col + w], m.act_lo[:, k, col:col + w])
                            for k in range(KT)]).then_inc(f_full, 1)
            pe.wait_ge(diag_ready, NT)
            for g, (tiles, col, width) in enumerate(GROUPS):
                for t in tiles:
                    c, w = tile_cols(t)
                    last = pe.matmul(bank[3 + g][:, c - col:c - col + w], ones[0:w, :], diag[0:w, t, 0:w], start=True, stop=True)
                last.then_inc(rms_full, 1)
            pe.wait_ge(f_step, 1)
            for t in range(NC):
                last = pe.transpose(bank[0][0:HEADS, P * t:P * t + P], cache_f[:, t, :], ident[:, :])
            last.then_inc(f_cache_full, 1)
            pe.wait_ge(w_split, 1)
            for t in range(NT):
                c, w = tile_cols(t)
                if t >= 2:
                    pe.wait_ge(proj_free[t % 2], t // 2)
                three_pass(pe, bank[6 + t % 2][0:w, 0:2 * DH],
                           [(m.act_hi[:, k, c:c + w], m.act_lo[:, k, c:c + w], m.kv_w_hi[:, k, :], m.kv_w_lo[:, k, :])
                            for k in range(KT)]).then_inc(proj_full[t % 2], 1)
            pe.wait_ge(w_split, 2)
            for c, (col, w) in enumerate(CHUNKS):
                b, nth = (1, 4) if c == 0 else (0, 5) if c == 1 else (1, 5)
                pe.wait_ge(proj_free[b], nth)
                three_pass(pe, bank[6 + b][:, 0:w],
                           [(m.g_w_hi[:, k, 0:DH], m.g_w_lo[:, k, 0:DH], m.act_hi[:, k, col:col + w], m.act_lo[:, k, col:col + w])
                            for k in range(KT)]).then_inc(proj_full[b], 1)
            pe.wait_ge(f_step, 12)
            for n, src in enumerate((log_f, f_cum)):
                for t in range(NT):
                    c, w = tile_cols(t)
                    last = pe.transpose(bank[1 + n][0:w, HEADS * t:HEADS * t + HEADS], src[:, c:c + w], ident[0:HEADS, 0:HEADS])
                last.then_inc(f_nat_full, 1)

        @block.scalar
        def _(act):
            act.wait_ge(const_loaded, 32)
            act.wait_ge(ones_ready, 1)

            def squares(t):
                c, w = tile_cols(t)
                act.wait_ge(x_loaded[t], 32 if t == 0 else 16)
                if t > 0:
                    act.wait_ge(squared, t)
                act.activation(square[0:w, :], x_nat[0:w, t, :], ACT.Square, accum_out=ssq[0:w, t:t + 1]).then_inc(squared, 1)

            for t in range(4):
                squares(t)
            for n, (g, k) in enumerate(parts):
                tiles, col, width = GROUPS[g]
                act.wait_ge(part_full, n + 1)
                act.activation(m.act_hi[:, k, col:col + width], bank[n % 4][:, 0:width], ACT.Copy,
                               scale=a_gain[:, k:k + 1]).then_inc(part_rounded, 1)
                if k == KT - 1 and g < 2:
                    for t in GROUPS[g + 1][0]:
                        squares(t)
            act.wait_ge(rms_step_v, 1)
            act.activation(rms_ln[:, :], ssq[:, :], ACT.Ln).then_inc(rms_step_a, 1)
            act.wait_ge(rms_step_a, 1)
            act.activation(m.rms_rows[:, :], rms_ln[:, :], ACT.Exp, scale=-0.5).then_inc(rms_step_a, 1)
            for g, (tiles, col, width) in enumerate(GROUPS):
                act.wait_ge(rms_full, g + 1)
                act.activation(m.rms_cols[:, col:col + width], bank[3 + g][:, 0:width], ACT.Copy).then_inc(rms_ready, 1)
            for t in range(NT):
                if t == 3:
                    act.wait_ge(f_step, 5)
                    act.activation(f_exp[:, :], f_abs[:, :], ACT.Exp, scale=-1.0).then_inc(f_act, 1)
                if t == 4:
                    act.wait_ge(f_step, 6)
                    act.activation(log_f[:, 0:T], f_abs[:, :], ACT.Ln).then_inc(f_act, 1)
                w = tile_cols(t)[1]
                act.wait_ge(proj_full[t % 2], t // 2 + 1)
                act.activation(m.kv_nat[0:w, t, :], bank[6 + t % 2][0:w, 0:2 * DH], ACT.Copy,
                               scale=m.rms_rows[0:w, t:t + 1]).then_inc(proj_free[t % 2], 1)

        @block.vector
        def _(dve):
            def part_low(n):
                g, k = parts[n]
                tiles, col, width = GROUPS[g]
                dve.wait_ge(part_rounded, n + 1)
                if n >= 3:
                    dve.wait_ge(xt_stored[n % 3], 16 * (n // 3))
                dve.tensor_copy(xt[:, n % 3, 0:width], bank[n % 4][:, 0:width]).then_inc(xt_ready, 1)
                dve.scalar_tensor_tensor(out=m.act_lo[:, k, col:col + width], in0=bank[n % 4][:, 0:width], scalar=a_gain[:, k:k + 1],
                                         in1=m.act_hi[:, k, col:col + width].bitcast(F32), op0=ALU.mult,
                                         op1=ALU.subtract).then_inc(part_free, 1)

            def newton_small():
                dve.wait_ge(rms_step_a, 2)
                y, v = m.rms_rows[:, :], ssq[:, :]
                dve.tensor_tensor(rms_t[:, :], y, y, ALU.mult).then_inc(rms_step_v, 1)
                dve.wait_ge(rms_step_v, 2)
                dve.scalar_tensor_tensor(out=rms_t[:, :], in0=rms_t[:, :], scalar=-0.5, in1=v, op0=ALU.mult, op1=ALU.mult).then_inc(rms_step_v, 1)
                dve.wait_ge(rms_step_v, 3)
                dve.scalar_tensor_tensor(out=y, in0=rms_t[:, :], scalar=1.5, in1=y, op0=ALU.add, op1=ALU.mult).then_inc(rms_step_v, 1)
                dve.wait_ge(rms_step_v, 4)
                for t in range(NT):
                    dve.tensor_scalar(diag[:, t, :], ident[:, :], m.rms_rows[:, t:t + 1], None, ALU.mult).then_inc(diag_ready, 1)

            for n in range(len(parts)):
                part_low(n)
            dve.wait_ge(squared, NT)
            dve.tensor_scalar(ssq[:, :], ssq[:, :], 1.0 / D, EPS, ALU.mult, ALU.add).then_inc(rms_step_v, 1)
            newton_small()
            dve.wait_ge(rms_ready, 3)
            for c, (col, w) in enumerate(CHUNKS):
                dve.wait_ge(f_full, c + 1)
                last = dve.tensor_tensor(f[:, col:col + w], bank[c][0:HEADS, 0:w], m.rms_cols[0:HEADS, col:col + w], ALU.mult)
            last.then_inc(f_step, 1)
            dve.wait_ge(f_step, 1)
            dve.tensor_scalar(f[:, :], f[:, :], b_f[:, 0:1], None, ALU.add).then_inc(f_step, 1)
            dve.wait_ge(f_cache_full, 1)
            dve.tensor_copy(log_f[:, T:T + PAST], bank[0][0:HEADS, :]).then_inc(f_step, 1)
            dve.wait_ge(f_step, 3)
            dve.tensor_scalar(f_abs[:, :], f[:, :], -1.0, None, ALU.mult).then_inc(f_step, 1)
            dve.wait_ge(f_step, 4)
            dve.tensor_tensor(f_abs[:, :], f_abs[:, :], f[:, :], ALU.max).then_inc(f_step, 1)
            dve.wait_ge(f_act, 1)
            dve.tensor_scalar(f_abs[:, :], f_exp[:, :], 1.0, None, ALU.add).then_inc(f_step, 1)
            dve.wait_ge(f_act, 2)
            dve.scalar_tensor_tensor(out=f_exp[:, :], in0=f_abs[:, :], scalar=-1.0, in1=f_exp[:, :], op0=ALU.add,
                                     op1=ALU.subtract).then_inc(f_step, 1)
            dve.wait_ge(f_step, 7)
            dve.tensor_tensor(f_exp[:, :], f_exp[:, :], log_f[:, 0:T], ALU.subtract).then_inc(f_step, 1)
            dve.wait_ge(f_step, 8)
            dve.scalar_tensor_tensor(out=log_f[:, 0:T], in0=f[:, :], scalar=0.0, in1=f_exp[:, :], op0=ALU.min,
                                     op1=ALU.add).then_inc(f_step, 1)
            dve.wait_ge(f_step, 9)
            dve.tensor_tensor_scan(f_cum[:, N_SAMPLE:T], row_ones[:, N_SAMPLE:T], log_f[:, N_SAMPLE:T], 0.0, ALU.mult, ALU.add).then_inc(f_step, 1)
            dve.tensor_tensor_scan(f_cum[:, T:T + PAST], row_ones[:, 0:PAST], log_f[:, T:T + PAST], 0.0, ALU.mult, ALU.add).then_inc(f_step, 1)
            dve.wait_ge(f_step, 11)
            dve.tensor_tensor_scan(f_cum[:, 0:N_SAMPLE], row_ones[:, 0:N_SAMPLE], log_f[:, 0:N_SAMPLE],
                                   f_cum[:, T + PAST - 1:T + PAST], ALU.mult, ALU.add).then_inc(f_step, 1)
            for c, (col, w) in enumerate(CHUNKS):
                b, nth = (1, 4) if c == 0 else (0, 5) if c == 1 else (1, 5)
                dve.wait_ge(proj_full[b], nth + 1)
                dve.scalar_tensor_tensor(out=m.query_32[:, col:col + w], in0=bank[6 + b][:, 0:w], scalar=-FOX_SCALE,
                                         in1=m.rms_cols[:, col:col + w], op0=ALU.mult, op1=ALU.mult).then_inc(proj_free[b], 1)
            dve.wait_ge(f_nat_full, 2)
            dve.tensor_copy(log_f_nat[0:SMALL, 0, :], bank[1][0:SMALL, 0:HEADS])
            dve.tensor_copy(log_f_nat[:, 1:NT, :], bank[1][:, HEADS:NT * HEADS].rearrange("p (t h) -> p t h", h=HEADS)).then_inc(f_step, 1)
            dve.tensor_scalar(m.f_query_all[0:SMALL, :, 0], bank[2][0:SMALL, 0:HEADS], -1.0, None, ALU.mult)
            dve.tensor_scalar(m.f_query_all[:, :, 1:NT].rearrange("p h t -> p t h"),
                              bank[2][:, HEADS:NT * HEADS].rearrange("p (t h) -> p t h", h=HEADS), -1.0, None, ALU.mult)


class Dram:

    def __init__(self, nc, a, outs):
        self.x_prompt, self.x_sample, self.meta = a["x_prompt"][0], a["x_sample"][0], a["meta"]
        self.cache_k = a["cache_fox_k"][0, 0].rearrange("t h d -> t (h d)")
        self.cache_v = a["cache_fox_v"][0, 0].rearrange("t h d -> t (h d)")
        self.cache_f = a["cache_fox_logf"][0, 0]
        self.cache_c, self.cache_r = a["cache_mla_ckv"][0], a["cache_mla_krope"][0]
        self.a_norm, self.a_b_forget, self.a_w_in = a["a_norm"], a["a_b_forget"], a["a_w_in"][0]
        self.a_w_out, self.b_w_out = a["a_w_out"][0], a["b_w_out"][0]
        self.kv_norm, self.kv_lat_norm, self.b_norm = a["kv_norm"], a["kv_lat_norm"], a["b_norm"]
        self.w_dkv, self.b_w_in = a["w_dkv"], a["b_w_in"][0]
        self.b_q_norm, self.b_w_uq, self.ukv = a["b_q_norm"], a["b_w_uq"][0], a["w_ukv"]
        self.final_norm = a["final_norm"]
        self.ident, self.rotate, self.cos, self.sin, self.masks = a["ident"], a["rotate"], a["cos"], a["sin"], a["masks"]
        (y_p, y_s, k_p, v_p, f_p, c_p, r_p, k_s, v_s, f_s, c_s, r_s) = outs
        self.y_prompt, self.y_sample = y_p[0], y_s[0]
        self.new_k_prompt, self.new_v_prompt = (x[0, 0].rearrange("t h d -> t (h d)") for x in (k_p, v_p))
        self.new_k_sample, self.new_v_sample = (x[0, 0].rearrange("t h d -> t (h d)") for x in (k_s, v_s))
        self.new_f_prompt, self.new_f_sample = f_p[0, 0], f_s[0, 0]
        self.new_c_prompt, self.new_c_sample, self.new_r_prompt, self.new_r_sample = c_p[0], c_s[0], r_p[0], r_s[0]

        def scratch(name, shape):
            return nc.dram_tensor(name, shape, F32, kind="Internal").ap()

        self.resid = scratch("resid", [D, T])
        self.f_cum = scratch("f_cum", [HEADS, T + PAST])
        self.gated = scratch("gated", [D, T])
        self.gated_b = scratch("gated_b", [D, T])
        self.resid_b = scratch("resid_b", [D, T])
        self.q_nope = scratch("q_nope", [D, T])
        self.q_rope = nc.dram_tensor("q_rope", [D, T], F32R, kind="Internal").ap()
        self.q_rope_small = scratch("q_rope_small", [HEADS * ROPE, SMALL])

    def fox_w(self, sec, h):
        start = (0, D, 2 * D, 3 * D + HEADS)[sec]
        return self.a_w_in[:, bass.ds(start + h * DH, DH)].rearrange("(k p) n -> p k n", p=P)

    def w_ukv(self, h):
        return self.ukv[:, bass.ds(h * 2 * DH, 2 * DH)].rearrange("(k p) n -> p k n", p=P)

    def w_gate(self, h):
        return self.b_w_in[:, bass.ds(Q_LORA + h * DH, DH)].rearrange("(k p) n -> p k n", p=P)


def out_projection(nc, m, dram, name, gated_src, w_out, resid_src, resid_dst, final):
    bank = m.bank
    with ExitStack() as st:
        sems = []
        st.callback(nc.all_engine_barrier)
        st.callback(nc.clear_and_free_semaphores, sems)

        def sb(n, shape, dtype=F32):
            return st.enter_context(nc.sbuf_tensor(name + n, shape, dtype))

        def sem(n):
            sems.append(nc.alloc_semaphore(name + n))
            return sems[-1]

        o_in = sb("o_in", [P, 2, T])
        o_hi, o_lo = sb("o_hi", [P, HEADS, T], F32R), sb("o_lo", [P, HEADS, T], F32R)
        w_in = sb("w_in", [P, 2, KT, P])
        w_hi = [sb("w_hi0", [P, KT, P], F32R), sb("w_hi1", [P, KT, P], F32R)]
        w_lo = [sb("w_lo0", [P, KT, P], F32R), sb("w_lo1", [P, KT, P], F32R)]
        resid = sb("resid", [P, 2, T])
        if not final:
            square, sq_sum = sb("square", [P, T]), sb("sq_sum", [P, T])
            sq_hi, sq_lo = o_hi[:, 0, :], o_lo[:, 0, :]
            ones = sb("ones", [P, P], F32R)
        o_loaded, o_rounded, o_split = [sem("o_loaded0"), sem("o_loaded1")], sem("o_rounded"), sem("o_split")
        w_loaded, w_rounded, w_split = [sem("w_loaded0"), sem("w_loaded1")], sem("w_rounded"), sem("w_split")
        y_full, y_summed = sem("y_full"), sem("y_summed")
        r_loaded, r_stored = [sem("r_loaded0"), sem("r_loaded1")], [sem("r_stored0"), sem("r_stored1")]
        x_rounded, x_split, squared, sq_added = sem("x_rounded"), sem("x_split"), sem("squared"), sem("sq_added")
        stat_split, stat_full, stat_v, stat_a = sem("stat_split"), sem("stat_full"), sem("stat_v"), sem("stat_a")
        ones_ready, pool_waited = sem("ones_ready"), sem("pool_waited")
        PAIRS = KT // 2
        block = st.enter_context(nc.Block())

        def w_cols(fb):
            return w_out[:, bass.ds(fb * P, P)].rearrange("(k p) n -> p k n", p=P)

        @block.sync
        def _(sp):
            def load_w(fb, q):
                sp.dma_start(w_in[:, q, :, :], w_cols(fb)).then_inc(w_loaded[q], 16)

            def load_resid(fb, q):
                sp.dma_start(resid[:, q, :], resid_src[bass.ds(fb * P, P), :]).then_inc(r_loaded[q], 16)

            load_w(0, 0)
            for h in range(HEADS):
                if h >= 2:
                    sp.wait_ge(o_split, h - 1)
                sp.dma_start(o_in[:, h % 2, :], gated_src[h * DH:h * DH + DH, :]).then_inc(o_loaded[h % 2], 16)
                if h == 0:
                    load_w(1, 1)
            load_resid(0, 0)
            load_resid(1, 1)

            def pair(i, last):
                for q in range(2):
                    if not last:
                        sp.wait_ge(w_split, 2 * i + q + 1)
                        load_w(2 * i + q + 2, q)
                for q in range(2):
                    if not final:
                        sp.wait_ge(y_summed, 2 * i + q + 1)
                        sp.dma_start(resid_dst[bass.ds((2 * i + q) * P, P), :], resid[:, q, :]).then_inc(r_stored[q], 16)
                for q in range(2):
                    if not last:
                        if final:
                            sp.wait_ge(y_summed, 2 * i + q + 1)
                        else:
                            sp.wait_ge(r_stored[q], 16 * i + 16)
                            sp.wait_ge(x_split, 2 * i + q + 1)
                            sp.wait_ge(squared, 2 * i + q + 1)
                        load_resid(2 * i + q + 2, q)

            with sp.Fori(0, PAIRS - 1) as i:
                pair(i, False)
            pair(PAIRS - 1, True)
            if not final:
                for q in range(2):
                    sp.wait_ge(r_stored[q], 16 * PAIRS)

        @block.gpsimd
        def _(pool):
            if not final:
                pool.memset(sq_sum[:, :], 0.0).then_inc(sq_added, 1)
                pool.memset(ones[:, :].bitcast(F32), 1.0).then_inc(ones_ready, 1)

            def split(i, q):
                n = 2 * i + q
                wait_apart(pool, w_loaded[q], 16 * i + 16, pool_waited)
                wait_apart(pool, y_full, 6 * i, pool_waited)
                pool.tensor_scalar(w_hi[q][:, :, :], w_in[:, q, :, :], 1.0, 0.0, ALU.mult, ALU.add).then_inc(w_rounded, 1)
                pool.wait_ge(w_rounded, n + 1)
                pool.tensor_tensor(w_lo[q][:, :, :], w_in[:, q, :, :], w_hi[q][:, :, :].bitcast(F32), ALU.subtract).then_inc(w_split, 1)

            def add(i, q):
                wait_apart(pool, squared, 2 * i + q + 1, pool_waited)
                pool.wait_ge(sq_added, 2 * i + q + 1)
                pool.tensor_tensor(sq_sum[:, :], sq_sum[:, :], square[:, :], ALU.add).then_inc(sq_added, 1)

            split(0, 0)
            split(0, 1)
            if not final:
                pool.wait_ge(ones_ready, 1)
            with pool.Fori(0, PAIRS - 1) as i:
                for q in range(2):
                    if not final:
                        add(i, q)
                    wait_apart(pool, y_full, 6 * i + 3 * q + 3, pool_waited)
                    n = 2 * i + q + 2
                    wait_apart(pool, w_loaded[q], 16 * i + 32, pool_waited)
                    pool.tensor_scalar(w_hi[q][:, :, :], w_in[:, q, :, :], 1.0, 0.0, ALU.mult, ALU.add).then_inc(w_rounded, 1)
                    pool.wait_ge(w_rounded, n + 1)
                    pool.tensor_tensor(w_lo[q][:, :, :], w_in[:, q, :, :], w_hi[q][:, :, :].bitcast(F32), ALU.subtract).then_inc(w_split, 1)
            if not final:
                for q in range(2):
                    add(PAIRS - 1, q)

        @block.tensor
        def _(pe):
            def product(i, q, k, c):
                col, w = CHUNKS[c]
                out = bank[3 * q + c][:, 0:w]
                pe.matmul(out, w_hi[q][:, k, :], o_hi[:, k, col:col + w], start=k == 0, stop=False)
                pe.matmul(out, w_hi[q][:, k, :], o_lo[:, k, col:col + w], start=False, stop=False)
                last = pe.matmul(out, w_lo[q][:, k, :], o_hi[:, k, col:col + w], start=False, stop=k == KT - 1)
                if k == KT - 1:
                    last.then_inc(y_full, 1)

            pe.wait_ge(w_split, 2)
            for k in range(KT):
                pe.wait_ge(o_split, k + 1)
                for q in range(2):
                    for c in range(3):
                        product(0, q, k, c)
            with pe.Fori(1, PAIRS) as i:
                for q in range(2):
                    pe.wait_ge(w_split, 2 * i + q + 1)
                    pe.wait_ge(y_summed, 2 * i + q - 1)
                    for c in range(3):
                        for k in range(KT):
                            product(i, q, k, c)
            if not final:
                pe.wait_ge(stat_split, 1)
                for c, (col, w) in enumerate(CHUNKS):
                    b = (6, 7, 0)[c]
                    if c == 2:
                        pe.wait_ge(y_summed, KT)
                    pe.matmul(bank[b][:, 0:w], ones[:, :], sq_hi[:, col:col + w], start=True, stop=False)
                    pe.matmul(bank[b][:, 0:w], ones[:, :], sq_lo[:, col:col + w], start=False, stop=True).then_inc(stat_full, 1)

        @block.scalar
        def _(act):
            for h in range(HEADS):
                act.wait_ge(o_loaded[h % 2], 16 * (h // 2) + 16)
                act.activation(o_hi[:, h, :], o_in[:, h % 2, :], ACT.Copy).then_inc(o_rounded, 1)
            if not final:
                act.wait_ge(ones_ready, 1)

                def tile(i, q):
                    n = 2 * i + q
                    act.wait_ge(y_summed, n + 1)
                    act.activation(m.act_hi[:, bass.ds(n, 1), :].rearrange("p a t -> p (a t)"), resid[:, q, :], ACT.Copy).then_inc(x_rounded, 1)
                    act.wait_ge(sq_added, n + 1)
                    act.activation(square[:, :], resid[:, q, :], ACT.Square).then_inc(squared, 1)

                with act.Fori(0, PAIRS) as i:
                    for q in range(2):
                        tile(i, q)
                act.wait_ge(sq_added, KT + 1)
                act.wait_ge(y_full, 3 * KT)
                act.activation(sq_hi, sq_sum[:, :], ACT.Copy).then_inc(stat_a, 1)
                act.wait_ge(stat_v, 1)
                act.activation(square[:, :], sq_sum[:, :], ACT.Ln).then_inc(stat_a, 1)
                act.wait_ge(stat_a, 2)
                act.activation(m.rms_cols[:, :], square[:, :], ACT.Exp, scale=-0.5).then_inc(stat_a, 1)

        @block.vector
        def _(dve):
            for h in range(HEADS):
                dve.wait_ge(o_rounded, h + 1)
                dve.tensor_tensor(o_lo[:, h, :], o_in[:, h % 2, :], o_hi[:, h, :].bitcast(F32), ALU.subtract).then_inc(o_split, 1)

            def tile(i, q):
                n = 2 * i + q
                dve.wait_ge(r_loaded[q], 16 * i + 16)
                for c, (col, w) in enumerate(CHUNKS):
                    dve.wait_ge(y_full, 3 * n + c + 1)
                    dst = m.stream[:, bass.ds(n, 1), col:col + w].rearrange("p a t -> p (a t)") if final else resid[:, q, col:col + w]
                    last = dve.tensor_tensor(dst, bank[3 * q + c][:, 0:w], resid[:, q, col:col + w], ALU.add)
                last.then_inc(y_summed, 1)
                if not final:
                    dve.wait_ge(x_rounded, n + 1)
                    dve.tensor_tensor(m.act_lo[:, bass.ds(n, 1), :].rearrange("p a t -> p (a t)"), resid[:, q, :],
                                      m.act_hi[:, bass.ds(n, 1), :].rearrange("p a t -> p (a t)").bitcast(F32), ALU.subtract).then_inc(x_split, 1)

            with dve.Fori(0, PAIRS) as i:
                for q in range(2):
                    tile(i, q)
            if not final:
                dve.wait_ge(stat_a, 1)
                dve.tensor_tensor(sq_lo, sq_sum[:, :], sq_hi.bitcast(F32), ALU.subtract).then_inc(stat_split, 1)
                newton_cols(dve, [bank[6], bank[7], bank[0]], stat_full, stat_v, stat_a, 3, D, sq_sum, square, m.rms_cols)


def newton_cols(dve, banks, full, step_v, step_a, a_count, n_features, var, tmp, y):
    for c, (col, w) in enumerate(CHUNKS):
        dve.wait_ge(full, c + 1)
        last = dve.tensor_scalar(var[:, col:col + w], banks[c][:, 0:w], 1.0 / n_features, EPS, ALU.mult, ALU.add)
    last.then_inc(step_v, 1)
    dve.wait_ge(step_a, a_count)
    dve.tensor_tensor(tmp[:, :], y[:, :], y[:, :], ALU.mult).then_inc(step_v, 1)
    dve.wait_ge(step_v, 2)
    dve.scalar_tensor_tensor(out=tmp[:, :], in0=tmp[:, :], scalar=-0.5, in1=var[:, :], op0=ALU.mult, op1=ALU.mult).then_inc(step_v, 1)
    dve.wait_ge(step_v, 3)
    dve.scalar_tensor_tensor(out=y[:, :], in0=tmp[:, :], scalar=1.5, in1=y[:, :], op0=ALU.add, op1=ALU.mult).then_inc(step_v, 1)
    dve.wait_ge(step_v, 4)


def latents(nc, m, dram):
    bank = m.bank
    ident = m.ident
    with ExitStack() as st:
        sems = []
        st.callback(nc.all_engine_barrier)
        st.callback(nc.clear_and_free_semaphores, sems)

        def sb(name, shape, dtype=F32):
            return st.enter_context(nc.sbuf_tensor("lat_" + name, shape, dtype))

        def sem(name):
            sems.append(nc.alloc_semaphore("lat_" + name))
            return sems[-1]

        KQ, KC = Q_LORA // P, KV_LORA // P
        BLOCKS = KQ + KC + 1
        KR = BLOCKS - 1
        RING = 3
        NATW = KV_LORA + ROPE
        stage = sb("stage", [P, RING, KT * P])
        nat = stage[:, :, :].rearrange("p a b -> p (a b)")[:, 0:NT * NATW].rearrange("p (t n) -> p t n", n=NATW)
        w_hi = [sb("w_hi0", [P, KT, P], F32R), sb("w_hi1", [P, KT, P], F32R)]
        w_lo = [sb("w_lo0", [P, KT, P], F32R), sb("w_lo1", [P, KT, P], F32R)]
        b_gain, kv_gain, q_gain, c_gain = sb("b_gain", [P, KT]), sb("kv_gain", [P, KT]), sb("q_gain", [P, KQ]), sb("c_gain", [P, KC])
        rotate_r, ones = sb("rotate_r", [P, P], F32R), sb("ones", [P, P], F32R)
        latent = sb("latent", [P, KC, T])
        cached = latent[:, :, :].rearrange("p a b -> p (a b)")[:, 0:NC * NATW].rearrange("p (t n) -> p t n", n=NATW)
        rope_k = sb("rope_k", [P, T])
        rotate = rope_k[:, 0:P]
        part_hi, part_lo = sb("part_hi", [P, T], F32R), sb("part_lo", [P, T], F32R)
        sq_sum, square, c_factor = sb("sq_sum", [P, T]), sb("square", [P, T]), sb("c_factor", [P, T])

        gains_loaded, cache_loaded = sem("gains_loaded"), sem("cache_loaded")
        w_loaded, w_scaled, w_rounded, w_split = [sem(f"w_loaded{r}") for r in range(RING)], sem("w_scaled"), sem("w_rounded"), sem("w_split")
        const_ready, rotate_ready = sem("const_ready"), sem("rotate_ready")
        cache_full, cache_rounded, cache_taken = sem("cache_full"), sem("cache_rounded"), sem("cache_taken")
        lat_full, lat_rounded, lat_taken = sem("lat_full"), sem("lat_rounded"), sem("lat_taken")
        squared, sq_added = sem("squared"), sem("sq_added")
        part_rounded, part_split = sem("part_rounded"), sem("part_split")
        sum_full, sum_taken, root = sem("sum_full"), sem("sum_taken"), sem("root")
        turned_full, vec_step = sem("turned_full"), sem("vec_step")
        rope_done, c_done, c_rounded, k_rounded = sem("rope_done"), sem("c_done"), sem("c_rounded"), sem("k_rounded")
        nat_full, nat_taken, stored = sem("nat_full"), sem("nat_taken"), sem("stored")
        block = st.enter_context(nc.Block())

        @block.sync
        def _(sp):
            for n in range(BLOCKS):
                r = n % RING
                if n >= RING:
                    sp.wait_ge(w_split, n - RING + 1)
                if n < KQ:
                    src = dram.b_w_in[:, P * n:P * n + P]
                else:
                    src = dram.w_dkv[:, P * (n - KQ):P * (n - KQ) + P] if n < KR else dram.w_dkv[:, KV_LORA:KV_LORA + ROPE]
                dst = stage[:, r, :].rearrange("p (k n) -> p k n", n=P)
                if n < KR:
                    sp.dma_start(dst, src.rearrange("(k p) n -> p k n", p=P)).then_inc(w_loaded[r], 16)
                else:
                    for half in (0, ROPE):
                        sp.dma_start(dst[:, :, half:half + ROPE], src.rearrange("(k p) n -> p k n", p=P)).then_inc(w_loaded[r], 16)
                if n == 0:
                    for dst_, src_ in ((b_gain, dram.b_norm), (kv_gain, dram.kv_norm), (q_gain, dram.b_q_norm),
                                       (c_gain, dram.kv_lat_norm), (rotate, dram.rotate), (m.cos, dram.cos), (m.sin, dram.sin)):
                        sp.dma_start(dst_[:, :], src_).then_inc(gains_loaded, 16)
                    sp.dma_start(cached[:, :, 0:KV_LORA], dram.cache_c.rearrange("(t p) n -> p t n", p=P)).then_inc(cache_loaded, 16)
                    sp.dma_start(cached[:, :, KV_LORA:NATW], dram.cache_r.rearrange("(t p) n -> p t n", p=P)).then_inc(cache_loaded, 16)
            sp.wait_ge(nat_taken, NT)
            for dst_p, dst_s, c0, c1 in ((dram.new_c_prompt, dram.new_c_sample, 0, KV_LORA),
                                         (dram.new_r_prompt, dram.new_r_sample, KV_LORA, NATW)):
                sp.dma_start(dst_s, nat[0:N_SAMPLE, 0, c0:c1]).then_inc(stored, 16)
                sp.dma_start(dst_p[0:N_META, :], nat[N_SAMPLE:SMALL, 0, c0:c1]).then_inc(stored, 16)
                sp.dma_start(dst_p[N_META:L, :].rearrange("(t p) d -> p t d", p=P), nat[:, 1:NT, c0:c1]).then_inc(stored, 16)
            sp.wait_ge(stored, 96)

        @block.gpsimd
        def _(pool):
            pool.memset(ones[:, :].bitcast(F32), 1.0).then_inc(const_ready, 1)
            pool.wait_ge(gains_loaded, 16 * 7)
            pool.tensor_scalar(rotate_r[:, :], rotate, 1.0, 0.0, ALU.mult, ALU.add).then_inc(rotate_ready, 1)

            def add(n):
                if n < KQ:
                    pool.wait_ge(lat_rounded, 3 * n + 3)
                else:
                    pool.wait_ge(squared, n - KQ + 1)
                pool.tensor_tensor(sq_sum[:, :], sq_sum[:, :], square[:, :], ALU.add).then_inc(sq_added, 1)

            for n in range(BLOCKS):
                r = n % RING
                pool.wait_ge(w_loaded[r], 16 * (n // RING) + (32 if n == KR else 16))
                w = stage[:, r, :].rearrange("p (k n) -> p k n", n=P)
                gain = b_gain if n < KQ else kv_gain
                for k in range(KT):
                    last = pool.tensor_scalar(w[:, k, :], w[:, k, :], gain[:, k:k + 1], 1.0, ALU.mult, ALU.mult)
                last.then_inc(w_scaled, 1)
                pool.wait_ge(w_scaled, n + 1)
                if n >= 2:
                    pool.wait_ge(lat_full, 3 * (n - 1))
                pool.tensor_scalar(w_hi[n % 2][:, :, :], w, 1.0, 0.0, ALU.mult, ALU.add).then_inc(w_rounded, 1)
                pool.wait_ge(w_rounded, n + 1)
                pool.tensor_tensor(w_lo[n % 2][:, :, :], w, w_hi[n % 2][:, :, :].bitcast(F32), ALU.subtract).then_inc(w_split, 1)
                if n == 2:
                    add(1)
                elif n == 3:
                    pool.wait_ge(sq_added, 1)
                    add(2)
            add(4)

        @block.tensor
        def _(pe):
            def block_products(n):
                if n >= 2:
                    pe.wait_ge(lat_taken, 3 * (n - 1))
                pe.wait_ge(w_split, n + 1)
                for c, (col, w) in enumerate(CHUNKS):
                    if n == 1 and c == 2:
                        pe.wait_ge(cache_taken, 3)
                    three_pass(pe, bank[3 * (n % 2) + c][:, 0:w],
                               [(w_hi[n % 2][:, k, :], w_lo[n % 2][:, k, :], m.act_hi[:, k, col:col + w], m.act_lo[:, k, col:col + w])
                                for k in range(KT)]).then_inc(lat_full, 1)

            def sums(which):
                pe.wait_ge(part_split, (1, 3)[which])
                for c, (col, w) in enumerate(CHUNKS):
                    pe.matmul(bank[(6, 7, 0)[c]][:, 0:w], ones[:, :], part_hi[:, col:col + w], start=True, stop=False)
                    pe.matmul(bank[(6, 7, 0)[c]][:, 0:w], ones[:, :], part_lo[:, col:col + w], start=False, stop=True).then_inc(sum_full, 1)

            pe.wait_ge(cache_loaded, 32)
            for k in range(KC):
                for t in range(NC):
                    last = pe.transpose(bank[6 + k][:, P * t:P * t + P], cached[:, t, P * k:P * k + P], ident[:, :])
                last.then_inc(cache_full, 1)
            for t in range(NC):
                last = pe.transpose(bank[5][0:ROPE, P * t:P * t + P], cached[:, t, KV_LORA:NATW], ident[:, :])
            last.then_inc(cache_full, 1)
            pe.wait_ge(const_ready, 1)
            for n in range(4):
                block_products(n)
            pe.wait_ge(lat_taken, 9)
            sums(0)
            pe.wait_ge(sum_taken, 1)
            block_products(4)
            block_products(5)
            pe.wait_ge(rotate_ready, 1)
            pe.wait_ge(part_split, 2)
            pe.wait_ge(lat_taken, 15)
            for c, (col, w) in enumerate(CHUNKS):
                pe.matmul(bank[(6, 7, 0)[c]][:, 0:w], rotate_r[:, :], part_hi[:, col:col + w], start=True, stop=False)
                pe.matmul(bank[(6, 7, 0)[c]][:, 0:w], rotate_r[:, :], part_lo[:, col:col + w], start=False, stop=True).then_inc(turned_full, 1)
            pe.wait_ge(rope_done, 1)
            sums(1)
            pe.wait_ge(sum_taken, 2)
            for t in range(NT):
                c, n = tile_cols(t)
                if t == 0:
                    pe.wait_ge(lat_taken, 18)
                    pe.wait_ge(c_done, 1)
                if t >= 8:
                    pe.wait_ge(nat_taken, t - 7)
                for k in range(KC):
                    pe.transpose(bank[t % 8][0:n, P * k:P * k + P], latent[:, k, c:c + n], ident[:, :])
                pe.transpose(bank[t % 8][0:n, KV_LORA:NATW], rope_k[0:ROPE, c:c + n], ident[0:ROPE, 0:ROPE]).then_inc(nat_full, 1)

        @block.scalar
        def _(act):
            act.wait_ge(gains_loaded, 16 * 7)
            for k in range(KC):
                act.wait_ge(cache_full, k + 1)
                act.activation(m.c_hi[:, k, T:T + PAST], bank[6 + k][:, :], ACT.Copy).then_inc(cache_rounded, 1)

            def squares(n):
                act.wait_ge(lat_taken, 3 * n + 3)
                act.activation((sq_sum if n == KQ else square)[:, :], latent[:, n - KQ, :], ACT.Square).then_inc(squared, 1)

            def sum_root(which, factor):
                act.wait_ge(sq_added, (2, 3)[which])
                if which:
                    act.wait_ge(turned_full, 3)
                act.activation(part_hi[:, :], sq_sum[:, :], ACT.Copy).then_inc(part_rounded, 1)
                act.wait_ge(root, 3 * which + 1)
                act.activation(square[:, :], sq_sum[:, :], ACT.Ln).then_inc(root, 1)
                act.wait_ge(root, 3 * which + 2)
                act.activation(factor[:, :], square[:, :], ACT.Exp, scale=-0.5).then_inc(root, 1)

            for n in range(KQ):
                if n == 2:
                    act.wait_ge(sq_added, 1)
                for c, (col, w) in enumerate(CHUNKS):
                    psum = bank[3 * (n % 2) + c][:, 0:w]
                    act.wait_ge(lat_full, 3 * n + c + 1)
                    act.activation(m.ql_hi[:, n, col:col + w], psum, ACT.Copy, scale=q_gain[:, n:n + 1])
                    act.activation((sq_sum if n == 0 else square)[:, col:col + w], psum, ACT.Square).then_inc(lat_rounded, 1)
            sum_root(0, m.q_factor)
            act.wait_ge(vec_step, 5)
            squares(3)
            squares(4)
            act.wait_ge(lat_taken, 18)
            act.activation(part_hi[:, :], rope_k[:, :], ACT.Copy).then_inc(part_rounded, 1)
            act.wait_ge(rope_done, 1)
            act.activation(m.rope_k_hi[:, :], rope_k[:, :], ACT.Copy).then_inc(k_rounded, 1)
            sum_root(1, c_factor)
            act.wait_ge(c_done, 1)
            act.activation(m.c_hi[:, :, 0:T], latent[:, :, :], ACT.Copy).then_inc(c_rounded, 1)
            for t in range(NT):
                n = tile_cols(t)[1]
                act.wait_ge(nat_full, t + 1)
                act.activation(nat[0:n, t, :], bank[t % 8][0:n, 0:NATW], ACT.Copy).then_inc(nat_taken, 1)

        @block.vector
        def _(dve):
            count = [0]

            def chain(ins):
                ins.then_inc(vec_step, 1)
                count[0] += 1
                dve.wait_ge(vec_step, count[0])

            def factors(which, n_features, factor, scale):
                dve.wait_ge(part_rounded, (1, 3)[which])
                dve.tensor_tensor(part_lo[:, :], sq_sum[:, :], part_hi[:, :].bitcast(F32), ALU.subtract).then_inc(part_split, 1)
                chain(dve.scalar_tensor_tensor(out=factor[:, :], in0=m.rms_cols[:, :], scalar=1.0 / n_features, in1=m.rms_cols[:, :],
                                               op0=ALU.mult, op1=ALU.mult))
                dve.wait_ge(part_split, (1, 3)[which])
                for c, (col, w) in enumerate(CHUNKS):
                    dve.wait_ge(sum_full, 3 * which + c + 1)
                    last = dve.tensor_tensor(sq_sum[:, col:col + w], bank[(6, 7, 0)[c]][:, 0:w], factor[:, col:col + w], ALU.mult)
                last.then_inc(sum_taken, 1)
                dve.wait_ge(sum_taken, which + 1)
                dve.tensor_scalar(sq_sum[:, :], sq_sum[:, :], 1.0, EPS, ALU.mult, ALU.add).then_inc(root, 1)
                dve.wait_ge(root, 3 * which + 3)
                y, var = factor[:, :], sq_sum[:, :]
                chain(dve.tensor_tensor(square[:, :], y, y, ALU.mult))
                chain(dve.scalar_tensor_tensor(out=square[:, :], in0=square[:, :], scalar=-0.5, in1=var, op0=ALU.mult, op1=ALU.mult))
                chain(dve.scalar_tensor_tensor(out=y, in0=square[:, :], scalar=1.5, in1=y, op0=ALU.add, op1=ALU.mult))
                chain(dve.scalar_tensor_tensor(out=y, in0=y, scalar=scale, in1=m.rms_cols[:, :], op0=ALU.mult, op1=ALU.mult))

            dve.wait_ge(gains_loaded, 16 * 7)
            for k in range(KC):
                dve.wait_ge(cache_rounded, k + 1)
                dve.tensor_tensor(m.c_lo[:, k, T:T + PAST], bank[6 + k][:, :], m.c_hi[:, k, T:T + PAST].bitcast(F32),
                                  ALU.subtract).then_inc(cache_taken, 1)
            dve.wait_ge(cache_full, 3)
            dve.tensor_copy(m.rope_k32[0:ROPE, P:P + PAST], bank[5][0:ROPE, :]).then_inc(cache_taken, 1)
            for n in range(KQ):
                for c, (col, w) in enumerate(CHUNKS):
                    dve.wait_ge(lat_rounded, 3 * n + c + 1)
                    dve.scalar_tensor_tensor(out=m.ql_lo[:, n, col:col + w], in0=bank[3 * (n % 2) + c][:, 0:w], scalar=q_gain[:, n:n + 1],
                                             in1=m.ql_hi[:, n, col:col + w].bitcast(F32), op0=ALU.mult, op1=ALU.subtract).then_inc(lat_taken, 1)

            def copy_latent(n):
                for c, (col, w) in enumerate(CHUNKS):
                    dve.wait_ge(lat_full, 3 * n + c + 1)
                    dve.tensor_copy(latent[:, n - KQ, col:col + w], bank[3 * (n % 2) + c][:, 0:w]).then_inc(lat_taken, 1)

            factors(0, Q_LORA, m.q_factor, MLA_SCALE)
            copy_latent(3)
            copy_latent(4)
            dve.wait_ge(rotate_ready, 1)
            for c, (col, w) in enumerate(CHUNKS):
                dve.wait_ge(lat_full, 3 * KR + c + 1)
                dve.tensor_tensor(rope_k[:, col:col + w], bank[3 * (KR % 2) + c][:, 0:w], m.rms_cols[:, col:col + w], ALU.mult).then_inc(lat_taken, 1)
            dve.wait_ge(lat_taken, 18)
            dve.wait_ge(part_rounded, 2)
            dve.tensor_tensor(part_lo[:, :], rope_k[:, :], part_hi[:, :].bitcast(F32), ALU.subtract).then_inc(part_split, 1)
            dve.wait_ge(part_split, 2)
            chain(dve.tensor_tensor(rope_k[:, :], rope_k[:, :], m.cos[:, :], ALU.mult))
            for c, (col, w) in enumerate(CHUNKS):
                dve.wait_ge(turned_full, c + 1)
                last = dve.tensor_tensor(c_factor[:, col:col + w], bank[(6, 7, 0)[c]][:, 0:w], m.sin[:, col:col + w], ALU.mult)
            chain(last)
            dve.tensor_tensor(rope_k[:, :], rope_k[:, :], c_factor[:, :], ALU.add).then_inc(rope_done, 1)
            dve.wait_ge(rope_done, 1)
            dve.tensor_copy(m.rope_k32[:, 0:P], rope_k[:, 0:P])
            dve.wait_ge(k_rounded, 1)
            dve.tensor_tensor(m.rope_k_lo[:, :], rope_k[:, :], m.rope_k_hi[:, :].bitcast(F32), ALU.subtract)
            factors(1, KV_LORA, c_factor, 1.0)
            for k in range(KC):
                last = dve.scalar_tensor_tensor(out=latent[:, k, :], in0=latent[:, k, :], scalar=c_gain[:, k:k + 1], in1=c_factor[:, :],
                                                op0=ALU.mult, op1=ALU.mult)
            last.then_inc(c_done, 1)
            dve.wait_ge(c_rounded, 1)
            dve.tensor_tensor(m.c_lo[:, :, 0:T], latent[:, :, :], m.c_hi[:, :, 0:T].bitcast(F32), ALU.subtract)


def queries(nc, m, dram):
    bank = m.bank
    with ExitStack() as st:
        sems = []
        st.callback(nc.all_engine_barrier)
        st.callback(nc.clear_and_free_semaphores, sems)

        def sb(name, shape, dtype=F32):
            return st.enter_context(nc.sbuf_tensor("q_" + name, shape, dtype))

        def sem(name):
            sems.append(nc.alloc_semaphore("q_" + name))
            return sems[-1]

        KQ, KC = Q_LORA // P, KV_LORA // P
        PW = 2 * QK_HEAD
        PAIRS = HEADS // 2
        W = KQ * PW
        flat = m.kv_nat[:, :, :].rearrange("p t n -> p (t n)")
        stage = [flat[:, W * q:W * q + W].rearrange("p (k a n) -> p k a n", k=KQ, a=2) for q in range(2)]
        g_stage = flat[:, 2 * W:2 * W + KT * DH].rearrange("p (k n) -> p k n", n=DH)
        w_hi = [sb("w_hi0", [P, KQ, PW], F32R), m.g_hi_space[:, 0:W].rearrange("p (k n) -> p k n", k=KQ)]
        w_lo = [sb("w_lo0", [P, KQ, PW], F32R), m.g_lo_space[:, 0:W].rearrange("p (k n) -> p k n", k=KQ)]
        rotate, rotate_r = sb("rotate", [P, P]), sb("rotate_r", [P, P], F32R)
        raw = sb("raw", [P, T])
        raw_hi, raw_lo = sb("raw_hi", [P, T], F32R), sb("raw_lo", [P, T], F32R)
        turned = sb("turned", [P, T])
        rope_hi, rope_lo = raw_hi, raw_lo
        nope = [m.query_32, m.stage_space]

        const_loaded, kv_w_loaded, g_w_loaded = sem("const_loaded"), sem("kv_w_loaded"), sem("g_w_loaded")
        w_loaded, w_rounded, w_split = [sem("w_loaded0"), sem("w_loaded1")], sem("w_rounded"), sem("w_split")
        pool_step = sem("pool_step")
        full, taken = sem("full"), sem("taken")
        raw_rounded, raw_split = sem("raw_rounded"), sem("raw_split")
        cos_done, sin_done, rope_ready, rope_rounded, rope_split = sem("cos_done"), sem("sin_done"), sem("rope_ready"), sem("rope_rounded"), sem("rope_split")
        nope_stored, small_stored, rope_stored = [sem("nope_stored0"), sem("nope_stored1")], sem("small_stored"), sem("rope_stored")
        g_w_split, kv_w_split, kv_full, kv_taken = sem("g_w_split"), sem("kv_w_split"), sem("kv_full"), sem("kv_taken")
        block = st.enter_context(nc.Block())
        USES = 12

        @block.sync
        def _(sp):
            def load_w(n, q):
                for k in range(KQ):
                    sp.dma_start(stage[q][:, k, :, :].rearrange("p a n -> p (a n)"), dram.b_w_uq[P * k:P * k + P, bass.ds(n * PW, PW)]).then_inc(w_loaded[q], 16)

            def store(n):
                for a in range(2):
                    sp.wait_ge(taken, USES * n + 3 * a + 6)
                    sp.dma_start(dram.q_nope[bass.ds((2 * n + a) * P, P), :], nope[a][:, :]).then_inc(nope_stored[a], 16)
                sp.wait_ge(rope_ready, n + 1)
                sp.dma_start(dram.q_rope_small[bass.ds(2 * n * ROPE, P), :], raw[:, 0:SMALL]).then_inc(small_stored, 16)

            sp.dma_start(rotate[:, :], dram.rotate).then_inc(const_loaded, 16)
            load_w(0, 0)
            load_w(1, 1)
            sp.dma_start(g_stage, dram.w_gate(0)).then_inc(g_w_loaded, 16)
            sp.dma_start(m.b_gain[:, :], dram.b_norm).then_inc(g_w_loaded, 16)
            kv_stage = nope[1][:, 0:2 * 2 * DH].rearrange("p (k n) -> p k n", n=2 * DH)
            sp.dma_start(kv_stage, dram.w_ukv(0)).then_inc(kv_w_loaded, 16)
            sp.wait_ge(w_split, 1)
            load_w(2, 0)
            store(0)
            sp.wait_ge(w_split, 2)
            load_w(3, 1)
            store(1)
            store(2)
            store(3)
            for a in range(2):
                sp.wait_ge(nope_stored[a], 16 * PAIRS)
            sp.wait_ge(small_stored, 16 * PAIRS)

        @block.gpsimd
        def _(pool):
            count = [0]

            def chain(ins):
                ins.then_inc(pool_step, 1)
                count[0] += 1
                pool.wait_ge(pool_step, count[0])

            def split(n):
                q = n % 2
                pool.wait_ge(w_loaded[q], 16 * KQ * (n // 2) + 16 * KQ)
                if n >= 2:
                    pool.wait_ge(full, USES * (n - 1))
                parts = []
                for k in range(KQ):
                    for c0, c1, s0, s1 in ((0, 2 * DH, 0, DH), (2 * DH, PW, DH, QK_HEAD)):
                        cut = lambda x: x[q][:, k, c0:c1].rearrange("p (a n) -> p a n", a=2)
                        parts.append((stage[q][:, k, :, s0:s1], cut(w_hi), cut(w_lo)))
                for s, hi, lo in parts:
                    last = pool.tensor_scalar(hi, s, 1.0, 0.0, ALU.mult, ALU.add)
                chain(last)
                for s, hi, lo in parts:
                    last = pool.tensor_tensor(lo, s, hi.bitcast(F32), ALU.subtract)
                last.then_inc(w_split, 1)

            def store_rope(n):
                pool.wait_ge(rope_split, n + 1)
                for a in range(2):
                    for b, part in enumerate((rope_hi, rope_lo)):
                        pool.dma_start(dram.q_rope[P * (2 * n + a) + ROPE * b:P * (2 * n + a) + ROPE * b + ROPE, :],
                                       part[ROPE * a:ROPE * a + ROPE, :]).then_inc(rope_stored, 16)

            pool.wait_ge(const_loaded, 16)
            chain(pool.tensor_scalar(rotate_r[:, :], rotate[:, :], 1.0, 0.0, ALU.mult, ALU.add))
            split(0)
            kv_stage = nope[1][:, 0:2 * 2 * DH].rearrange("p (k n) -> p k n", n=2 * DH)
            pool.wait_ge(kv_w_loaded, 16)
            chain(pool.tensor_scalar(m.kv_w_hi[:, :, :], kv_stage, 1.0, 0.0, ALU.mult, ALU.add))
            pool.tensor_tensor(m.kv_w_lo[:, :, :], kv_stage, m.kv_w_hi[:, :, :].bitcast(F32), ALU.subtract).then_inc(kv_w_split, 1)
            split(1)
            pool.memset(m.mask_big[:, :], -BIG)
            pool.memset(m.mask_rows[:, 64:128], 0.0)
            pool.memset(m.mask_rows[:, 0:64], 1.0)
            pool.memset(m.mask_rows[:, 128:256], 1.0)
            pool.wait_ge(g_w_loaded, 32)
            for k in range(KT):
                last = pool.tensor_scalar(g_stage[:, k, :], g_stage[:, k, :], m.b_gain[:, k:k + 1], 1.0, ALU.mult, ALU.mult)
            chain(last)
            store_rope(0)
            split(2)
            store_rope(1)
            split(3)
            pool.wait_ge(w_split, 4)
            chain(pool.memset(m.kv_nat[:, 0, :], 0.0))
            store_rope(2)
            pool.wait_ge(full, USES * PAIRS)
            chain(pool.tensor_scalar(m.g_w_hi, g_stage, 1.0, 0.0, ALU.mult, ALU.add))
            pool.tensor_tensor(m.g_w_lo, g_stage, m.g_w_hi.bitcast(F32), ALU.subtract).then_inc(g_w_split, 1)
            store_rope(3)
            pool.wait_ge(rope_stored, 16 * 4 * PAIRS)

        @block.tensor
        def _(pe):
            def next_bank(n, u):
                out = bank[(USES * n + u) % 8]
                if USES * n + u >= 8:
                    pe.wait_ge(taken, USES * n + u - 7)
                return out

            pe.wait_ge(pool_step, 1)
            for n in range(PAIRS):
                q = n % 2
                pe.wait_ge(w_split, n + 1)
                for s, lhs in enumerate((slice(2 * DH, PW), slice(0, DH), slice(DH, 2 * DH))):
                    for c, (col, w) in enumerate(CHUNKS):
                        out = next_bank(n, 3 * s + c)
                        three_pass(pe, out[:, 0:w], [(w_hi[q][:, k, lhs], w_lo[q][:, k, lhs], m.ql_hi[:, k, col:col + w], m.ql_lo[:, k, col:col + w])
                                                     for k in range(KQ)]).then_inc(full, 1)
                pe.wait_ge(raw_split, n + 1)
                for c, (col, w) in enumerate(CHUNKS):
                    out = next_bank(n, 9 + c)
                    pe.matmul(out[:, 0:w], rotate_r[:, :], raw_hi[:, col:col + w], start=True, stop=False)
                    pe.matmul(out[:, 0:w], rotate_r[:, :], raw_lo[:, col:col + w], start=False, stop=True).then_inc(full, 1)
            pe.wait_ge(kv_w_split, 1)
            pe.wait_ge(taken, USES * PAIRS)
            for t in range(NT + NC):
                c, n = tile_cols(t) if t < NT else (T + P * (t - NT), P)
                if t >= 8:
                    pe.wait_ge(kv_taken, t - 7)
                three_pass(pe, bank[t % 8][0:n, 0:2 * DH],
                           [(m.c_hi[:, k, c:c + n], m.c_lo[:, k, c:c + n], m.kv_w_hi[:, k, :], m.kv_w_lo[:, k, :]) for k in range(KC)]
                           ).then_inc(kv_full, 1)

        @block.scalar
        def _(act):
            for n in range(PAIRS):
                act.wait_ge(taken, USES * n + 3)
                if n:
                    act.wait_ge(rope_stored, 16 * 4 * n)
                act.activation(raw_hi[:, :], raw[:, :], ACT.Copy).then_inc(raw_rounded, 1)
                act.wait_ge(rope_ready, n + 1)
                act.activation(rope_hi[:, :], raw[:, :], ACT.Copy).then_inc(rope_rounded, 1)
            act.wait_ge(pool_step, 8)
            for t in range(NT + NC):
                n = P if t >= NT else tile_cols(t)[1]
                act.wait_ge(kv_full, t + 1)
                if t == 9:
                    act.wait_ge(g_w_split, 1)
                act.activation(m.kv_nat[0:n, t, :], bank[t % 8][0:n, 0:2 * DH], ACT.Copy).then_inc(kv_taken, 1)

        @block.vector
        def _(dve):
            def take(n, u, dst):
                col, w = CHUNKS[u % 3]
                dve.wait_ge(full, USES * n + u + 1)
                last = dve.tensor_tensor(dst[:, col:col + w], bank[(USES * n + u) % 8][:, 0:w], m.q_factor[:, col:col + w], ALU.mult)
                last.then_inc(taken, 1)

            dve.wait_ge(kv_w_split, 1)
            for n in range(PAIRS):
                if n:
                    dve.wait_ge(rope_split, n)
                    dve.wait_ge(small_stored, 16 * n)
                for u in range(3):
                    take(n, u, raw)
                dve.wait_ge(taken, USES * n + 3)
                dve.wait_ge(raw_rounded, n + 1)
                if n:
                    dve.wait_ge(rope_stored, 16 * 4 * n)
                dve.tensor_tensor(raw_lo[:, :], raw[:, :], raw_hi[:, :].bitcast(F32), ALU.subtract).then_inc(raw_split, 1)
                dve.wait_ge(raw_split, n + 1)
                dve.tensor_tensor(raw[:, :], raw[:, :], m.cos[:, :], ALU.mult).then_inc(cos_done, 1)
                for a in range(2):
                    if n:
                        dve.wait_ge(nope_stored[a], 16 * n)
                    for u in range(3 * a + 3, 3 * a + 6):
                        take(n, u, nope[a])
                for c, (col, w) in enumerate(CHUNKS):
                    u = 9 + c
                    dve.wait_ge(full, USES * n + u + 1)
                    dve.tensor_tensor(turned[:, col:col + w], bank[(USES * n + u) % 8][:, 0:w], m.sin[:, col:col + w], ALU.mult).then_inc(taken, 1)
                dve.wait_ge(taken, USES * n + USES)
                dve.wait_ge(cos_done, n + 1)
                dve.tensor_tensor(raw[:, :], raw[:, :], turned[:, :], ALU.add).then_inc(rope_ready, 1)
                dve.wait_ge(rope_ready, n + 1)
                dve.wait_ge(rope_rounded, n + 1)
                dve.tensor_tensor(rope_lo[:, :], raw[:, :], rope_hi[:, :].bitcast(F32), ALU.subtract).then_inc(rope_split, 1)


def final_norm(nc, m, dram):
    ident = m.ident
    with ExitStack() as st:
        sems = []
        st.callback(nc.all_engine_barrier)
        st.callback(nc.clear_and_free_semaphores, sems)

        def sb(name, shape, dtype=F32):
            return st.enter_context(nc.sbuf_tensor("final_" + name, shape, dtype))

        def sem(name):
            sems.append(nc.alloc_semaphore("final_" + name))
            return sems[-1]

        gain = sb("gain", [P, D])
        square = sb("square", [P, D])
        y = sb("y", [P, 3, D])
        ssq, ln, rms, tmp = sb("ssq", [P, NT]), sb("ln", [P, NT]), sb("rms", [P, NT]), sb("tmp", [P, NT])
        gain_loaded, turned, squared, mean, root, step = sem("gain_loaded"), sem("turned"), sem("squared"), sem("mean"), sem("root"), sem("step")
        y_ready, y_stored = sem("y_ready"), [sem("y_stored0"), sem("y_stored1"), sem("y_stored2")]
        block = st.enter_context(nc.Block())
        RING = 4

        def banks(t, n):
            return m.psum[0:n, 2 * (t % RING):2 * (t % RING) + 2, :]

        def rows(x, n):
            return x.rearrange("p (a b) -> p a b", a=2)

        @block.sync
        def _(sp):
            sp.dma_start(gain[:, :], dram.final_norm.to_broadcast([P, D])).then_inc(gain_loaded, 16)
            for t in range(NT):
                sp.wait_ge(y_ready, t + 1)
                if t == 0:
                    sp.dma_start(dram.y_sample, y[0:N_SAMPLE, 0, :]).then_inc(y_stored[0], 16)
                else:
                    sp.dma_start(dram.y_prompt[P * (t - 1):P * t, :], y[:, t % 3, :]).then_inc(y_stored[t % 3], 16)
            for q in range(3):
                sp.wait_ge(y_stored[q], 16 * (NT // 3))

        @block.tensor
        def _(pe):
            for t in range(NT):
                c, n = tile_cols(t)
                if t >= RING:
                    pe.wait_ge(y_ready, t - RING + 1)
                for k in range(KT):
                    last = pe.transpose(m.bank[2 * (t % RING) + k // 4][0:n, P * (k % 4):P * (k % 4) + P], m.stream[:, k, c:c + n], ident[:, :])
                last.then_inc(turned, 1)

        @block.scalar
        def _(act):
            def squares(t):
                n = tile_cols(t)[1]
                act.wait_ge(turned, t + 1)
                if t:
                    act.wait_ge(squared, t)
                act.activation(rows(square[0:n, :], n), banks(t, n), ACT.Square, accum_out=ssq[0:n, t:t + 1]).then_inc(squared, 1)

            def roots(t):
                n = tile_cols(t)[1]
                act.wait_ge(mean, t + 1)
                act.activation(ln[0:n, t:t + 1], ssq[0:n, t:t + 1], ACT.Ln).then_inc(root, 1)
                act.wait_ge(root, 2 * t + 1)
                act.activation(rms[0:n, t:t + 1], ln[0:n, t:t + 1], ACT.Exp, scale=-0.5).then_inc(root, 1)

            squares(0)
            for t in range(NT):
                if t + 1 < NT:
                    squares(t + 1)
                roots(t)

        @block.vector
        def _(dve):
            def means(t):
                n = tile_cols(t)[1]
                dve.wait_ge(squared, t + 1)
                v = ssq[0:n, t:t + 1]
                dve.tensor_scalar(v, v, 1.0 / D, EPS, ALU.mult, ALU.add).then_inc(mean, 1)

            def scaled(t):
                n = tile_cols(t)[1]
                r, v, x = rms[0:n, t:t + 1], ssq[0:n, t:t + 1], tmp[0:n, t:t + 1]
                dve.wait_ge(root, 2 * t + 2)
                dve.tensor_tensor(x, r, r, ALU.mult).then_inc(step, 1)
                dve.wait_ge(step, 3 * t + 1)
                dve.scalar_tensor_tensor(out=x, in0=x, scalar=-0.5, in1=v, op0=ALU.mult, op1=ALU.mult).then_inc(step, 1)
                dve.wait_ge(step, 3 * t + 2)
                dve.scalar_tensor_tensor(out=r, in0=x, scalar=1.5, in1=r, op0=ALU.add, op1=ALU.mult).then_inc(step, 1)
                dve.wait_ge(step, 3 * t + 3)
                if t >= 3:
                    dve.wait_ge(y_stored[t % 3], 16 * (t // 3))
                dve.scalar_tensor_tensor(out=rows(y[0:n, t % 3, :], n), in0=banks(t, n), scalar=r, in1=rows(gain[0:n, :], n),
                                         op0=ALU.mult, op1=ALU.mult).then_inc(y_ready, 1)

            means(0)
            dve.wait_ge(gain_loaded, 16)
            for t in range(NT):
                if t + 1 < NT:
                    means(t + 1)
                scaled(t)


def build(nc, a, outs):
    dram = Dram(nc, a, outs)
    with ExitStack() as whole:
        m = Memory(nc)
        m.psum = whole.enter_context(nc.psum_tensor("psum", [P, 8, 512], F32))
        m.bank = [m.psum[:, b, :] for b in range(8)]
        m.score_banks = lambda first, n: m.psum[:, first:first + n, :]
        m.ident = m.sbuf(whole, "ident", [P, P])
        with ExitStack() as st:
            m.act_hi = m.sbuf(st, "act_hi", [P, KT, T], F32R)
            m.act_lo = m.sbuf(st, "act_lo", [P, KT, T], F32R)
            m.rms_cols = m.sbuf(st, "rms_cols", [P, T])
            with ExitStack() as fox:
                m.kv_act_hi, m.kv_act_lo = m.act_hi, m.act_lo
                m.query_32 = m.sbuf(fox, "query_32", [P, T])
                m.kv_nat = m.sbuf(fox, "kv_nat", [P, NT, 2 * DH])
                m.rms_rows = m.sbuf(fox, "rms_rows", [P, NT])
                m.f_query_all = m.sbuf(fox, "f_query_all", [P, HEADS, NT])
                m.stage = m.sbuf(fox, "stage", [P, KT, 2 * DH])
                m.kv_w_hi = m.sbuf(fox, "kv_w_hi", [P, KT, 2 * DH], F32R)
                m.kv_w_lo = m.sbuf(fox, "kv_w_lo", [P, KT, 2 * DH], F32R)
                m.g_w_hi = m.sbuf(fox, "g_w_hi", [P, KT, 2 * DH], F32R)
                m.g_w_lo = m.sbuf(fox, "g_w_lo", [P, KT, 2 * DH], F32R)
                embed(nc, m, dram)
                attention(nc, m, True, dram)
            out_projection(nc, m, dram, "mix_", dram.gated, dram.a_w_out, dram.resid, dram.resid_b, False)
            m.prefix = "b_"
            with ExitStack() as mla:
                m.c_hi = m.sbuf(mla, "c_hi", [P, KV_LORA // P, T + PAST], F32R)
                m.c_lo = m.sbuf(mla, "c_lo", [P, KV_LORA // P, T + PAST], F32R)
                m.rope_k_hi = m.sbuf(mla, "rope_k_hi", [P, T], F32R)
                m.rope_k_lo = m.sbuf(mla, "rope_k_lo", [P, T], F32R)
                m.rope_k32 = m.sbuf(mla, "rope_k32", [P, P + PAST])
                with ExitStack() as low:
                    m.ql_hi = m.sbuf(low, "ql_hi", [P, Q_LORA // P, T], F32R, side="right")
                    m.ql_lo = m.sbuf(low, "ql_lo", [P, Q_LORA // P, T], F32R, side="right")
                    m.q_factor = m.sbuf(low, "q_factor", [P, T], side="right")
                    m.cos = m.sbuf(low, "cos", [P, T], side="right")
                    m.sin = m.sbuf(low, "sin", [P, T], side="right")
                    latents(nc, m, dram)
                    m.mask_rows = m.sbuf(mla, "mask_rows", [P, 2 * P], BF16)
                    m.mask_big = m.sbuf(mla, "mask_big", [P, S9W // 2], BF16)
                    m.mask_first = m.mask_rows[:, 0:P]
                    m.mask_sample = m.mask_rows[:, 64 - N_SAMPLE:64 + N_META]
                    m.mask_meta = m.mask_rows[:, P - N_SAMPLE:P + N_META]
                    m.mask_all = m.mask_rows[:, P:2 * P]
                    m.kv_act_hi, m.kv_act_lo = m.c_hi, m.c_lo
                    m.kv_nat = m.sbuf(mla, "kv_nat", [P, NT + NC, 2 * DH])
                    m.kv_w_hi = m.sbuf(mla, "kv_w_hi", [P, KV_LORA // P, 2 * DH], F32R)
                    m.kv_w_lo = m.sbuf(mla, "kv_w_lo", [P, KV_LORA // P, 2 * DH], F32R)
                    m.g_hi_space = m.sbuf(mla, "g_hi_space", [P, QW], F32R)
                    m.g_lo_space = m.sbuf(mla, "g_lo_space", [P, QW], F32R)
                    m.stage_space = m.sbuf(mla, "stage_space", [P, T])
                    m.b_gain = m.sbuf(mla, "b_gain", [P, KT])
                    m.query_32 = m.sbuf(mla, "query_32", [P, T])
                    m.g_w_hi, m.g_w_lo, m.stage = (x[:, 0:KT * DH].rearrange("p (k n) -> p k n", n=DH)
                                                   for x in (m.g_hi_space, m.g_lo_space, m.stage_space))
                    queries(nc, m, dram)
                attention(nc, m, False, dram)
        m.stream = m.sbuf(whole, "stream", [P, KT, T])
        out_projection(nc, m, dram, "end_", dram.gated_b, dram.b_w_out, dram.resid_b, None, True)
        final_norm(nc, m, dram)


def constants():
    pos = np.concatenate([PAST + np.arange(N_SAMPLE), np.arange(L)]).astype(np.float32)
    half = ROPE // 2
    inv = (np.float32(10000.0) ** (-np.arange(half, dtype=np.float32) / np.float32(half))).astype(np.float32)
    ang = (inv[:, None] * pos[None, :]).astype(np.float32)
    rotate = np.zeros((P, P), np.float32)
    for r in range(half):
        for o in (0, ROPE):
            rotate[o + half + r, o + r] = -1.0
            rotate[o + r, o + half + r] = 1.0
    masks = np.zeros((3, P), np.float32)
    masks[0, :64] = 1.0
    masks[1] = 1.0
    masks[2] = -BIG
    return {"ident": np.eye(P, dtype=np.float32), "rotate": rotate,
            "cos": np.tile(np.cos(ang).astype(np.float32), (4, 1)), "sin": np.tile(np.sin(ang).astype(np.float32), (4, 1)),
            "masks": masks}


INPUTS = ["x_prompt", "x_sample", "cache_fox_k", "cache_fox_v", "cache_fox_logf", "cache_mla_ckv", "cache_mla_krope",
          "meta", "a_norm", "a_w_in", "a_b_forget", "a_w_out", "kv_norm", "w_dkv", "kv_lat_norm", "w_ukv", "b_norm",
          "b_w_in", "b_q_norm", "b_w_uq", "b_w_out", "final_norm"]
OUTPUTS = [(1, SEQ, D), (1, N_SAMPLE, D), (1, 1, L, HEADS, DH), (1, 1, L, HEADS, DH), (1, 1, L, HEADS), (1, L, KV_LORA),
           (1, L, ROPE), (1, 1, N_SAMPLE, HEADS, DH), (1, 1, N_SAMPLE, HEADS, DH), (1, 1, N_SAMPLE, HEADS),
           (1, N_SAMPLE, KV_LORA), (1, N_SAMPLE, ROPE)]


def laid_out(inputs):
    arrays = {n: np.asarray(inputs[n]) for n in INPUTS}
    for n in ("a_norm", "kv_norm", "kv_lat_norm", "b_norm", "b_q_norm"):
        arrays[n] = arrays[n].reshape(-1, P).T
    arrays["final_norm"] = arrays["final_norm"].reshape(1, D)
    arrays["a_b_forget"] = arrays["a_b_forget"].reshape(HEADS, 1)
    return {n: np.ascontiguousarray(x) for n, x in arrays.items()} | constants()


def kernel(**inputs):
    import concourse.bacc as bacc
    from concourse.bass_utils import run_bass_kernel_spmd

    nc = bacc.Bacc("TRN2", target_bir_lowering=False, num_devices=1)
    arrays = laid_out(inputs)
    a = {n: nc.dram_tensor(f"in_{n}", x.shape, F32, kind="ExternalInput").ap() for n, x in arrays.items()}
    outs = [nc.dram_tensor(f"out_{i}", s, F32, kind="ExternalOutput").ap() for i, s in enumerate(OUTPUTS)]
    build(nc, a, outs)
    r = run_bass_kernel_spmd(nc, [{f"in_{n}": x for n, x in arrays.items()}], core_ids=[0])
    return tuple(r.results[0][f"out_{i}"] for i in range(len(OUTPUTS)))
```

```python
from contextlib import ExitStack

import numpy as np

import concourse.bass as bass
from concourse import mybir

F32 = mybir.dt.float32
F32R = mybir.dt.float32r
BF16 = mybir.dt.bfloat16
ALU = mybir.AluOpType
ACT = mybir.ActivationFunctionType
AX_X = mybir.AxisListType.X

P = 128
D = 1024
KT = D // P
HEADS = 8
DH = 128
N_SAMPLE, N_META, SEQ, PAST = 32, 16, 1024, 512
L = N_META + SEQ
SMALL = N_SAMPLE + N_META
T = SMALL + SEQ
NT = 1 + SEQ // P
NC = PAST // P
ROPE, KV_LORA, Q_LORA = 64, 256, 384
QK_HEAD = DH + ROPE
QW = Q_LORA // P * 2 * QK_HEAD
FOX_SCALE = DH ** -0.5
MLA_SCALE = QK_HEAD ** -0.5
EPS = 1e-6
BIG = 1e30
FMAX = 3.0e38

CHUNK_W = 358
CHUNKS = [(0, CHUNK_W), (CHUNK_W, CHUNK_W), (2 * CHUNK_W, T - 2 * CHUNK_W)]
GROUPS = [(range(0, 4), 0, SMALL + 3 * P), (range(4, 8), SMALL + 3 * P, 4 * P), (range(8, 9), SMALL + 7 * P, P)]
S9W = (PAST + SMALL) // 2


def tile_cols(t):
    return (0, SMALL) if t == 0 else (SMALL + P * (t - 1), P)


def score_pieces(i):
    end = SMALL + P * (i + 1)
    used = end - N_SAMPLE
    if i == 0:
        return N_SAMPLE, 1, 256, used
    if i < 3:
        return N_SAMPLE, 1, used, used
    if i < 7:
        return N_SAMPLE, 2, used // 2, used
    return end - 3 * 348, 3, 348, 3 * 348


def prob_groups(i):
    blocks = list(range(i + 2))
    return [blocks[n:n + 4] for n in range(0, len(blocks), 4)]


def prob_signals(i):
    return 1 + sum(min(2, len(prob_groups(n))) for n in range(i))


TURNS = [("K", g) for g in range(3)] + [("C", 0), ("S", 0)] + [
    (i, g) for i in range(8) for g in range(len(prob_groups(i)))]
TURNS_PER_BANK = [(len(TURNS) + 1) // 2, len(TURNS) // 2]
SPLIT_TURNS = [u for u in TURNS if u[0] not in ("C", "S")]


def head_steps(fox, last):
    if fox:
        fill = {"start": "g1", 0: "", 1: "g2", 2: "k0", 3: "k1 k2", 4: "k3 k4", 5: "k5", 6: "k6 k7", "end": "k8 q0", "after": "q1 q2"}
    else:
        fill = {"start": "g1", 0: "", 1: "k0 k1", 2: "k2 k3", 3: "k4 k5", 4: "k6 k7", 5: "k8 k9", 6: "g2", "end": "k10 k11 k12", "after": ""}
    kinds = {"g": "gate", "k": "next_kv", "q": "next_q"}

    def filled(slot):
        return [(kinds[f[0]], int(f[1:])) for f in fill[slot].split() if not (last and f[0] in "kq")]

    def gate_done(c):
        return [("gate_tanh", c), ("gate_mul", c)]

    steps = [("turn_keys", 0), ("turn_keys", 1), ("gate", 0), ("split_query", 0), ("turn_keys", 2), ("turn_cache", 0),
             ("small_scores", 0), ("scores", 0), ("small_max", 0), ("max", 0), ("small_exp", 0), ("exp", 0),
             ("small_rescale", 0), ("rescale", 0)]
    steps += gate_done(0) + [("split_values", 0)] + filled("start") + [("turn_small", 0)]
    gate_2, gated_3 = (5, 6) if fox else (7, 7)
    for i in range(8):
        groups = len(prob_groups(i))
        steps += [("turn_probs", (i, g)) for g in range(min(groups, 2))]
        if i < 7:
            steps += [("scores", i + 1), ("max", i + 1)]
        if i == 1:
            steps += gate_done(1) + [("gated", 0)]
        if i == gate_2:
            steps += gate_done(2)
        if i in (2, 4, gated_3):
            steps += [("gated", {2: 1, 4: 2}.get(i, 3))]
        projections = filled(i if i < 7 else "end")
        takes = [("take_kv", n) for kind, n in projections if kind == "next_kv"]
        between = projections[:1] if i == 7 else []
        steps += between + [("turn_probs", (i, g)) for g in range(2, groups)]
        if not fox:
            steps += takes
        if i < 7:
            steps += [("exp", i + 1), ("rescale", i + 1)]
        if i == 0:
            steps += [("small_values", 0)]
        steps += projections[len(between):]
        if fox:
            steps += takes
        if i % 2:
            steps += [("values", i // 2)]
    return steps + filled("after") + [("gated", 4)]


class Turns:

    def __init__(self, fox):
        self.tables = {}
        for last in (False, True):
            banks, seen = {}, [0, 0]
            for n, s in enumerate(s for s in head_steps(fox, last) if s[0] in ("gate", "next_kv", "next_q")):
                banks[s] = (n % 2, seen[n % 2])
                seen[n % 2] += 1
            self.tables[last] = banks
            if not last:
                self.proj_per_head = seen

    def proj(self, step, h):
        b, nth = self.tables[isinstance(h, int) and h == HEADS - 1][step]
        return b, self.proj_per_head[b] * h + nth

    def after_next_kv(self, h):
        return [(b, 1 + max(nth for s, (bank, nth) in self.tables[False].items() if s[0] == "next_kv" and bank == b)
                 + self.proj_per_head[b] * h) for b in range(2)]

    @staticmethod
    def turn(use, h):
        n = TURNS.index(use)
        return n % 2, TURNS_PER_BANK[n % 2] * h + n // 2

    @staticmethod
    def split(use, h):
        return len(SPLIT_TURNS) * h + SPLIT_TURNS.index(use)


def three_pass(pe, out, terms, start=True, stop=True):
    n = len(terms)
    for k, (lh, ll, rh, rl) in enumerate(terms):
        pe.matmul(out, lh, rh, start=start and k == 0, stop=False)
        pe.matmul(out, lh, rl, start=False, stop=False)
        last = pe.matmul(out, ll, rh, start=False, stop=stop and k == n - 1)
    return last


def wait_apart(eng, sem, value, waited):
    eng.wait_ge(sem, value)
    eng.sem_inc(waited, 1)


class Memory:

    def __init__(self, nc):
        self.nc = nc
        self.prefix = ""

    def sbuf(self, stack, name, shape, dtype=F32, side=None):
        return stack.enter_context(self.nc.sbuf_tensor(self.prefix + name, shape, dtype, side=side))


def attention(nc, m, fox, dram):
    pre = "fox_" if fox else "mla_"
    turns = Turns(fox)
    NKV = NT if fox else NT + NC
    bank = m.bank
    S, PT, O, PJ = bank[0:3], bank[3:5], bank[5], bank[6:8]
    ident = m.ident

    with ExitStack() as st:
        sems = []
        st.callback(nc.all_engine_barrier)
        st.callback(nc.clear_and_free_semaphores, sems)

        def sb(name, shape, dtype=F32):
            return st.enter_context(nc.sbuf_tensor(pre + name, shape, dtype))

        def sem(name):
            sems.append(nc.alloc_semaphore(pre + name))
            return sems[-1]

        key_hi, key_lo = sb("key_hi", [P, T], F32R), sb("key_lo", [P, T], F32R)
        key_32 = sb("key_32", [P, P])
        query_hi, query_lo = sb("query_hi", [P, T], F32R), sb("query_lo", [P, T], F32R)
        value_hi, value_lo = sb("value_hi", [P, NT, DH], F32R), sb("value_lo", [P, NT, DH], F32R)
        gate = sb("gate", [P, T])
        gate_tanh = sb("gate_tanh", [P, CHUNK_W])
        probs = sb("probs", [P, T])
        probs_s = sb("probs_s", [SMALL, PAST + SMALL])
        pT_hi, pT_lo = sb("pT_hi", [P, NT, 2 * P], F32R), sb("pT_lo", [P, NT, 2 * P], F32R)
        pT_s = sb("pT_s", [P, NC + 1, P])
        out_buf = sb("out_buf", [P, 2, 2 * P])
        cache_keyT = out_buf[:, :, :].rearrange("p a b -> p (a b)")
        neg_max, row_sum, row_inv = sb("neg_max", [P, NT]), sb("row_sum", [P, NT]), sb("row_inv", [P, NT])
        kv_nat, query_32 = m.kv_nat, m.query_32
        if fox:
            cache_k, cache_v = sb("cache_k", [P, NC, DH]), sb("cache_v", [P, NC, DH])
            f_keys = sb("f_keys", [P, T + PAST])
            f_query = sb("f_query", [P, NT])
            decay = [sb("decay0", [P, T]), sb("decay1", [P, T])]
            decay_s = probs_s
            value_small = sb("value_small", [P, DH])
        else:
            rope_q = sb("rope_q", [P, T], F32R)
            rope_qs = sb("rope_qs", [ROPE, SMALL])
            value_small = m.kv_nat[:, 0, DH:2 * DH]

        proj_full, proj_free = [sem("proj_full0"), sem("proj_full1")], [sem("proj_free0"), sem("proj_free1")]
        turn_full, turn_free = [sem("turn_full0"), sem("turn_full1")], [sem("turn_free0"), sem("turn_free1")]
        turn_rounded = sem("turn_rounded")
        scores_full, max_done, exp_done, probs_ready = sem("scores_full"), sem("max_done"), sem("exp_done"), sem("probs_ready")
        out_full, out_ready, out_stored = sem("out_full"), sem("out_ready"), [sem("out_stored0"), sem("out_stored1")]
        gate_tanhed, gate_ready = sem("gate_tanhed"), sem("gate_ready")
        query_rounded, value_rounded = sem("query_rounded"), sem("value_rounded")
        query_split, value_split = sem("query_split"), sem("value_split")
        kv_stored = sem("kv_stored")
        zeroed, vec_step, pool_step = sem("zeroed"), sem("vec_step"), sem("pool_step")
        kv_w_loaded, kv_w_split, qg_w_loaded, qg_w_split = sem("kv_w_loaded"), sem("kv_w_split"), sem("qg_w_loaded"), sem("qg_w_split")
        cache_loaded, f_loaded, f_query_ready = sem("cache_loaded"), sem("f_loaded"), sem("f_query_ready")
        decay_ready = sem("decay_ready")
        pe_waited, dve_waited, pool_waited = sem("pe_waited"), sem("dve_waited"), sem("pool_waited")
        q_loaded, rope_loaded, rope_split_loaded = sem("q_loaded"), sem("rope_loaded"), sem("rope_split_loaded")

        block = st.enter_context(nc.Block())
        KC = KT if fox else KV_LORA // P
        kv_w_hi, kv_w_lo = m.kv_w_hi, m.kv_w_lo
        g_w_hi, g_w_lo = m.g_w_hi, m.g_w_lo
        GCOL = DH if fox else 0

        def heads(eng, body):
            with eng.Fori(0, HEADS - 1) as h:
                body(h, False)
            body(HEADS - 1, True)

        FIRST = 1
        started = turn_free + proj_free + out_stored + [exp_done, max_done, out_ready, gate_ready, qg_w_split, out_full]

        @block.tensor
        def _(pe):
            for first in started:
                pe.sem_inc(first, FIRST)

            def turn_keys(h, g):
                tiles, col, width = GROUPS[g]
                b, nth = turns.turn(("K", g), h)
                wait_apart(pe, turn_free[b], FIRST + nth, pe_waited)
                for t in tiles:
                    c, n = tile_cols(t)
                    last = pe.transpose(PT[b][:, c - col:c - col + n], kv_nat[0:n, t, 0:DH], ident[0:n, 0:n])
                last.then_inc(turn_full[b], 1)

            def turn_cache(h):
                b, nth = turns.turn(("C", 0), h)
                if fox:
                    pe.wait_ge(cache_loaded, 32 * h + 32)
                pe.wait_ge(turn_free[b], FIRST + nth)
                for t in range(NC):
                    src = cache_k[:, t, :] if fox else kv_nat[:, NT + t, 0:DH]
                    last = pe.transpose(PT[b][:, P * t:P * t + P], src, ident[:, :])
                last.then_inc(turn_full[b], 1)

            def gate_chunk(h, c):
                b, nth = turns.proj(("gate", c), h)
                col, w = CHUNKS[c]
                if c == 0:
                    pe.wait_ge(qg_w_split, FIRST + h)
                pe.wait_ge(proj_free[b], FIRST + nth)
                three_pass(pe, PJ[b][:, 0:w],
                           [(g_w_hi[:, k, GCOL:GCOL + DH], g_w_lo[:, k, GCOL:GCOL + DH],
                             m.act_hi[:, k, col:col + w], m.act_lo[:, k, col:col + w]) for k in range(KT)]
                           ).then_inc(proj_full[b], 1)

            def small_scores(h):
                pe.wait_ge(exp_done if not fox else max_done, FIRST + NT * h)
                b, nth = turns.turn(("C", 0), h)
                pe.wait_ge(turn_free[b], FIRST + nth + 1)
                b, nth = turns.turn(("K", 0), h)
                pe.wait_ge(turn_free[b], FIRST + nth + 1)
                if fox:
                    for b in range(2):
                        pe.wait_ge(proj_free[b], FIRST + turns.proj_per_head[b] * h)
                else:
                    pe.wait_ge(q_loaded, 16 * h + 16)
                if not fox:
                    pe.wait_ge(rope_loaded, 16 * h + 16)
                q = query_32[:, 0:SMALL]
                pieces = [(0, 0, S9W, cache_keyT, 0), (1, 0, PAST - S9W, cache_keyT, S9W), (1, PAST - S9W, P, key_32, 0)]
                for b, c, n, keys, kc in pieces:
                    last = pe.matmul(S[b][0:SMALL, c:c + n], q, keys[:, kc:kc + n], start=True, stop=fox)
                    if not fox:
                        hidden = N_SAMPLE if keys is key_32 else n
                        half = hidden // 2
                        for e in (c, c + half):
                            pe.matmul(S[b][0:SMALL, e:e + half], m.mask_meta[0:1, :], m.mask_big[0:1, 0:half], start=False, stop=False)
                        if keys is key_32:
                            pe.matmul(S[b][0:SMALL, c + N_SAMPLE:c + SMALL], m.mask_sample[0:1, :], m.mask_big[0:1, 0:N_META],
                                      start=False, stop=False)
                        rc = kc if keys is key_32 else P + kc
                        last = pe.matmul(S[b][0:SMALL, c:c + n], rope_qs[:, :],
                                         m.rope_k32[0:ROPE, rc:rc + n], start=False, stop=True)
                last.then_inc(scores_full, 1)

            def scores(h, i):
                first, pieces, w, used = score_pieces(i)
                if i == 0:
                    first_bank = 2
                    pe.wait_ge(query_split, h + 1)
                    for g in range(3):
                        b, nth = turns.turn(("K", g), h)
                        pe.wait_ge(turn_free[b], FIRST + nth + 1)
                    if not fox:
                        pe.wait_ge(rope_split_loaded, 32 * h + 32)
                else:
                    first_bank = 0
                    pe.wait_ge(exp_done if not fox else max_done, FIRST + NT * h + i + 1)
                qc, _ = tile_cols(i + 1)
                for p in range(pieces):
                    out = S[first_bank + p][:, 0:w]
                    k0 = first + p * w
                    last = three_pass(pe, out, [(query_hi[:, qc:qc + P], query_lo[:, qc:qc + P],
                                                 key_hi[:, k0:k0 + w], key_lo[:, k0:k0 + w])], stop=fox)
                    if fox:
                        continue
                    if i == 7 and p == 0:
                        pe.matmul(out[:, 0:4], m.mask_all[0:1, :], m.mask_big[0:1, 0:4], start=False, stop=False)
                    if p == pieces - 1:
                        e = first + used - k0 - 64
                        pe.matmul(out[:, e:e + 64], m.mask_first[0:1, :], m.mask_big[0:1, 0:64], start=False, stop=False)
                    pe.matmul(out, rope_q[:, qc:qc + P], m.rope_k_hi[:, k0:k0 + w], start=False, stop=False)
                    last = pe.matmul(out, rope_q[0:ROPE, qc:qc + P], m.rope_k_lo[0:ROPE, k0:k0 + w], start=False, stop=True)
                last.then_inc(scores_full, 1)

            def turn_small(h):
                b, nth = turns.turn(("S", 0), h)
                pe.wait_ge(probs_ready, prob_signals(8) * h + 1)
                wait_apart(pe, turn_free[b], FIRST + nth, pe_waited)
                for k in range(NC + 1):
                    n = P if k < NC else SMALL
                    last = pe.transpose(PT[b][0:n, SMALL * k:SMALL * k + SMALL], probs_s[:, P * k:P * k + n],
                                        ident[0:SMALL, 0:SMALL])
                last.then_inc(turn_full[b], 1)

            def turn_probs(h, i, g):
                b, nth = turns.turn((i, g), h)
                if g < 2:
                    pe.wait_ge(probs_ready, prob_signals(8) * h + prob_signals(i) + g + 1)
                if g == 0:
                    wait_apart(pe, turn_free[b], FIRST + nth, pe_waited)
                else:
                    pe.wait_ge(turn_free[b], FIRST + nth)
                for s, k in enumerate(prob_groups(i)[g]):
                    c, n = tile_cols(k)
                    last = pe.transpose(PT[b][0:n, P * s:P * s + P], probs[:, c:c + n], ident[:, :])
                last.then_inc(turn_full[b], 1)

            def small_values(h):
                b, nth = turns.turn(("S", 0), h)
                pe.wait_ge(turn_free[b], FIRST + nth + 1)
                pe.wait_ge(value_split, h + 1)
                pe.wait_ge(out_ready, FIRST + 5 * h)
                for k in range(NC):
                    v = cache_v[:, k, :] if fox else kv_nat[:, NT + k, DH:2 * DH]
                    pe.matmul(O[:, 0:P], v, pT_s[:, k, :], start=k == 0, stop=False)
                pe.matmul(O[:, 0:P], value_small[0:SMALL, :], pT_s[0:SMALL, NC, :], start=False, stop=True).then_inc(out_full, 1)

            def values(h, j):
                for g in range(len(prob_groups(2 * j + 1))):
                    b, nth = turns.turn((2 * j + 1, g), h)
                    pe.wait_ge(turn_free[b], FIRST + nth + 1)
                pe.wait_ge(zeroed, h + 1)
                pe.wait_ge(out_ready, FIRST + 5 * h + 1 + j)
                terms = []
                for k in range(2 * j + 3):
                    n = tile_cols(k)[1]
                    terms.append((value_hi[0:n, k, :], value_lo[0:n, k, :], pT_hi[0:n, k, :], pT_lo[0:n, k, :]))
                three_pass(pe, O[:, 0:2 * P], terms).then_inc(out_full, 1)

            def next_kv(h, t):
                b, nth = turns.proj(("next_kv", t), h)
                if t == 0:
                    pe.wait_ge(kv_w_split, h + 1)
                pe.wait_ge(proj_free[b], FIRST + nth)
                if t < NT:
                    c, n = tile_cols(t)
                else:
                    c, n = T + P * (t - NT), P
                last = three_pass(pe, PJ[b][0:n, 0:2 * DH],
                                  [(m.kv_act_hi[:, k, c:c + n], m.kv_act_lo[:, k, c:c + n], kv_w_hi[:, k, :], kv_w_lo[:, k, :])
                                   for k in range(KC)])
                last.then_inc(proj_full[b], 1)

            def next_q(h, c):
                b, nth = turns.proj(("next_q", c), h)
                col, w = CHUNKS[c]
                if c == 0:
                    pe.wait_ge(qg_w_split, FIRST + h + 1)
                pe.wait_ge(proj_free[b], FIRST + nth)
                three_pass(pe, PJ[b][:, 0:w],
                           [(g_w_hi[:, k, 0:DH], g_w_lo[:, k, 0:DH], m.act_hi[:, k, col:col + w], m.act_lo[:, k, col:col + w])
                            for k in range(KT)]).then_inc(proj_full[b], 1)

            def head(h, last):
                for step, n in head_steps(fox, last):
                    if step == "turn_keys":
                        turn_keys(h, n)
                    elif step == "turn_cache":
                        turn_cache(h)
                    elif step == "gate":
                        gate_chunk(h, n)
                    elif step == "small_scores":
                        small_scores(h)
                    elif step == "scores":
                        scores(h, n)
                    elif step == "turn_small":
                        turn_small(h)
                    elif step == "turn_probs":
                        turn_probs(h, *n)
                    elif step == "small_values":
                        small_values(h)
                    elif step == "values":
                        values(h, n)
                    elif step == "next_kv":
                        next_kv(h, n)
                    elif step == "next_q":
                        next_q(h, n)
                if not last:
                    for b, count in turns.after_next_kv(h):
                        pe.wait_ge(proj_free[b], FIRST + count)

            heads(pe, head)

        @block.scalar
        def _(act):
            def turn_keys(h, g):
                if g == 0:
                    for b in range(2):
                        act.wait_ge(proj_free[b], FIRST + turns.proj_per_head[b] * h)
                tiles, col, width = GROUPS[g]
                b, nth = turns.turn(("K", g), h)
                act.wait_ge(turn_full[b], nth + 1)
                act.activation(key_hi[:, col:col + width], PT[b][:, 0:width], ACT.Copy).then_inc(turn_rounded, 1)

            def split_query(h):
                if not fox:
                    act.wait_ge(q_loaded, 16 * h + 16)
                act.activation(query_hi[:, :], query_32[:, :], ACT.Copy).then_inc(query_rounded, 1)

            def split_values(h):
                act.activation(value_hi[:, :, :], kv_nat[:, 0:NT, DH:2 * DH], ACT.Copy).then_inc(value_rounded, 1)

            def turn_cache(h):
                b, nth = turns.turn(("C", 0), h)
                act.wait_ge(turn_full[b], nth + 1)
                act.wait_ge(out_stored[0], FIRST + 16 * 3 * h)
                act.wait_ge(out_stored[1], FIRST + 16 * 2 * h)
                act.activation(cache_keyT[:, :], PT[b][:, :], ACT.Copy).then_inc(turn_free[b], 1)

            def gate_tanh_chunk(h, c):
                col, w = CHUNKS[c]
                b, nth = turns.proj(("gate", c), h)
                act.wait_ge(proj_free[b], FIRST + nth + 1)
                act.wait_ge(gate_ready, FIRST + 3 * h + c)
                act.activation(gate_tanh[:, 0:w], gate[:, col:col + w], ACT.Tanh, scale=0.5).then_inc(gate_tanhed, 1)

            def small_exp(h):
                act.wait_ge(max_done, FIRST + NT * h + 1)
                if fox:
                    act.activation(probs_s[:, :], decay_s[:, :], ACT.Exp, scale=-1.0,
                                   bias=neg_max[0:SMALL, 0:1], accum_out=row_sum[0:SMALL, 0:1]).then_inc(exp_done, 1)
                else:
                    src = m.score_banks(0, 2)[0:SMALL, :, 0:S9W]
                    act.activation(probs_s[:, :].rearrange("p (a b) -> p a b", a=2), src, ACT.Exp,
                                   bias=neg_max[0:SMALL, 0:1], accum_out=row_sum[0:SMALL, 0:1]).then_inc(exp_done, 1)

            def exp(h, i):
                first, pieces, w, used = score_pieces(i)
                act.wait_ge(max_done, FIRST + NT * h + i + 2)
                bias, total = neg_max[:, i + 1:i + 2], row_sum[:, i + 1:i + 2]
                if fox:
                    act.activation(probs[:, first:first + used], decay[i % 2][:, first:first + used], ACT.Exp, scale=-1.0,
                                   bias=bias, accum_out=total).then_inc(exp_done, 1)
                else:
                    w = min(w, used)
                    act.activation(probs[:, first:first + used].rearrange("p (a b) -> p a b", a=pieces),
                                   m.score_banks(2 if i == 0 else 0, pieces)[:, :, 0:w], ACT.Exp,
                                   bias=bias, accum_out=total).then_inc(exp_done, 1)

            def turn_small(h):
                b, nth = turns.turn(("S", 0), h)
                act.wait_ge(turn_full[b], nth + 1)
                act.activation(pT_s[:, :, 0:SMALL], PT[b][:, 0:SMALL * (NC + 1)].rearrange("p (a b) -> p a b", b=SMALL),
                               ACT.Copy).then_inc(turn_free[b], 1)

            def turn_probs(h, i, g):
                q, blocks = P * (i % 2), prob_groups(i)[g]
                b, nth = turns.turn((i, g), h)
                n = len(blocks)
                act.wait_ge(turn_full[b], nth + 1)
                act.activation(pT_hi[:, blocks[0]:blocks[0] + n, q:q + P],
                               PT[b][:, 0:P * n].rearrange("p (a b) -> p a b", b=P), ACT.Copy).then_inc(turn_rounded, 1)

            def take_kv(h, t):
                b, nth = turns.proj(("next_kv", t), h)
                if t == 0:
                    act.wait_ge(value_split, h + 1)
                    act.wait_ge(kv_stored, 96 * h + 96)
                act.wait_ge(proj_full[b], nth + 1)
                n = tile_cols(t)[1]
                act.activation(kv_nat[0:n, t, :], PJ[b][0:n, 0:2 * DH], ACT.Copy, scale=m.rms_rows[0:n, t:t + 1]).then_inc(proj_free[b], 1)

            def head(h, last):
                for step, n in head_steps(fox, last):
                    if step == "turn_keys":
                        turn_keys(h, n)
                    elif step == "split_query":
                        split_query(h)
                    elif step == "split_values":
                        split_values(h)
                    elif step == "turn_cache":
                        turn_cache(h)
                    elif step == "gate_tanh":
                        gate_tanh_chunk(h, n)
                    elif step == "small_exp":
                        small_exp(h)
                    elif step == "exp":
                        exp(h, n)
                    elif step == "turn_small":
                        turn_small(h)
                    elif step == "turn_probs":
                        turn_probs(h, *n)
                    elif step == "take_kv" and fox:
                        take_kv(h, n)

            heads(act, head)

        @block.vector
        def _(dve):
            steps_done = [0]

            def chain(ins, h):
                ins.then_inc(vec_step, 1)
                steps_done[0] += 1
                dve.wait_ge(vec_step, STEPS * h + steps_done[0])

            def turn_keys(h, g):
                tiles, col, width = GROUPS[g]
                b, nth = turns.turn(("K", g), h)
                dve.wait_ge(turn_rounded, turns.split(("K", g), h) + 1)
                if g == 0:
                    dve.tensor_copy(key_32[:, :], PT[b][:, 0:P])
                dve.tensor_tensor(key_lo[:, col:col + width], PT[b][:, 0:width],
                                  key_hi[:, col:col + width].bitcast(F32), ALU.subtract).then_inc(turn_free[b], 1)

            def split_query(h):
                dve.wait_ge(query_rounded, h + 1)
                dve.tensor_tensor(query_lo[:, :], query_32[:, :], query_hi[:, :].bitcast(F32), ALU.subtract).then_inc(query_split, 1)

            def split_values(h):
                dve.wait_ge(value_rounded, h + 1)
                if fox:
                    dve.tensor_copy(value_small[0:SMALL, :], kv_nat[0:SMALL, 0, DH:2 * DH])
                dve.tensor_tensor(value_lo[:, :, :], kv_nat[:, 0:NT, DH:2 * DH], value_hi[:, :, :].bitcast(F32),
                                  ALU.subtract).then_inc(value_split, 1)

            def gate_chunk(h, c):
                b, nth = turns.proj(("gate", c), h)
                col, w = CHUNKS[c]
                dve.wait_ge(proj_full[b], nth + 1)
                dve.tensor_tensor(gate[:, col:col + w], PJ[b][:, 0:w], m.rms_cols[:, col:col + w], ALU.mult).then_inc(proj_free[b], 1)

            def gate_mul(h, c):
                col, w = CHUNKS[c]
                dve.wait_ge(gate_tanhed, 3 * h + c + 1)
                dve.scalar_tensor_tensor(out=gate[:, col:col + w], in0=gate_tanh[:, 0:w], scalar=1.0, in1=gate[:, col:col + w],
                                         op0=ALU.add, op1=ALU.mult).then_inc(gate_ready, 1)

            def rescale(h, n):
                rows, prob = SMALL, probs_s[:, :]
                if n:
                    first, _, _, used = score_pieces(n - 1)
                    rows, prob = P, probs[:, first:first + used]
                dve.wait_ge(exp_done, FIRST + NT * h + n + 1)
                chain(dve.reciprocal(row_inv[0:rows, n:n + 1], row_sum[0:rows, n:n + 1]), h)
                pieces = [prob]
                if n and len(prob_groups(n - 1)) > 1:
                    border = SMALL + 3 * P - first
                    pieces = [prob[:, 0:border], prob[:, border:used]]
                for piece in pieces:
                    dve.tensor_scalar(piece, piece, row_inv[0:rows, n:n + 1], None, ALU.mult).then_inc(probs_ready, 1)

            def small_max(h):
                dve.wait_ge(scores_full, NT * h + 1)
                src = m.score_banks(0, 2)[0:SMALL, :, 0:S9W]
                if fox:
                    wait_apart(dve, decay_ready, NT * h + 1, dve_waited)
                    halves = lambda x: x.rearrange("p (a b) -> p a b", a=2)
                    dve.tensor_tensor_reduce(halves(decay_s[:, :]), src, halves(decay_s[:, :]), 1.0, FMAX,
                                             ALU.add, ALU.min, neg_max[0:SMALL, 0:1]).then_inc(max_done, 1)
                else:
                    dve.tensor_reduce(neg_max[0:SMALL, 0:1], src, mybir.AxisListType.XY, ALU.max, negate=True).then_inc(max_done, 1)

            def row_max(h, i):
                first, pieces, w, used = score_pieces(i)
                w = min(w, used)
                dve.wait_ge(scores_full, NT * h + i + 2)
                src = m.score_banks(2 if i == 0 else 0, pieces)[:, :, 0:w]
                if fox:
                    wait_apart(dve, decay_ready, NT * h + i + 2, dve_waited)
                    cut = lambda x: x[:, first:first + used].rearrange("p (a b) -> p a b", a=pieces)
                    dve.tensor_tensor_reduce(cut(decay[i % 2]), src, cut(decay[i % 2]), 1.0, FMAX,
                                             ALU.add, ALU.min, neg_max[:, i + 1:i + 2]).then_inc(max_done, 1)
                else:
                    dve.tensor_reduce(neg_max[:, i + 1:i + 2], src, mybir.AxisListType.XY, ALU.max, negate=True).then_inc(max_done, 1)

            def turn_probs(h, i, g):
                q, blocks = P * (i % 2), prob_groups(i)[g]
                b, nth = turns.turn((i, g), h)
                k, n = blocks[0], len(blocks)
                dve.wait_ge(turn_rounded, turns.split((i, g), h) + 1)
                dve.tensor_tensor(pT_lo[:, k:k + n, q:q + P], PT[b][:, 0:P * n].rearrange("p (a b) -> p a b", b=P),
                                  pT_hi[:, k:k + n, q:q + P].bitcast(F32), ALU.subtract).then_inc(turn_free[b], 1)

            def gated(h, n):
                col, w = (0, SMALL) if n == 0 else (SMALL + 2 * P * (n - 1), 2 * P)
                dve.wait_ge(out_full, FIRST + 5 * h + n + 1)
                dve.wait_ge(gate_ready, FIRST + 3 * h + (1, 1, 2, 3, 3)[n])
                dve.wait_ge(out_stored[n % 2], FIRST + 16 * ((3, 2)[n % 2] * h + n // 2))
                dve.scalar_tensor_tensor(out=out_buf[:, n % 2, 0:w], in0=O[:, 0:w], scalar=0.5, in1=gate[:, col:col + w],
                                         op0=ALU.mult, op1=ALU.mult).then_inc(out_ready, 1)

            def take_kv(h, t):
                b, nth = turns.proj(("next_kv", t), h)
                if t == 0:
                    dve.wait_ge(out_full, FIRST + 5 * h + 1)
                dve.wait_ge(proj_full[b], nth + 1)
                n = P if t >= NT else tile_cols(t)[1]
                dve.tensor_copy(kv_nat[0:n, t, :], PJ[b][0:n, 0:2 * DH]).then_inc(proj_free[b], 1)

            def next_q(h, c):
                b, nth = turns.proj(("next_q", c), h)
                col, w = CHUNKS[c]
                dve.wait_ge(proj_full[b], nth + 1)
                dve.scalar_tensor_tensor(out=query_32[:, col:col + w], in0=PJ[b][:, 0:w], scalar=-FOX_SCALE,
                                         in1=m.rms_cols[:, col:col + w], op0=ALU.mult, op1=ALU.mult).then_inc(proj_free[b], 1)

            def head(h, last):
                steps_done[0] = 0
                for step, n in head_steps(fox, last):
                    if step == "turn_keys":
                        turn_keys(h, n)
                    elif step == "split_query":
                        split_query(h)
                    elif step == "split_values":
                        split_values(h)
                    elif step == "gate":
                        gate_chunk(h, n)
                    elif step == "gate_mul":
                        gate_mul(h, n)
                    elif step == "small_max":
                        small_max(h)
                    elif step == "max":
                        row_max(h, n)
                    elif step == "small_rescale":
                        rescale(h, 0)
                    elif step == "rescale":
                        rescale(h, n + 1)
                    elif step == "turn_probs":
                        turn_probs(h, *n)
                    elif step == "gated":
                        gated(h, n)
                    elif step == "take_kv" and not fox:
                        take_kv(h, n)
                    elif step == "next_q":
                        next_q(h, n)
                assert steps_done[0] == STEPS

            STEPS = NT
            heads(dve, head)

        @block.gpsimd
        def _(pool):
            pool.memset(pT_hi[:, :, :].bitcast(F32), 0.0)
            pool.memset(pT_lo[:, :, :].bitcast(F32), 0.0)
            pool.memset(pT_s[:, :, :], 0.0)
            if fox:
                pool.memset(decay[0][:, 0:N_SAMPLE], BIG)
                pool.memset(decay[1][:, 0:N_SAMPLE], BIG)
            pool.memset(probs[:, 0:N_SAMPLE], 0.0).then_inc(pool_step, 1)
            pool.wait_ge(pool_step, 1)
            DECAYS_AFTER = [[2], [], [], [3, 4], [5], [6], [7], []]
            PSTEPS = 20 if fox else 3
            kv_stage = None if fox else m.stage[:, 0:4, :].rearrange("p (k a) n -> p k (a n)", a=2)
            taken = [0]

            def chain(ins, h):
                ins.then_inc(pool_step, 1)
                taken[0] += 1
                wait_apart(pool, pool_step, 1 + PSTEPS * h + taken[0], pool_waited)

            def zero_upper(h):
                wait_apart(pool, out_full, FIRST + 5 * h, pool_waited)
                pool.memset(pT_hi[:, 2:7:2, 0:P].bitcast(F32), 0.0)
                pool.memset(pT_lo[:, 2:7:2, 0:P].bitcast(F32), 0.0).then_inc(zeroed, 1)

            def split_piece(h, stage, hi, lo):
                chain(pool.tensor_scalar(hi, stage, 1.0, 0.0, ALU.mult, ALU.add), h)
                return pool.tensor_tensor(lo, stage, hi.bitcast(F32), ALU.subtract)

            def split_weights(h, stage, hi, lo, done):
                split_piece(h, stage, hi, lo).then_inc(done, 1)

            def decay_tile(h, i):
                n = SMALL + P * (i + 1) - N_SAMPLE
                d = decay[i % 2]
                wait_apart(pool, exp_done, FIRST + NT * h + (i if i >= 2 else 0), pool_waited)
                chain(pool.tensor_scalar(d[:, N_SAMPLE:N_SAMPLE + n], f_keys[:, N_SAMPLE:N_SAMPLE + n], 1.0,
                                         f_query[:, i + 1:i + 2], ALU.mult, ALU.add), h)
                e = N_SAMPLE + n - P
                pool.affine_select(out=d[:, e:e + P], in_=d[:, e:e + P], compare_op=ALU.is_ge, fill=BIG, base=0,
                                   pattern=[[-1, P]], channel_multiplier=1).then_inc(decay_ready, 1)

            def decay_small(h):
                own = decay_s[:, PAST:PAST + SMALL]
                chain(pool.tensor_scalar(decay_s[:, 0:PAST], f_keys[0:SMALL, T:T + PAST], 1.0, f_query[0:SMALL, 0:1],
                                         ALU.mult, ALU.add), h)
                chain(pool.tensor_scalar(own, f_keys[0:SMALL, 0:SMALL], 1.0, f_query[0:SMALL, 0:1], ALU.mult, ALU.add), h)
                chain(pool.affine_select(out=own, in_=own, compare_op=ALU.is_ge, fill=BIG, base=0,
                                         pattern=[[-1, SMALL]], channel_multiplier=1), h)
                pool.memset(decay_s[N_SAMPLE:SMALL, 0:PAST + N_SAMPLE], BIG).then_inc(decay_ready, 1)
                wait_apart(pool, decay_ready, NT * h + 1, pool_waited)

            def load_rope(h):
                for n, part in enumerate((dram.q_rope_hi, dram.q_rope_lo)):
                    pool.dma_start(rope_q[ROPE * n:ROPE * n + ROPE, :], part[bass.ds(h * ROPE, ROPE), :]).then_inc(rope_split_loaded, 16)

            def head(h, last):
                taken[0] = 0
                zero_upper(h)
                if fox:
                    wait_apart(pool, f_loaded, 16 * h + 16, pool_waited)
                    wait_apart(pool, exp_done, FIRST + NT * h, pool_waited)
                    chain(pool.tensor_copy(f_query[:, :], m.f_query_all[:, h, :] if isinstance(h, int) else
                                           m.f_query_all[:, bass.ds(h, 1), :].rearrange("p a t -> p (a t)")), h)
                    decay_small(h)
                    decay_tile(h, 0)
                    decay_tile(h, 1)
                    for i in range(8):
                        if not last:
                            if i == 0:
                                wait_apart(pool, kv_w_loaded, 32 * h + 32, pool_waited)
                            if i == 4:
                                b, nth = turns.proj(("gate", 2), h)
                                wait_apart(pool, proj_full[b], nth + 1, pool_waited)
                                wait_apart(pool, qg_w_loaded, 32 * h + 32, pool_waited)
                            k = slice(2 * (i % 4), 2 * (i % 4) + 2)
                            hi, lo = (kv_w_hi, kv_w_lo) if i < 4 else (g_w_hi, g_w_lo)
                            last_split = split_piece(h, m.stage[:, k, :], hi[:, k, :], lo[:, k, :])
                            if i % 4 == 3:
                                last_split.then_inc(kv_w_split if i < 4 else qg_w_split, 1)
                        for tile in DECAYS_AFTER[i]:
                            decay_tile(h, tile)
                else:
                    if not last:
                        wait_apart(pool, kv_w_loaded, 16 * h + 16, pool_waited)
                        split_weights(h, kv_stage, kv_w_hi[:, :, :], kv_w_lo[:, :, :], kv_w_split)
                        b, nth = turns.proj(("gate", 2), h)
                        wait_apart(pool, proj_full[b], nth + 1, pool_waited)
                        wait_apart(pool, qg_w_loaded, 16 * h + 16, pool_waited)
                        for k in range(KT):
                            last_scaled = pool.tensor_scalar(m.stage[:, k, :], m.stage[:, k, :], m.b_gain[:, k:k + 1], 1.0,
                                                             ALU.mult, ALU.mult)
                        chain(last_scaled, h)
                        split_weights(h, m.stage[:, :, :], g_w_hi[:, :, :], g_w_lo[:, :, :], qg_w_split)
                        wait_apart(pool, scores_full, NT * h + NT, pool_waited)
                        load_rope(h + 1)

            if not fox:
                load_rope(0)
            heads(pool, head)

        @block.sync
        def _(sp):
            def store_out(h, n, col, w):
                sp.wait_ge(out_ready, FIRST + 5 * h + n + 1)
                sp.dma_start((dram.gated if fox else dram.gated_b)[bass.ds(h * DH, DH), col:col + w], out_buf[:, n % 2, 0:w]).then_inc(out_stored[n % 2], 16)

            def load_cache(h):
                sp.dma_start(cache_k[:, :, :], dram.cache_k[:, bass.ds(h * DH, DH)].rearrange("(t p) d -> p t d", p=P)).then_inc(cache_loaded, 16)
                sp.dma_start(cache_v[:, :, :], dram.cache_v[:, bass.ds(h * DH, DH)].rearrange("(t p) d -> p t d", p=P)).then_inc(cache_loaded, 16)

            def load_f_keys(h):
                sp.dma_start(f_keys[:, :], dram.f_cum[bass.ds(h, 1), :].to_broadcast([P, T + PAST])).then_inc(f_loaded, 16)

            def load_queries(h):
                sp.dma_start(query_32[:, :], dram.q_nope[bass.ds(h * DH, DH), :]).then_inc(q_loaded, 16)

            def load_rope(h):
                sp.dma_start(rope_qs[:, :], dram.q_rope_small[bass.ds(h * ROPE, ROPE), :]).then_inc(rope_loaded, 16)

            kv_stage = None if fox else m.stage[:, 0:4, :].rearrange("p (k a) n -> p k (a n)", a=2)
            if fox:
                load_cache(0)
                load_f_keys(0)
            else:
                load_queries(0)
                load_rope(0)

            def head(h, last):
                if fox and not last:
                    sp.wait_ge(qg_w_split, FIRST + h)
                    for n, sec in enumerate((1, 2)):
                        sp.dma_start(m.stage[:, :, DH * n:DH * n + DH], dram.fox_w(sec, h + 1)).then_inc(kv_w_loaded, 16)
                if fox:
                    for b in range(2):
                        sp.wait_ge(proj_free[b], FIRST + turns.proj_per_head[b] * h)
                    for dst_p, dst_s, col in ((dram.new_k_prompt, dram.new_k_sample, 0), (dram.new_v_prompt, dram.new_v_sample, DH)):
                        sp.dma_start(dst_s[:, bass.ds(h * DH, DH)], kv_nat[0:N_SAMPLE, 0, col:col + DH]).then_inc(kv_stored, 16)
                        sp.dma_start(dst_p[0:N_META, bass.ds(h * DH, DH)], kv_nat[N_SAMPLE:SMALL, 0, col:col + DH]).then_inc(kv_stored, 16)
                        sp.dma_start(dst_p[N_META:L, bass.ds(h * DH, DH)].rearrange("(t p) d -> p t d", p=P),
                                     kv_nat[:, 1:NT, col:col + DH]).then_inc(kv_stored, 16)
                if not fox and not last:
                    sp.wait_ge(qg_w_split, FIRST + h)
                    sp.dma_start(kv_stage, dram.w_ukv(h + 1)).then_inc(kv_w_loaded, 16)
                store_out(h, 0, 0, SMALL)
                if not last:
                    if fox:
                        load_cache(h + 1)
                    else:
                        sp.wait_ge(value_split, h + 1)
                        sp.wait_ge(scores_full, NT * h + 1)
                        load_queries(h + 1)
                        load_rope(h + 1)
                store_out(h, 1, SMALL, 2 * P)
                if not fox and not last:
                    sp.wait_ge(kv_w_split, h + 1)
                    sp.dma_start(m.stage[:, :, :], dram.w_gate(h + 1)).then_inc(qg_w_loaded, 16)
                if fox and not last:
                    sp.wait_ge(kv_w_split, h + 1)
                    for n, sec in enumerate((0, 3)):
                        sp.dma_start(m.stage[:, :, DH * n:DH * n + DH], dram.fox_w(sec, h + 1)).then_inc(qg_w_loaded, 16)
                store_out(h, 2, SMALL + 2 * P, 2 * P)
                store_out(h, 3, SMALL + 4 * P, 2 * P)
                if fox and not last:
                    sp.wait_ge(decay_ready, NT * h + NT)
                    load_f_keys(h + 1)
                store_out(h, 4, SMALL + 6 * P, 2 * P)

            heads(sp, head)
            sp.wait_ge(out_stored[0], FIRST + 16 * 3 * HEADS)
            sp.wait_ge(out_stored[1], FIRST + 16 * 2 * HEADS)
            if fox:
                sp.wait_ge(kv_stored, 96 * HEADS)


def embed(nc, m, dram):
    bank = m.bank
    ident = m.ident
    with ExitStack() as st:
        sems = []
        st.callback(nc.all_engine_barrier)
        st.callback(nc.clear_and_free_semaphores, sems)

        def sb(name, shape, dtype=F32):
            return st.enter_context(nc.sbuf_tensor("embed_" + name, shape, dtype))

        def sem(name):
            sems.append(nc.alloc_semaphore("embed_" + name))
            return sems[-1]

        x_nat = sb("x_nat", [P, NT, D])
        square = sb("square", [P, D])
        XT = 6
        xt = sb("xt", [P, XT, 512])
        ones = sb("ones", [P, P])
        diag = sb("diag", [P, NT, P])
        a_gain = sb("a_gain", [P, KT])
        ssq, rms_ln, rms_t = sb("ssq", [P, NT]), sb("rms_ln", [P, NT]), sb("rms_t", [P, NT])
        wf, wf_hi, wf_lo = sb("wf", [P, KT, HEADS]), sb("wf_hi", [P, KT, HEADS], F32R), sb("wf_lo", [P, KT, HEADS], F32R)
        b_f = sb("b_f", [HEADS, 1])
        cache_f = sb("cache_f", [P, NC, HEADS])
        f, f_abs, f_exp = (x_nat[:, :, :].rearrange("p t d -> p (t d)")[0:HEADS, T * n:T * n + T] for n in range(3))
        log_f = sb("log_f", [HEADS, T + PAST])
        f_cum = sb("f_cum", [HEADS, T + PAST])
        row_ones = sb("row_ones", [HEADS, T])
        log_f_nat = sb("log_f_nat", [P, NT, HEADS])

        x_loaded = [sem(f"x_loaded{t}") for t in range(NT)]
        const_loaded, f_in_loaded, kv_w_loaded, q_w_loaded, w_split = sem("const_loaded"), sem("f_in_loaded"), sem("kv_w_loaded"), sem("q_w_loaded"), sem("w_split")
        part_full, part_rounded, part_free = sem("part_full"), sem("part_rounded"), sem("part_free")
        xt_ready, xt_stored = [sem("xt_ready0"), sem("xt_ready1")], [sem(f"xt_stored{n}") for n in range(XT)]
        squared, rms_step_v, rms_step_a = sem("squared"), sem("rms_step_v"), sem("rms_step_a")
        ones_ready, diag_ready = sem("ones_ready"), sem("diag_ready")
        rms_full, rms_ready = sem("rms_full"), sem("rms_ready")
        f_full, f_step, f_act = sem("f_full"), sem("f_step"), sem("f_act")
        f_cache_full, f_nat_full, f_stored = sem("f_cache_full"), sem("f_nat_full"), sem("f_stored")
        proj_full, proj_free = [sem("proj_full0"), sem("proj_full1")], [sem("proj_free0"), sem("proj_free1")]
        wf_split = sem("wf_split")
        block = st.enter_context(nc.Block())

        parts = [(g, k) for g in range(3) for k in range(KT)]

        @block.sync
        def _(sp):
            for t in range(NT):
                if t == 0:
                    sp.dma_start(x_nat[0:N_SAMPLE, 0, :], dram.x_sample).then_inc(x_loaded[0], 16)
                    sp.dma_start(x_nat[N_SAMPLE:SMALL, 0, :], dram.meta).then_inc(x_loaded[0], 16)
                    sp.dma_start(ident[:, :], dram.ident).then_inc(const_loaded, 16)
                    sp.dma_start(a_gain[:, :], dram.a_norm).then_inc(const_loaded, 16)
                else:
                    sp.dma_start(x_nat[:, t, :], dram.x_prompt[P * (t - 1):P * t, :]).then_inc(x_loaded[t], 16)
                if t == 3:
                    sp.dma_start(wf[:, :, :], dram.a_w_in[:, 3 * D:3 * D + HEADS].rearrange("(k p) n -> p k n", p=P)).then_inc(f_in_loaded, 16)
                    sp.dma_start(b_f[:, :], dram.a_b_forget).then_inc(f_in_loaded, 16)
                    sp.dma_start(cache_f[:, :, :], dram.cache_f.rearrange("(t p) h -> p t h", p=P)).then_inc(f_in_loaded, 16)
                    for n, sec in enumerate((1, 2)):
                        sp.dma_start(m.stage[:, :, DH * n:DH * n + DH], dram.fox_w(sec, 0)).then_inc(kv_w_loaded, 16)
            for n, (g, k) in enumerate(parts):
                sp.wait_ge(xt_ready[n % 2], n // 2 + 1)
                _, col, width = GROUPS[g]
                sp.dma_start(dram.resid[P * k:P * k + P, col:col + width], xt[:, n % XT, 0:width]).then_inc(xt_stored[n % XT], 16)
                if n == 4:
                    sp.wait_ge(w_split, 1)
                    for i, sec in enumerate((0, 3)):
                        sp.dma_start(m.stage[:, :, DH * i:DH * i + DH], dram.fox_w(sec, 0)).then_inc(q_w_loaded, 16)
            sp.wait_ge(f_step, 12)
            sp.dma_start(dram.f_cum, f_cum[:, :]).then_inc(f_stored, 16)
            sp.wait_ge(f_step, 13)
            sp.dma_start(dram.new_f_sample, log_f_nat[0:N_SAMPLE, 0, :]).then_inc(f_stored, 16)
            sp.dma_start(dram.new_f_prompt[0:N_META, :], log_f_nat[N_SAMPLE:SMALL, 0, :]).then_inc(f_stored, 16)
            sp.dma_start(dram.new_f_prompt[N_META:L, :].rearrange("(t p) h -> p t h", p=P), log_f_nat[:, 1:NT, :]).then_inc(f_stored, 16)
            sp.wait_ge(f_stored, 64)
            for n in range(XT):
                sp.wait_ge(xt_stored[n], 16 * (len(parts) // XT))

        @block.gpsimd
        def _(pool):
            pool.memset(ones[:, :], 1.0)
            pool.memset(row_ones[:, :], 1.0)
            pool.memset(m.kv_nat[:, 0, :], 0.0)
            pool.memset(m.f_query_all[:, :, :], 0.0)
            pool.memset(ssq[:, :], float(D)).then_inc(ones_ready, 1)
            pool.wait_ge(f_in_loaded, 48)
            pool.tensor_scalar(wf_hi[:, :, :], wf[:, :, :], 1.0, 0.0, ALU.mult, ALU.add).then_inc(wf_split, 1)
            pool.wait_ge(wf_split, 1)
            pool.tensor_tensor(wf_lo[:, :, :], wf[:, :, :], wf_hi[:, :, :].bitcast(F32), ALU.subtract).then_inc(wf_split, 1)
            for n, (loaded, hi, lo) in enumerate(((kv_w_loaded, m.kv_w_hi, m.kv_w_lo), (q_w_loaded, m.g_w_hi, m.g_w_lo))):
                pool.wait_ge(loaded, 32)
                pool.tensor_scalar(hi[:, :, :], m.stage[:, :, :], 1.0, 0.0, ALU.mult, ALU.add).then_inc(wf_split, 1)
                pool.wait_ge(wf_split, n + 3)
                pool.tensor_tensor(lo[:, :, :], m.stage[:, :, :], hi[:, :, :].bitcast(F32), ALU.subtract).then_inc(w_split, 1)

        @block.tensor
        def _(pe):
            pe.wait_ge(const_loaded, 32)
            for n, (g, k) in enumerate(parts):
                tiles, col, width = GROUPS[g]
                if n >= 8:
                    pe.wait_ge(part_free, n - 7)
                for t in tiles:
                    c, w = tile_cols(t)
                    if k == 0:
                        pe.wait_ge(x_loaded[t], 32 if t == 0 else 16)
                    last = pe.transpose(bank[n % 8][:, c - col:c - col + w], x_nat[0:w, t, P * k:P * k + P], ident[0:w, 0:w])
                last.then_inc(part_full, 1)
            pe.wait_ge(part_free, len(parts))
            pe.wait_ge(wf_split, 2)
            for c, (col, w) in enumerate(CHUNKS):
                three_pass(pe, bank[c][0:HEADS, 0:w],
                           [(wf_hi[:, k, :], wf_lo[:, k, :], m.act_hi[:, k, col:col + w], m.act_lo[:, k, col:col + w])
                            for k in range(KT)]).then_inc(f_full, 1)
            pe.wait_ge(diag_ready, NT)
            for g, (tiles, col, width) in enumerate(GROUPS):
                for t in tiles:
                    c, w = tile_cols(t)
                    last = pe.matmul(bank[3 + g][:, c - col:c - col + w], ones[0:w, :], diag[0:w, t, 0:w], start=True, stop=True)
                last.then_inc(rms_full, 1)
            pe.wait_ge(f_step, 1)
            for t in range(NC):
                last = pe.transpose(bank[0][0:HEADS, P * t:P * t + P], cache_f[:, t, :], ident[:, :])
            last.then_inc(f_cache_full, 1)
            pe.wait_ge(w_split, 1)
            for t in range(NT):
                c, w = tile_cols(t)
                if t >= 2:
                    pe.wait_ge(proj_free[t % 2], t // 2)
                three_pass(pe, bank[6 + t % 2][0:w, 0:2 * DH],
                           [(m.act_hi[:, k, c:c + w], m.act_lo[:, k, c:c + w], m.kv_w_hi[:, k, :], m.kv_w_lo[:, k, :])
                            for k in range(KT)]).then_inc(proj_full[t % 2], 1)
            pe.wait_ge(w_split, 2)
            for c, (col, w) in enumerate(CHUNKS):
                b, nth = (1, 4) if c == 0 else (0, 5) if c == 1 else (1, 5)
                pe.wait_ge(proj_free[b], nth)
                three_pass(pe, bank[6 + b][:, 0:w],
                           [(m.g_w_hi[:, k, 0:DH], m.g_w_lo[:, k, 0:DH], m.act_hi[:, k, col:col + w], m.act_lo[:, k, col:col + w])
                            for k in range(KT)]).then_inc(proj_full[b], 1)
            pe.wait_ge(f_step, 12)
            for n, src in enumerate((log_f, f_cum)):
                for t in range(NT):
                    c, w = tile_cols(t)
                    last = pe.transpose(bank[1 + n][0:w, HEADS * t:HEADS * t + HEADS], src[:, c:c + w], ident[0:HEADS, 0:HEADS])
                last.then_inc(f_nat_full, 1)

        @block.scalar
        def _(act):
            act.wait_ge(const_loaded, 32)
            act.wait_ge(ones_ready, 1)

            def squares(t):
                c, w = tile_cols(t)
                act.wait_ge(x_loaded[t], 32 if t == 0 else 16)
                if t > 0:
                    act.wait_ge(squared, t)
                act.activation(square[0:w, :], x_nat[0:w, t, :], ACT.Square, accum_out=ssq[0:w, t:t + 1]).then_inc(squared, 1)

            for t in range(4):
                squares(t)
            for n, (g, k) in enumerate(parts):
                tiles, col, width = GROUPS[g]
                act.wait_ge(part_full, n + 1)
                if n % 2:
                    if n >= XT:
                        act.wait_ge(xt_stored[n % XT], 16 * (n // XT))
                    act.activation(xt[:, n % XT, 0:width], bank[n % 8][:, 0:width], ACT.Copy).then_inc(xt_ready[1], 1)
                act.activation(m.act_hi[:, k, col:col + width], bank[n % 8][:, 0:width], ACT.Copy,
                               scale=a_gain[:, k:k + 1]).then_inc(part_rounded, 1)
                if k == KT - 1 and g < 2:
                    for t in GROUPS[g + 1][0]:
                        squares(t)
            act.wait_ge(rms_step_v, 1)
            act.activation(rms_ln[:, :], ssq[:, :], ACT.Ln).then_inc(rms_step_a, 1)
            act.wait_ge(rms_step_a, 1)
            act.activation(m.rms_rows[:, :], rms_ln[:, :], ACT.Exp, scale=-0.5).then_inc(rms_step_a, 1)
            for g, (tiles, col, width) in enumerate(GROUPS):
                act.wait_ge(rms_full, g + 1)
                act.activation(m.rms_cols[:, col:col + width], bank[3 + g][:, 0:width], ACT.Copy).then_inc(rms_ready, 1)
            for t in range(NT):
                if t == 3:
                    act.wait_ge(f_step, 5)
                    act.activation(f_exp[:, :], f_abs[:, :], ACT.Exp, scale=-1.0).then_inc(f_act, 1)
                if t == 4:
                    act.wait_ge(f_step, 6)
                    act.activation(log_f[:, 0:T], f_abs[:, :], ACT.Ln).then_inc(f_act, 1)
                w = tile_cols(t)[1]
                act.wait_ge(proj_full[t % 2], t // 2 + 1)
                act.activation(m.kv_nat[0:w, t, :], bank[6 + t % 2][0:w, 0:2 * DH], ACT.Copy,
                               scale=m.rms_rows[0:w, t:t + 1]).then_inc(proj_free[t % 2], 1)

        @block.vector
        def _(dve):
            def part_low(n):
                g, k = parts[n]
                tiles, col, width = GROUPS[g]
                dve.wait_ge(part_rounded, n + 1)
                if n % 2 == 0:
                    if n >= XT:
                        dve.wait_ge(xt_stored[n % XT], 16 * (n // XT))
                    dve.tensor_copy(xt[:, n % XT, 0:width], bank[n % 8][:, 0:width]).then_inc(xt_ready[0], 1)
                dve.scalar_tensor_tensor(out=m.act_lo[:, k, col:col + width], in0=bank[n % 8][:, 0:width], scalar=a_gain[:, k:k + 1],
                                         in1=m.act_hi[:, k, col:col + width].bitcast(F32), op0=ALU.mult,
                                         op1=ALU.subtract).then_inc(part_free, 1)

            def newton_small():
                dve.wait_ge(rms_step_a, 2)
                y, v = m.rms_rows[:, :], ssq[:, :]
                dve.tensor_tensor(rms_t[:, :], y, y, ALU.mult).then_inc(rms_step_v, 1)
                dve.wait_ge(rms_step_v, 2)
                dve.scalar_tensor_tensor(out=rms_t[:, :], in0=rms_t[:, :], scalar=-0.5, in1=v, op0=ALU.mult, op1=ALU.mult).then_inc(rms_step_v, 1)
                dve.wait_ge(rms_step_v, 3)
                dve.scalar_tensor_tensor(out=y, in0=rms_t[:, :], scalar=1.5, in1=y, op0=ALU.add, op1=ALU.mult).then_inc(rms_step_v, 1)
                dve.wait_ge(rms_step_v, 4)
                for t in range(NT):
                    dve.tensor_scalar(diag[:, t, :], ident[:, :], m.rms_rows[:, t:t + 1], None, ALU.mult).then_inc(diag_ready, 1)

            for n in range(len(parts)):
                part_low(n)
            dve.wait_ge(squared, NT)
            dve.tensor_scalar(ssq[:, :], ssq[:, :], 1.0 / D, EPS, ALU.mult, ALU.add).then_inc(rms_step_v, 1)
            newton_small()
            dve.wait_ge(rms_ready, 3)
            for c, (col, w) in enumerate(CHUNKS):
                dve.wait_ge(f_full, c + 1)
                last = dve.tensor_tensor(f[:, col:col + w], bank[c][0:HEADS, 0:w], m.rms_cols[0:HEADS, col:col + w], ALU.mult)
            last.then_inc(f_step, 1)
            dve.wait_ge(f_step, 1)
            dve.tensor_scalar(f[:, :], f[:, :], b_f[:, 0:1], None, ALU.add).then_inc(f_step, 1)
            dve.wait_ge(f_cache_full, 1)
            dve.tensor_copy(log_f[:, T:T + PAST], bank[0][0:HEADS, :]).then_inc(f_step, 1)
            dve.wait_ge(f_step, 3)
            dve.tensor_scalar(f_abs[:, :], f[:, :], -1.0, None, ALU.mult).then_inc(f_step, 1)
            dve.wait_ge(f_step, 4)
            dve.tensor_tensor(f_abs[:, :], f_abs[:, :], f[:, :], ALU.max).then_inc(f_step, 1)
            dve.wait_ge(f_act, 1)
            dve.tensor_scalar(f_abs[:, :], f_exp[:, :], 1.0, None, ALU.add).then_inc(f_step, 1)
            dve.wait_ge(f_act, 2)
            dve.scalar_tensor_tensor(out=f_exp[:, :], in0=f_abs[:, :], scalar=-1.0, in1=f_exp[:, :], op0=ALU.add,
                                     op1=ALU.subtract).then_inc(f_step, 1)
            dve.wait_ge(f_step, 7)
            dve.tensor_tensor(f_exp[:, :], f_exp[:, :], log_f[:, 0:T], ALU.subtract).then_inc(f_step, 1)
            dve.wait_ge(f_step, 8)
            dve.scalar_tensor_tensor(out=log_f[:, 0:T], in0=f[:, :], scalar=0.0, in1=f_exp[:, :], op0=ALU.min,
                                     op1=ALU.add).then_inc(f_step, 1)
            dve.wait_ge(f_step, 9)
            dve.tensor_tensor_scan(f_cum[:, N_SAMPLE:T], row_ones[:, N_SAMPLE:T], log_f[:, N_SAMPLE:T], 0.0, ALU.mult, ALU.add).then_inc(f_step, 1)
            dve.tensor_tensor_scan(f_cum[:, T:T + PAST], row_ones[:, 0:PAST], log_f[:, T:T + PAST], 0.0, ALU.mult, ALU.add).then_inc(f_step, 1)
            dve.wait_ge(f_step, 11)
            dve.tensor_tensor_scan(f_cum[:, 0:N_SAMPLE], row_ones[:, 0:N_SAMPLE], log_f[:, 0:N_SAMPLE],
                                   f_cum[:, T + PAST - 1:T + PAST], ALU.mult, ALU.add).then_inc(f_step, 1)
            for c, (col, w) in enumerate(CHUNKS):
                b, nth = (1, 4) if c == 0 else (0, 5) if c == 1 else (1, 5)
                dve.wait_ge(proj_full[b], nth + 1)
                dve.scalar_tensor_tensor(out=m.query_32[:, col:col + w], in0=bank[6 + b][:, 0:w], scalar=-FOX_SCALE,
                                         in1=m.rms_cols[:, col:col + w], op0=ALU.mult, op1=ALU.mult).then_inc(proj_free[b], 1)
            dve.wait_ge(f_nat_full, 2)
            dve.tensor_copy(log_f_nat[0:SMALL, 0, :], bank[1][0:SMALL, 0:HEADS])
            dve.tensor_copy(log_f_nat[:, 1:NT, :], bank[1][:, HEADS:NT * HEADS].rearrange("p (t h) -> p t h", h=HEADS)).then_inc(f_step, 1)
            dve.tensor_scalar(m.f_query_all[0:SMALL, :, 0], bank[2][0:SMALL, 0:HEADS], -1.0, None, ALU.mult)
            dve.tensor_scalar(m.f_query_all[:, :, 1:NT].rearrange("p h t -> p t h"),
                              bank[2][:, HEADS:NT * HEADS].rearrange("p (t h) -> p t h", h=HEADS), -1.0, None, ALU.mult)


class Dram:

    def __init__(self, nc, a, outs):
        self.x_prompt, self.x_sample, self.meta = a["x_prompt"][0], a["x_sample"][0], a["meta"]
        self.cache_k = a["cache_fox_k"][0, 0].rearrange("t h d -> t (h d)")
        self.cache_v = a["cache_fox_v"][0, 0].rearrange("t h d -> t (h d)")
        self.cache_f = a["cache_fox_logf"][0, 0]
        self.cache_c, self.cache_r = a["cache_mla_ckv"][0], a["cache_mla_krope"][0]
        self.a_norm, self.a_b_forget, self.a_w_in = a["a_norm"], a["a_b_forget"], a["a_w_in"][0]
        self.a_w_out, self.b_w_out = a["a_w_out"][0], a["b_w_out"][0]
        self.kv_norm, self.kv_lat_norm, self.b_norm = a["kv_norm"], a["kv_lat_norm"], a["b_norm"]
        self.w_dkv, self.b_w_in = a["w_dkv"], a["b_w_in"][0]
        self.b_q_norm, self.b_w_uq, self.ukv = a["b_q_norm"], a["b_w_uq"][0], a["w_ukv"]
        self.final_norm = a["final_norm"]
        self.ident, self.rotate, self.cos, self.sin = a["ident"], a["rotate"], a["cos"], a["sin"]
        (y_p, y_s, k_p, v_p, f_p, c_p, r_p, k_s, v_s, f_s, c_s, r_s) = outs
        self.y_prompt, self.y_sample = y_p[0], y_s[0]
        self.new_k_prompt, self.new_v_prompt = (x[0, 0].rearrange("t h d -> t (h d)") for x in (k_p, v_p))
        self.new_k_sample, self.new_v_sample = (x[0, 0].rearrange("t h d -> t (h d)") for x in (k_s, v_s))
        self.new_f_prompt, self.new_f_sample = f_p[0, 0], f_s[0, 0]
        self.new_c_prompt, self.new_c_sample, self.new_r_prompt, self.new_r_sample = c_p[0], c_s[0], r_p[0], r_s[0]

        def scratch(name, shape):
            return nc.dram_tensor(name, shape, F32, kind="Internal").ap()

        self.resid = scratch("resid", [D, T])
        self.f_cum = scratch("f_cum", [HEADS, T + PAST])
        self.gated = scratch("gated", [D, T])
        self.gated_b = scratch("gated_b", [D, T])
        self.resid_b = scratch("resid_b", [D, T])
        self.q_nope = scratch("q_nope", [D, T])
        self.q_rope_hi, self.q_rope_lo = (nc.dram_tensor(n, [HEADS * ROPE, T], F32R, kind="Internal").ap() for n in ("q_rope_hi", "q_rope_lo"))
        self.q_rope_small = scratch("q_rope_small", [HEADS * ROPE, SMALL])

    def fox_w(self, sec, h):
        start = (0, D, 2 * D, 3 * D + HEADS)[sec]
        return self.a_w_in[:, bass.ds(start + h * DH, DH)].rearrange("(k p) n -> p k n", p=P)

    def w_ukv(self, h):
        return self.ukv[:, bass.ds(h * 2 * DH, 2 * DH)].rearrange("(k p) n -> p k n", p=P)

    def w_gate(self, h):
        return self.b_w_in[:, bass.ds(Q_LORA + h * DH, DH)].rearrange("(k p) n -> p k n", p=P)


def load_latent_weights(eng, dram, n, dst, done):
    if n == KV_LORA // P:
        parts = [(dst[:, :, half:half + ROPE], dram.w_dkv[:, KV_LORA:KV_LORA + ROPE]) for half in (0, ROPE)]
    elif n < KV_LORA // P:
        parts = [(dst, dram.w_dkv[:, P * n:P * n + P])]
    else:
        col = P * n - KV_LORA - P
        parts = [(dst, dram.b_w_in[:, col:col + P])]
    for d, src in parts:
        eng.dma_start(d, src.rearrange("(k p) n -> p k n", p=P)).then_inc(done, 16)


def out_projection(nc, m, dram, name, gated_src, w_out, resid_src, resid_dst, final):
    bank = m.bank
    with ExitStack() as st:
        sems = []
        st.callback(nc.all_engine_barrier)
        st.callback(nc.clear_and_free_semaphores, sems)

        def sb(n, shape, dtype=F32):
            return st.enter_context(nc.sbuf_tensor(name + n, shape, dtype))

        def sem(n):
            sems.append(nc.alloc_semaphore(name + n))
            return sems[-1]

        o_in = sb("o_in", [P, 2, T])
        o_hi, o_lo = sb("o_hi", [P, HEADS, T], F32R), sb("o_lo", [P, HEADS, T], F32R)
        w_in, w_hi, w_lo = m.w_in, m.w_hi, m.w_lo
        resid = sb("resid", [P, 2, T])
        square, sq_sum = sb("square", [P, T]), m.sq_sum
        if not final:
            sq_hi, sq_lo = o_hi[:, 0, :], o_lo[:, 0, :]
            ones = sb("ones", [P, P], F32R)
        o_loaded, o_rounded, o_split = [sem("o_loaded0"), sem("o_loaded1")], sem("o_rounded"), sem("o_split")
        w_loaded, w_rounded, w_split = [sem("w_loaded0"), sem("w_loaded1")], sem("w_rounded"), sem("w_split")
        y_full, y_summed = sem("y_full"), sem("y_summed")
        r_loaded, r_stored = [sem("r_loaded0"), sem("r_loaded1")], [sem("r_stored0"), sem("r_stored1")]
        x_rounded, x_split, squared, sq_added = sem("x_rounded"), sem("x_split"), sem("squared"), sem("sq_added")
        stat_split, stat_full, stat_a = sem("stat_split"), sem("stat_full"), sem("stat_a")
        next_loaded, next_scaled = [sem(f"next_loaded{n}") for n in range(3)], sem("next_scaled")
        first_split = sem("first_split")
        ones_ready, pool_waited = sem("ones_ready"), sem("pool_waited")
        PAIRS = KT // 2
        block = st.enter_context(nc.Block())

        def w_cols(fb):
            return w_out[:, bass.ds(fb * P, P)].rearrange("(k p) n -> p k n", p=P)

        @block.sync
        def _(sp):
            def load_w(fb, q):
                sp.dma_start(w_in[:, q, :, :], w_cols(fb)).then_inc(w_loaded[q], 16)

            def load_resid(fb, q):
                sp.dma_start(resid[:, q, :], resid_src[bass.ds(fb * P, P), :]).then_inc(r_loaded[q], 16)

            load_w(0, 0)
            for h in range(HEADS):
                if h >= 2:
                    sp.wait_ge(o_split, h - 1)
                sp.dma_start(o_in[:, h % 2, :], gated_src[h * DH:h * DH + DH, :]).then_inc(o_loaded[h % 2], 16)
                if h == 0:
                    load_w(1, 1)
                if h == 2 and not final:
                    sp.dma_start(m.q_in_gain[:, :], dram.b_norm).then_inc(next_loaded[0], 16)
                    sp.dma_start(m.kv_in_gain[:, :], dram.kv_norm).then_inc(next_loaded[0], 16)
                    load_latent_weights(sp, dram, 0, w_in[:, 2, :, :], next_loaded[0])
            load_resid(0, 0)
            load_resid(1, 1)

            def pair(i, last):
                for q in range(2):
                    if not last:
                        sp.wait_ge(w_split, 2 * i + q + 1)
                        load_w(2 * i + q + 2, q)
                for q in range(2):
                    if not final:
                        sp.wait_ge(y_summed, 2 * i + q + 1)
                        sp.dma_start(resid_dst[bass.ds((2 * i + q) * P, P), :], resid[:, q, :]).then_inc(r_stored[q], 16)
                for q in range(2):
                    if not last:
                        if final:
                            sp.wait_ge(y_summed, 2 * i + q + 1)
                        else:
                            sp.wait_ge(r_stored[q], 16 * i + 16)
                            sp.wait_ge(x_split, 2 * i + q + 1)
                            sp.wait_ge(squared, 2 * i + q + 1)
                        load_resid(2 * i + q + 2, q)

            with sp.Fori(0, PAIRS - 1) as i:
                pair(i, False)
            pair(PAIRS - 1, True)
            if not final:
                for n in (1, 2):
                    sp.wait_ge(w_split, KT - 2 + n)
                    load_latent_weights(sp, dram, n, w_in[:, n - 1, :, :], next_loaded[n])
                for q in range(2):
                    sp.wait_ge(r_stored[q], 16 * PAIRS)
                sp.wait_ge(next_loaded[2], 32)

        @block.gpsimd
        def _(pool):
            pool.memset(sq_sum[:, :], 0.0).then_inc(sq_added, 1)
            if not final:
                pool.memset(ones[:, :].bitcast(F32), 1.0).then_inc(ones_ready, 1)

            def split(i, q):
                n = 2 * i + q
                wait_apart(pool, w_loaded[q], 16 * i + 16, pool_waited)
                wait_apart(pool, y_full, 6 * i, pool_waited)
                pool.tensor_scalar(w_hi[q][:, :, :], w_in[:, q, :, :], 1.0, 0.0, ALU.mult, ALU.add).then_inc(w_rounded, 1)
                pool.wait_ge(w_rounded, n + 1)
                pool.tensor_tensor(w_lo[q][:, :, :], w_in[:, q, :, :], w_hi[q][:, :, :].bitcast(F32), ALU.subtract).then_inc(w_split, 1)

            def add(i, q):
                wait_apart(pool, squared, 2 * i + q + 1, pool_waited)
                pool.wait_ge(sq_added, 2 * i + q + 1)
                pool.tensor_tensor(sq_sum[:, :], sq_sum[:, :], square[:, :], ALU.add).then_inc(sq_added, 1)

            pool.wait_ge(first_split, 1)
            pool.sem_inc(w_split, 1)
            split(0, 1)
            if not final:
                pool.wait_ge(ones_ready, 1)
            with pool.Fori(0, PAIRS - 1) as i:
                for q in range(2):
                    wait_apart(pool, y_full, 6 * i + 3 * q + 3, pool_waited)
                    n = 2 * i + q + 2
                    wait_apart(pool, w_loaded[q], 16 * i + 32, pool_waited)
                    pool.tensor_scalar(w_hi[q][:, :, :], w_in[:, q, :, :], 1.0, 0.0, ALU.mult, ALU.add).then_inc(w_rounded, 1)
                    pool.wait_ge(w_rounded, n + 1)
                    pool.tensor_tensor(w_lo[q][:, :, :], w_in[:, q, :, :], w_hi[q][:, :, :].bitcast(F32), ALU.subtract).then_inc(w_split, 1)
                    add(i, q)
            if not final:
                for n in range(2):
                    slot = (n + 2) % 3
                    pool.wait_ge(next_loaded[n], (48, 16)[n])
                    for k in range(KT):
                        last = pool.tensor_scalar(w_in[:, slot, k, :], w_in[:, slot, k, :], m.kv_in_gain[:, k:k + 1], 1.0, ALU.mult, ALU.mult)
                    last.then_inc(next_scaled, 1)
                    pool.wait_ge(next_scaled, 2 * n + 1)
                    pool.wait_ge(y_full, 3 * (KT - 1 + n))
                    pool.tensor_scalar(w_hi[n][:, :, :], w_in[:, slot, :, :], 1.0, 0.0, ALU.mult, ALU.add).then_inc(next_scaled, 1)
                    pool.wait_ge(next_scaled, 2 * n + 2)
                    pool.tensor_tensor(w_lo[n][:, :, :], w_in[:, slot, :, :], w_hi[n][:, :, :].bitcast(F32), ALU.subtract)
                    if n == 0:
                        add(PAIRS - 1, 0)
                        add(PAIRS - 1, 1)
            else:
                for q in range(2):
                    add(PAIRS - 1, q)

        @block.tensor
        def _(pe):
            def product(i, q, k, c):
                col, w = CHUNKS[c]
                out = bank[3 * q + c][:, 0:w]
                pe.matmul(out, w_hi[q][:, k, :], o_hi[:, k, col:col + w], start=k == 0, stop=False)
                pe.matmul(out, w_hi[q][:, k, :], o_lo[:, k, col:col + w], start=False, stop=False)
                last = pe.matmul(out, w_lo[q][:, k, :], o_hi[:, k, col:col + w], start=False, stop=k == KT - 1)
                if k == KT - 1:
                    last.then_inc(y_full, 1)

            pe.wait_ge(first_split, 1)
            for k in range(KT):
                pe.wait_ge(o_split, k + 1)
                for q in range(2):
                    if k == 0 and q == 1:
                        pe.wait_ge(w_split, 2)
                    for c in range(3):
                        product(0, q, k, c)
            with pe.Fori(1, PAIRS) as i:
                for q in range(2):
                    pe.wait_ge(w_split, 2 * i + q + 1)
                    pe.wait_ge(y_summed, 2 * i + q - 1)
                    for c in range(3):
                        for k in range(KT):
                            product(i, q, k, c)
            if not final:
                pe.wait_ge(stat_split, 1)
                for c, (col, w) in enumerate(CHUNKS):
                    b = (6, 7, 0)[c]
                    if c == 2:
                        pe.wait_ge(y_summed, KT)
                    pe.matmul(bank[b][:, 0:w], ones[:, :], sq_hi[:, col:col + w], start=True, stop=False)
                    pe.matmul(bank[b][:, 0:w], ones[:, :], sq_lo[:, col:col + w], start=False, stop=True).then_inc(stat_full, 1)

        @block.scalar
        def _(act):
            act.wait_ge(w_loaded[0], 16)
            act.activation(w_hi[0][:, :, :], w_in[:, 0, :, :], ACT.Copy).then_inc(w_rounded, 1)
            for h in range(HEADS):
                act.wait_ge(o_loaded[h % 2], 16 * (h // 2) + 16)
                act.activation(o_hi[:, h, :], o_in[:, h % 2, :], ACT.Copy).then_inc(o_rounded, 1)
            if not final:
                act.wait_ge(ones_ready, 1)

            def tile(i, q):
                n = 2 * i + q
                act.wait_ge(y_summed, n + 1)
                if final:
                    y = m.stream[:, bass.ds(n, 1), :].rearrange("p a t -> p (a t)")
                else:
                    y = resid[:, q, :]
                    act.activation(m.act_hi[:, bass.ds(n, 1), :].rearrange("p a t -> p (a t)"), y, ACT.Copy).then_inc(x_rounded, 1)
                act.wait_ge(sq_added, n + 1)
                act.activation(square[:, :], y, ACT.Square).then_inc(squared, 1)

            with act.Fori(0, PAIRS) as i:
                for q in range(2):
                    tile(i, q)
            if not final:
                act.wait_ge(sq_added, KT + 1)
                act.wait_ge(y_full, 3 * KT)
                act.activation(sq_hi, sq_sum[:, :], ACT.Copy).then_inc(stat_a, 1)

        @block.vector
        def _(dve):
            dve.wait_ge(w_rounded, 1)
            dve.tensor_tensor(w_lo[0][:, :, :], w_in[:, 0, :, :], w_hi[0][:, :, :].bitcast(F32), ALU.subtract).then_inc(first_split, 1)
            for h in range(HEADS):
                dve.wait_ge(o_rounded, h + 1)
                dve.tensor_tensor(o_lo[:, h, :], o_in[:, h % 2, :], o_hi[:, h, :].bitcast(F32), ALU.subtract).then_inc(o_split, 1)

            def tile(i, q):
                n = 2 * i + q
                dve.wait_ge(r_loaded[q], 16 * i + 16)
                for c, (col, w) in enumerate(CHUNKS):
                    dve.wait_ge(y_full, 3 * n + c + 1)
                    dst = m.stream[:, bass.ds(n, 1), col:col + w].rearrange("p a t -> p (a t)") if final else resid[:, q, col:col + w]
                    last = dve.tensor_tensor(dst, bank[3 * q + c][:, 0:w], resid[:, q, col:col + w], ALU.add)
                last.then_inc(y_summed, 1)
                if not final:
                    dve.wait_ge(x_rounded, n + 1)
                    dve.tensor_tensor(m.act_lo[:, bass.ds(n, 1), :].rearrange("p a t -> p (a t)"), resid[:, q, :],
                                      m.act_hi[:, bass.ds(n, 1), :].rearrange("p a t -> p (a t)").bitcast(F32), ALU.subtract).then_inc(x_split, 1)

            with dve.Fori(0, PAIRS) as i:
                for q in range(2):
                    tile(i, q)
            if not final:
                dve.wait_ge(stat_a, 1)
                dve.tensor_tensor(sq_lo, sq_sum[:, :], sq_hi.bitcast(F32), ALU.subtract).then_inc(stat_split, 1)
                for c, (col, w) in enumerate(CHUNKS):
                    dve.wait_ge(stat_full, c + 1)
                    dve.tensor_scalar(m.rms_cols[:, col:col + w], bank[(6, 7, 0)[c]][:, 0:w], 1.0 / D, EPS, ALU.mult, ALU.add)


def latents(nc, m, dram):
    bank = m.bank
    ident = m.ident
    with ExitStack() as st:
        sems = []
        st.callback(nc.all_engine_barrier)
        st.callback(nc.clear_and_free_semaphores, sems)

        def sb(name, shape, dtype=F32):
            return st.enter_context(nc.sbuf_tensor("lat_" + name, shape, dtype))

        def sem(name):
            sems.append(nc.alloc_semaphore("lat_" + name))
            return sems[-1]

        KQ, KC = Q_LORA // P, KV_LORA // P
        BLOCKS = KC + 1 + KQ
        KR, Q0 = KC, KC + 1
        SUM_BANKS, TURNED = ((3, 6, 7), (0, 6, 7)), (0, 6, 7)
        RING = 3
        NATW = KV_LORA + ROPE
        stage, w_hi, w_lo = m.w_in, m.w_hi, m.w_lo
        nat = stage[:, :, :, :].rearrange("p a k n -> p (a k n)")[:, 0:NT * NATW].rearrange("p (t n) -> p t n", n=NATW)
        q_gain, c_gain = sb("q_gain", [P, KQ]), sb("c_gain", [P, KC])
        rotate_r, ones = sb("rotate_r", [P, P], F32R), sb("ones", [P, P], F32R)
        latent = sb("latent", [P, KC, T])
        cached = latent[:, :, :].rearrange("p a b -> p (a b)")[:, 0:NC * NATW].rearrange("p (t n) -> p t n", n=NATW)
        rope_k = sb("rope_k", [P, T])
        rotate = rope_k[:, 0:P]
        part_hi, part_lo = sb("part_hi", [P, T], F32R), sb("part_lo", [P, T], F32R)
        sq_sum, square, c_factor = sb("sq_sum", [P, T]), sb("square", [P, T]), sb("c_factor", [P, T])

        gains_loaded, cache_loaded = sem("gains_loaded"), sem("cache_loaded")
        w_loaded, w_scaled, w_rounded, w_split = [sem(f"w_loaded{r}") for r in range(RING)], sem("w_scaled"), sem("w_rounded"), sem("w_split")
        const_ready, rotate_ready = sem("const_ready"), sem("rotate_ready")
        cache_full, cache_rounded, cache_taken = sem("cache_full"), sem("cache_rounded"), sem("cache_taken")
        lat_full, lat_rounded, lat_taken = sem("lat_full"), sem("lat_rounded"), sem("lat_taken")
        squared, sq_added = sem("squared"), sem("sq_added")
        part_rounded, part_split = sem("part_rounded"), sem("part_split")
        sum_full, sum_taken, root = sem("sum_full"), sem("sum_taken"), sem("root")
        turned_full, turned_taken, vec_step = sem("turned_full"), sem("turned_taken"), sem("vec_step")
        rope_done, c_done, c_rounded, k_rounded = sem("rope_done"), sem("c_done"), sem("c_rounded"), sem("k_rounded")
        rms_step = sem("rms_step")
        nat_full, nat_taken, stored = sem("nat_full"), sem("nat_taken"), sem("stored")
        block = st.enter_context(nc.Block())

        @block.sync
        def _(sp):
            for dst, src in ((q_gain, dram.b_q_norm), (c_gain, dram.kv_lat_norm), (rotate, dram.rotate), (m.cos, dram.cos), (m.sin, dram.sin)):
                sp.dma_start(dst[:, :], src).then_inc(gains_loaded, 16)
            sp.dma_start(cached[:, :, 0:KV_LORA], dram.cache_c.rearrange("(t p) n -> p t n", p=P)).then_inc(cache_loaded, 16)
            sp.dma_start(cached[:, :, KV_LORA:NATW], dram.cache_r.rearrange("(t p) n -> p t n", p=P)).then_inc(cache_loaded, 16)
            for n in range(3, BLOCKS):
                r = (n + 2) % RING
                if n == BLOCKS - 1:
                    sp.wait_ge(w_split, 1)
                load_latent_weights(sp, dram, n, stage[:, r, :, :], w_loaded[r])
            sp.wait_ge(nat_taken, NT)
            for dst_p, dst_s, c0, c1 in ((dram.new_c_prompt, dram.new_c_sample, 0, KV_LORA),
                                         (dram.new_r_prompt, dram.new_r_sample, KV_LORA, NATW)):
                sp.dma_start(dst_s, nat[0:N_SAMPLE, 0, c0:c1]).then_inc(stored, 16)
                sp.dma_start(dst_p[0:N_META, :], nat[N_SAMPLE:SMALL, 0, c0:c1]).then_inc(stored, 16)
                sp.dma_start(dst_p[N_META:L, :].rearrange("(t p) d -> p t d", p=P), nat[:, 1:NT, c0:c1]).then_inc(stored, 16)
            sp.wait_ge(stored, 96)

        @block.gpsimd
        def _(pool):
            pool.memset(ones[:, :].bitcast(F32), 1.0).then_inc(const_ready, 1)
            pool.wait_ge(gains_loaded, 16 * 5)
            pool.tensor_scalar(rotate_r[:, :], rotate, 1.0, 0.0, ALU.mult, ALU.add).then_inc(rotate_ready, 1)

            def add(n):
                if n < Q0:
                    pool.wait_ge(squared, n + 1)
                else:
                    pool.wait_ge(lat_rounded, 3 * (n - Q0) + 3)
                pool.tensor_tensor(sq_sum[:, :], sq_sum[:, :], square[:, :], ALU.add).then_inc(sq_added, 1)

            for n in range(2, BLOCKS):
                r = (n + 2) % RING
                if n > 2:
                    pool.wait_ge(w_loaded[r], 16)
                w = stage[:, r, :, :]
                gain = m.q_in_gain if n >= Q0 else m.kv_in_gain
                for k in range(KT):
                    last = pool.tensor_scalar(w[:, k, :], w[:, k, :], gain[:, k:k + 1], 1.0, ALU.mult, ALU.mult)
                last.then_inc(w_scaled, 1)
                pool.wait_ge(w_scaled, n - 1)
                pool.wait_ge(lat_full, 3 * (n - 1))
                pool.tensor_scalar(w_hi[n % 2][:, :, :], w, 1.0, 0.0, ALU.mult, ALU.add).then_inc(w_rounded, 1)
                pool.wait_ge(w_rounded, n - 1)
                pool.tensor_tensor(w_lo[n % 2][:, :, :], w, w_hi[n % 2][:, :, :].bitcast(F32), ALU.subtract).then_inc(w_split, 1)
                if n == 2:
                    add(1)
            add(4)
            pool.wait_ge(sq_added, 2)
            add(5)

        @block.tensor
        def _(pe):
            def block_products(n):
                if n >= 2:
                    pe.wait_ge(lat_taken, 3 * (n - 1))
                    pe.wait_ge(w_split, n - 1)
                for c, (col, w) in enumerate(CHUNKS):
                    if n == 1 and c == 2:
                        pe.wait_ge(cache_taken, 3)
                    three_pass(pe, bank[3 * (n % 2) + c][:, 0:w],
                               [(w_hi[n % 2][:, k, :], w_lo[n % 2][:, k, :], m.act_hi[:, k, col:col + w], m.act_lo[:, k, col:col + w])
                                for k in range(KT)]).then_inc(lat_full, 1)

            def sums(which):
                pe.wait_ge(part_split, (1, 3)[which])
                for c, (col, w) in enumerate(CHUNKS):
                    out = bank[SUM_BANKS[which][c]][:, 0:w]
                    pe.matmul(out, ones[:, :], part_hi[:, col:col + w], start=True, stop=False)
                    pe.matmul(out, ones[:, :], part_lo[:, col:col + w], start=False, stop=True).then_inc(sum_full, 1)

            def turn_out(t):
                c, n = tile_cols(t)
                b = 1 + t % 2
                if t >= 2:
                    pe.wait_ge(nat_taken, t - 1)
                for k in range(KC):
                    pe.transpose(bank[b][0:n, P * k:P * k + P], latent[:, k, c:c + n], ident[:, :])
                pe.transpose(bank[b][0:n, KV_LORA:NATW], rope_k[0:ROPE, c:c + n], ident[0:ROPE, 0:ROPE]).then_inc(nat_full, 1)

            block_products(0)
            pe.wait_ge(cache_loaded, 32)
            for k in range(KC):
                for t in range(NC):
                    last = pe.transpose(bank[6 + k][:, P * t:P * t + P], cached[:, t, P * k:P * k + P], ident[:, :])
                last.then_inc(cache_full, 1)
            for t in range(NC):
                last = pe.transpose(bank[5][0:ROPE, P * t:P * t + P], cached[:, t, KV_LORA:NATW], ident[:, :])
            last.then_inc(cache_full, 1)
            pe.wait_ge(const_ready, 1)
            block_products(1)
            block_products(2)
            pe.wait_ge(lat_taken, 6)
            sums(0)
            pe.wait_ge(sum_taken, 1)
            block_products(3)
            pe.wait_ge(rotate_ready, 1)
            pe.wait_ge(part_split, 2)
            pe.wait_ge(sum_taken, 3)
            pe.wait_ge(lat_taken, 9)
            for c, (col, w) in enumerate(CHUNKS):
                pe.matmul(bank[TURNED[c]][:, 0:w], rotate_r[:, :], part_hi[:, col:col + w], start=True, stop=False)
                pe.matmul(bank[TURNED[c]][:, 0:w], rotate_r[:, :], part_lo[:, col:col + w], start=False, stop=True).then_inc(turned_full, 1)
            pe.wait_ge(turned_taken, 1)
            block_products(4)
            block_products(5)
            pe.wait_ge(lat_taken, 15)
            pe.wait_ge(turned_taken, 3)
            pe.wait_ge(rope_done, 1)
            pe.wait_ge(c_done, 1)
            turn_out(0)
            turn_out(1)
            sums(1)
            for t in range(2, NT):
                turn_out(t)

        @block.scalar
        def _(act):
            act.activation(square[:, :], m.rms_cols[:, :], ACT.Ln).then_inc(rms_step, 1)
            act.wait_ge(rms_step, 1)
            act.activation(c_factor[:, :], square[:, :], ACT.Exp, scale=-0.5).then_inc(rms_step, 1)
            act.wait_ge(gains_loaded, 16 * 5)

            def squares(n):
                act.wait_ge(lat_taken, 3 * n + 3)
                act.activation((square if n else sq_sum)[:, :], latent[:, n, :], ACT.Square).then_inc(squared, 1)

            def rounded_sums(which):
                act.wait_ge(sq_added, (1, 3)[which])
                act.activation(part_hi[:, :], sq_sum[:, :], ACT.Copy).then_inc(part_rounded, 1)

            def roots(which, factor):
                act.wait_ge(root, 3 * which + 1)
                act.activation(square[:, :], sq_sum[:, :], ACT.Ln).then_inc(root, 1)
                act.wait_ge(root, 3 * which + 2)
                act.activation(factor[:, :], square[:, :], ACT.Exp, scale=-0.5).then_inc(root, 1)

            def query_block(n):
                if n == 2:
                    act.wait_ge(sq_added, 2)
                for c, (col, w) in enumerate(CHUNKS):
                    psum = bank[3 * ((Q0 + n) % 2) + c][:, 0:w]
                    act.wait_ge(lat_full, 3 * (Q0 + n) + c + 1)
                    act.activation(m.ql_hi[:, n, col:col + w], psum, ACT.Copy, scale=q_gain[:, n:n + 1])
                    act.activation((square if n else sq_sum)[:, col:col + w], psum, ACT.Square).then_inc(lat_rounded, 1)

            for k in range(KC):
                act.wait_ge(cache_full, k + 1)
                act.activation(m.c_hi[:, k, T:T + PAST], bank[6 + k][:, :], ACT.Copy).then_inc(cache_rounded, 1)
            squares(0)
            squares(1)
            rounded_sums(0)
            act.wait_ge(lat_taken, 9)
            act.wait_ge(sum_full, 3)
            act.activation(part_hi[:, :], rope_k[:, :], ACT.Copy).then_inc(part_rounded, 1)
            roots(0, c_factor)
            act.wait_ge(vec_step, 9)
            query_block(0)
            act.wait_ge(rope_done, 1)
            act.activation(m.rope_k_hi[:, :], rope_k[:, :], ACT.Copy).then_inc(k_rounded, 1)
            act.wait_ge(c_done, 1)
            act.activation(m.c_hi[:, :, 0:T], latent[:, :, :], ACT.Copy).then_inc(c_rounded, 1)
            query_block(1)
            query_block(2)
            rounded_sums(1)
            for t in range(NT):
                n = tile_cols(t)[1]
                act.wait_ge(nat_full, t + 1)
                act.activation(nat[0:n, t, :], bank[1 + t % 2][0:n, 0:NATW], ACT.Copy).then_inc(nat_taken, 1)
                if t == 4:
                    roots(1, m.q_factor)

        @block.vector
        def _(dve):
            count = [0]

            def chain(ins):
                ins.then_inc(vec_step, 1)
                count[0] += 1
                dve.wait_ge(vec_step, count[0])

            def sums_low(which, n_features, factor):
                dve.wait_ge(part_rounded, (1, 3)[which])
                dve.tensor_tensor(part_lo[:, :], sq_sum[:, :], part_hi[:, :].bitcast(F32), ALU.subtract).then_inc(part_split, 1)
                chain(dve.scalar_tensor_tensor(out=factor[:, :], in0=m.rms_cols[:, :], scalar=1.0 / n_features, in1=m.rms_cols[:, :],
                                               op0=ALU.mult, op1=ALU.mult))

            def means(which, factor):
                for c, (col, w) in enumerate(CHUNKS):
                    dve.wait_ge(sum_full, 3 * which + c + 1)
                    dve.tensor_tensor(sq_sum[:, col:col + w], bank[SUM_BANKS[which][c]][:, 0:w], factor[:, col:col + w],
                                      ALU.mult).then_inc(sum_taken, 1)
                dve.wait_ge(sum_taken, 3 * which + 3)
                dve.tensor_scalar(sq_sum[:, :], sq_sum[:, :], 1.0, EPS, ALU.mult, ALU.add).then_inc(root, 1)

            def factors(which, factor, scale):
                dve.wait_ge(root, 3 * which + 3)
                y, var = factor[:, :], sq_sum[:, :]
                chain(dve.tensor_tensor(square[:, :], y, y, ALU.mult))
                chain(dve.scalar_tensor_tensor(out=square[:, :], in0=square[:, :], scalar=-0.5, in1=var, op0=ALU.mult, op1=ALU.mult))
                chain(dve.scalar_tensor_tensor(out=y, in0=square[:, :], scalar=1.5, in1=y, op0=ALU.add, op1=ALU.mult))
                chain(dve.scalar_tensor_tensor(out=y, in0=y, scalar=scale, in1=m.rms_cols[:, :], op0=ALU.mult, op1=ALU.mult))

            def copy_latent(n):
                for c, (col, w) in enumerate(CHUNKS):
                    dve.wait_ge(lat_full, 3 * n + c + 1)
                    dve.tensor_copy(latent[:, n, col:col + w], bank[3 * (n % 2) + c][:, 0:w]).then_inc(lat_taken, 1)

            def query_low(n):
                for c, (col, w) in enumerate(CHUNKS):
                    dve.wait_ge(lat_rounded, 3 * n + c + 1)
                    dve.scalar_tensor_tensor(out=m.ql_lo[:, n, col:col + w], in0=bank[3 * ((Q0 + n) % 2) + c][:, 0:w], scalar=q_gain[:, n:n + 1],
                                             in1=m.ql_hi[:, n, col:col + w].bitcast(F32), op0=ALU.mult, op1=ALU.subtract).then_inc(lat_taken, 1)

            dve.wait_ge(rms_step, 2)
            chain(dve.tensor_tensor(square[:, :], c_factor[:, :], c_factor[:, :], ALU.mult))
            chain(dve.scalar_tensor_tensor(out=square[:, :], in0=square[:, :], scalar=-0.5, in1=m.rms_cols[:, :], op0=ALU.mult, op1=ALU.mult))
            chain(dve.scalar_tensor_tensor(out=m.rms_cols[:, :], in0=square[:, :], scalar=1.5, in1=c_factor[:, :], op0=ALU.add, op1=ALU.mult))
            dve.wait_ge(gains_loaded, 16 * 5)
            for k in range(KC):
                dve.wait_ge(cache_rounded, k + 1)
                dve.tensor_tensor(m.c_lo[:, k, T:T + PAST], bank[6 + k][:, :], m.c_hi[:, k, T:T + PAST].bitcast(F32),
                                  ALU.subtract).then_inc(cache_taken, 1)
            dve.wait_ge(cache_full, 3)
            dve.tensor_copy(m.rope_k32[0:ROPE, P:P + PAST], bank[5][0:ROPE, :]).then_inc(cache_taken, 1)
            copy_latent(0)
            copy_latent(1)
            sums_low(0, KV_LORA, c_factor)
            dve.wait_ge(rotate_ready, 1)
            for c, (col, w) in enumerate(CHUNKS):
                dve.wait_ge(lat_full, 3 * KR + c + 1)
                dve.tensor_tensor(rope_k[:, col:col + w], bank[3 * (KR % 2) + c][:, 0:w], m.rms_cols[:, col:col + w], ALU.mult).then_inc(lat_taken, 1)
            means(0, c_factor)
            dve.wait_ge(lat_taken, 9)
            dve.wait_ge(part_rounded, 2)
            dve.tensor_tensor(part_lo[:, :], rope_k[:, :], part_hi[:, :].bitcast(F32), ALU.subtract).then_inc(part_split, 1)
            dve.wait_ge(part_split, 2)
            chain(dve.tensor_tensor(rope_k[:, :], rope_k[:, :], m.cos[:, :], ALU.mult))
            factors(0, c_factor, 1.0)
            for k in range(KC):
                last = dve.scalar_tensor_tensor(out=latent[:, k, :], in0=latent[:, k, :], scalar=c_gain[:, k:k + 1], in1=c_factor[:, :],
                                                op0=ALU.mult, op1=ALU.mult)
            last.then_inc(c_done, 1)
            query_low(0)
            dve.wait_ge(c_done, 1)
            for c, (col, w) in enumerate(CHUNKS):
                dve.wait_ge(turned_full, c + 1)
                dve.tensor_tensor(c_factor[:, col:col + w], bank[TURNED[c]][:, 0:w], m.sin[:, col:col + w], ALU.mult).then_inc(turned_taken, 1)
            dve.wait_ge(turned_taken, 3)
            dve.tensor_tensor(rope_k[:, :], rope_k[:, :], c_factor[:, :], ALU.add).then_inc(rope_done, 1)
            dve.wait_ge(rope_done, 1)
            dve.tensor_copy(m.rope_k32[:, 0:P], rope_k[:, 0:P])
            dve.wait_ge(k_rounded, 1)
            dve.tensor_tensor(m.rope_k_lo[:, :], rope_k[:, :], m.rope_k_hi[:, :].bitcast(F32), ALU.subtract)
            dve.wait_ge(c_rounded, 1)
            dve.tensor_tensor(m.c_lo[:, :, 0:T], latent[:, :, :], m.c_hi[:, :, 0:T].bitcast(F32), ALU.subtract)
            query_low(1)
            query_low(2)
            sums_low(1, Q_LORA, m.q_factor)
            means(1, m.q_factor)
            factors(1, m.q_factor, MLA_SCALE)


def queries(nc, m, dram):
    bank = m.bank
    with ExitStack() as st:
        sems = []
        st.callback(nc.all_engine_barrier)
        st.callback(nc.clear_and_free_semaphores, sems)

        def sb(name, shape, dtype=F32):
            return st.enter_context(nc.sbuf_tensor("q_" + name, shape, dtype))

        def sem(name):
            sems.append(nc.alloc_semaphore("q_" + name))
            return sems[-1]

        KQ, KC = Q_LORA // P, KV_LORA // P
        PW = 2 * QK_HEAD
        PAIRS = HEADS // 2
        W = KQ * PW
        flat = m.kv_nat[:, :, :].rearrange("p t n -> p (t n)")
        stage = [flat[:, W * q:W * q + W].rearrange("p (k a n) -> p k a n", k=KQ, a=2) for q in range(2)]
        g_stage = flat[:, 2 * W:2 * W + KT * DH].rearrange("p (k n) -> p k n", n=DH)
        w_hi = [sb("w_hi0", [P, KQ, PW], F32R), m.g_hi_space[:, 0:W].rearrange("p (k n) -> p k n", k=KQ)]
        w_lo = [sb("w_lo0", [P, KQ, PW], F32R), m.g_lo_space[:, 0:W].rearrange("p (k n) -> p k n", k=KQ)]
        rotate, rotate_r = sb("rotate", [P, P]), sb("rotate_r", [P, P], F32R)
        raw = sb("raw", [P, T])
        raw_hi, raw_lo = sb("raw_hi", [P, T], F32R), sb("raw_lo", [P, T], F32R)
        turned = sb("turned", [P, T])
        rope_hi, rope_lo = raw_hi, raw_lo
        nope = [m.query_32, m.stage_space]

        const_loaded, kv_w_loaded, g_w_loaded = sem("const_loaded"), sem("kv_w_loaded"), sem("g_w_loaded")
        w_loaded, w_rounded, w_split = [sem("w_loaded0"), sem("w_loaded1")], sem("w_rounded"), sem("w_split")
        pool_step, first_split = sem("pool_step"), sem("first_split")
        full, taken = sem("full"), sem("taken")
        raw_rounded, raw_split = sem("raw_rounded"), sem("raw_split")
        cos_done, sin_done, rope_ready, rope_rounded, rope_split = sem("cos_done"), sem("sin_done"), sem("rope_ready"), sem("rope_rounded"), sem("rope_split")
        nope_stored, small_stored, rope_stored = [sem("nope_stored0"), sem("nope_stored1")], sem("small_stored"), sem("rope_stored")
        g_w_split, kv_w_split, kv_full, kv_taken = sem("g_w_split"), sem("kv_w_split"), sem("kv_full"), sem("kv_taken")
        block = st.enter_context(nc.Block())
        USES = 12

        def weight_parts(q):
            parts = []
            for c0, c1, s0, s1 in ((2 * DH, PW, DH, QK_HEAD), (0, 2 * DH, 0, DH)):
                for k in range(KQ):
                    hi, lo = (x[q][:, k, c0:c1].rearrange("p (a n) -> p a n", a=2) for x in (w_hi, w_lo))
                    parts.append((stage[q][:, k, :, s0:s1], hi, lo))
            return parts

        @block.sync
        def _(sp):
            def load_w(n, q):
                for k in range(KQ):
                    sp.dma_start(stage[q][:, k, :, :].rearrange("p a n -> p (a n)"), dram.b_w_uq[P * k:P * k + P, bass.ds(n * PW, PW)]).then_inc(w_loaded[q], 16)

            def store(n):
                for a in range(2):
                    sp.wait_ge(taken, USES * n + 3 * a + 6)
                    sp.dma_start(dram.q_nope[bass.ds((2 * n + a) * P, P), :], nope[a][:, :]).then_inc(nope_stored[a], 16)
                sp.wait_ge(rope_ready, n + 1)
                sp.dma_start(dram.q_rope_small[bass.ds(2 * n * ROPE, P), :], raw[:, 0:SMALL]).then_inc(small_stored, 16)

            load_w(0, 0)
            sp.dma_start(rotate[:, :], dram.rotate).then_inc(const_loaded, 16)
            load_w(1, 1)
            sp.dma_start(g_stage, dram.w_gate(0)).then_inc(g_w_loaded, 16)
            sp.dma_start(m.b_gain[:, :], dram.b_norm).then_inc(g_w_loaded, 16)
            kv_stage = nope[1][:, 0:2 * 2 * DH].rearrange("p (k n) -> p k n", n=2 * DH)
            sp.dma_start(kv_stage, dram.w_ukv(0)).then_inc(kv_w_loaded, 16)
            sp.wait_ge(first_split, 6)
            load_w(2, 0)
            store(0)
            sp.wait_ge(w_split, 1)
            load_w(3, 1)
            store(1)
            store(2)
            store(3)
            for a in range(2):
                sp.wait_ge(nope_stored[a], 16 * PAIRS)
            sp.wait_ge(small_stored, 16 * PAIRS)

        @block.gpsimd
        def _(pool):
            count = [0]

            def chain(ins):
                ins.then_inc(pool_step, 1)
                count[0] += 1
                pool.wait_ge(pool_step, count[0])

            def split(n):
                q = n % 2
                pool.wait_ge(w_loaded[q], 16 * KQ * (n // 2) + 16 * KQ)
                if n >= 2:
                    pool.wait_ge(full, USES * (n - 1))
                parts = weight_parts(q)
                for s, hi, lo in parts:
                    last = pool.tensor_scalar(hi, s, 1.0, 0.0, ALU.mult, ALU.add)
                chain(last)
                for s, hi, lo in parts:
                    last = pool.tensor_tensor(lo, s, hi.bitcast(F32), ALU.subtract)
                last.then_inc(w_split, 1)

            def store_rope(n):
                pool.wait_ge(rope_split, n + 1)
                for dst, part in ((dram.q_rope_hi, rope_hi), (dram.q_rope_lo, rope_lo)):
                    pool.dma_start(dst[2 * ROPE * n:2 * ROPE * n + 2 * ROPE, :], part[:, :]).then_inc(rope_stored, 16)

            pool.wait_ge(const_loaded, 16)
            chain(pool.tensor_scalar(rotate_r[:, :], rotate[:, :], 1.0, 0.0, ALU.mult, ALU.add))
            kv_stage = nope[1][:, 0:2 * 2 * DH].rearrange("p (k n) -> p k n", n=2 * DH)
            pool.wait_ge(kv_w_loaded, 16)
            chain(pool.tensor_scalar(m.kv_w_hi[:, :, :], kv_stage, 1.0, 0.0, ALU.mult, ALU.add))
            pool.tensor_tensor(m.kv_w_lo[:, :, :], kv_stage, m.kv_w_hi[:, :, :].bitcast(F32), ALU.subtract).then_inc(kv_w_split, 1)
            split(1)
            pool.memset(m.mask_big[:, :], -BIG)
            pool.memset(m.mask_rows[:, 64:128], 0.0)
            pool.memset(m.mask_rows[:, 0:64], 1.0)
            pool.memset(m.mask_rows[:, 128:256], 1.0)
            pool.wait_ge(g_w_loaded, 32)
            for k in range(KT):
                last = pool.tensor_scalar(g_stage[:, k, :], g_stage[:, k, :], m.b_gain[:, k:k + 1], 1.0, ALU.mult, ALU.mult)
            chain(last)
            store_rope(0)
            split(2)
            store_rope(1)
            split(3)
            pool.wait_ge(w_split, 3)
            chain(pool.memset(m.kv_nat[:, 0, :], 0.0))
            store_rope(2)
            pool.wait_ge(full, USES * PAIRS)
            chain(pool.tensor_scalar(m.g_w_hi, g_stage, 1.0, 0.0, ALU.mult, ALU.add))
            pool.tensor_tensor(m.g_w_lo, g_stage, m.g_w_hi.bitcast(F32), ALU.subtract).then_inc(g_w_split, 1)
            store_rope(3)
            pool.wait_ge(rope_stored, 16 * 2 * PAIRS)

        @block.tensor
        def _(pe):
            def next_bank(n, u):
                out = bank[(USES * n + u) % 8]
                if USES * n + u >= 8:
                    pe.wait_ge(taken, USES * n + u - 7)
                return out

            for n in range(PAIRS):
                q = n % 2
                for s, lhs in enumerate((slice(2 * DH, PW), slice(0, DH), slice(DH, 2 * DH))):
                    if n:
                        pe.wait_ge(w_split, n)
                    elif s < 2:
                        pe.wait_ge(first_split, KQ * (s + 1))
                    for c, (col, w) in enumerate(CHUNKS):
                        out = next_bank(n, 3 * s + c)
                        three_pass(pe, out[:, 0:w], [(w_hi[q][:, k, lhs], w_lo[q][:, k, lhs], m.ql_hi[:, k, col:col + w], m.ql_lo[:, k, col:col + w])
                                                     for k in range(KQ)]).then_inc(full, 1)
                pe.wait_ge(pool_step, 1)
                pe.wait_ge(raw_split, n + 1)
                for c, (col, w) in enumerate(CHUNKS):
                    out = next_bank(n, 9 + c)
                    pe.matmul(out[:, 0:w], rotate_r[:, :], raw_hi[:, col:col + w], start=True, stop=False)
                    pe.matmul(out[:, 0:w], rotate_r[:, :], raw_lo[:, col:col + w], start=False, stop=True).then_inc(full, 1)
            pe.wait_ge(kv_w_split, 1)
            pe.wait_ge(taken, USES * PAIRS)
            for t in range(NT + NC):
                c, n = tile_cols(t) if t < NT else (T + P * (t - NT), P)
                if t >= 8:
                    pe.wait_ge(kv_taken, t - 7)
                three_pass(pe, bank[t % 8][0:n, 0:2 * DH],
                           [(m.c_hi[:, k, c:c + n], m.c_lo[:, k, c:c + n], m.kv_w_hi[:, k, :], m.kv_w_lo[:, k, :]) for k in range(KC)]
                           ).then_inc(kv_full, 1)

        @block.scalar
        def _(act):
            act.wait_ge(w_loaded[0], 16 * KQ)
            for w, hi, lo in weight_parts(0):
                act.activation(hi, w, ACT.Copy).then_inc(w_rounded, 1)
            for n in range(PAIRS):
                act.wait_ge(taken, USES * n + 3)
                if n:
                    act.wait_ge(rope_stored, 16 * 2 * n)
                act.activation(raw_hi[:, :], raw[:, :], ACT.Copy).then_inc(raw_rounded, 1)
                act.wait_ge(rope_ready, n + 1)
                act.activation(rope_hi[:, :], raw[:, :], ACT.Copy).then_inc(rope_rounded, 1)
            act.wait_ge(pool_step, 7)
            for t in range(NT + NC):
                n = P if t >= NT else tile_cols(t)[1]
                act.wait_ge(kv_full, t + 1)
                if t == 9:
                    act.wait_ge(g_w_split, 1)
                act.activation(m.kv_nat[0:n, t, :], bank[t % 8][0:n, 0:2 * DH], ACT.Copy).then_inc(kv_taken, 1)

        @block.vector
        def _(dve):
            def take(n, u, dst):
                col, w = CHUNKS[u % 3]
                dve.wait_ge(full, USES * n + u + 1)
                last = dve.tensor_tensor(dst[:, col:col + w], bank[(USES * n + u) % 8][:, 0:w], m.q_factor[:, col:col + w], ALU.mult)
                last.then_inc(taken, 1)

            for n, (w, hi, lo) in enumerate(weight_parts(0)):
                dve.wait_ge(w_rounded, n + 1)
                dve.tensor_tensor(lo, w, hi.bitcast(F32), ALU.subtract).then_inc(first_split, 1)
            dve.wait_ge(kv_w_split, 1)
            for n in range(PAIRS):
                if n:
                    dve.wait_ge(rope_split, n)
                    dve.wait_ge(small_stored, 16 * n)
                for u in range(3):
                    take(n, u, raw)
                dve.wait_ge(taken, USES * n + 3)
                dve.wait_ge(raw_rounded, n + 1)
                if n:
                    dve.wait_ge(rope_stored, 16 * 2 * n)
                dve.tensor_tensor(raw_lo[:, :], raw[:, :], raw_hi[:, :].bitcast(F32), ALU.subtract).then_inc(raw_split, 1)
                dve.wait_ge(raw_split, n + 1)
                dve.tensor_tensor(raw[:, :], raw[:, :], m.cos[:, :], ALU.mult).then_inc(cos_done, 1)
                for a in range(2):
                    if n:
                        dve.wait_ge(nope_stored[a], 16 * n)
                    for u in range(3 * a + 3, 3 * a + 6):
                        take(n, u, nope[a])
                for c, (col, w) in enumerate(CHUNKS):
                    u = 9 + c
                    dve.wait_ge(full, USES * n + u + 1)
                    dve.tensor_tensor(turned[:, col:col + w], bank[(USES * n + u) % 8][:, 0:w], m.sin[:, col:col + w], ALU.mult).then_inc(taken, 1)
                dve.wait_ge(taken, USES * n + USES)
                dve.wait_ge(cos_done, n + 1)
                dve.tensor_tensor(raw[:, :], raw[:, :], turned[:, :], ALU.add).then_inc(rope_ready, 1)
                dve.wait_ge(rope_ready, n + 1)
                dve.wait_ge(rope_rounded, n + 1)
                dve.tensor_tensor(rope_lo[:, :], raw[:, :], rope_hi[:, :].bitcast(F32), ALU.subtract).then_inc(rope_split, 1)


def final_norm(nc, m, dram):
    ident = m.ident
    with ExitStack() as st:
        def sb(name, shape, dtype=F32):
            return st.enter_context(nc.sbuf_tensor("final_" + name, shape, dtype))

        def sem(name):
            return nc.alloc_semaphore("final_" + name)

        gain = sb("gain", [P, D])
        ones = sb("ones", [P, 1])
        y = sb("y", [P, 4, D])
        mean, ln, rms, tmp = sb("mean", [P, NT]), sb("ln", [P, NT]), sb("rms", [P, NT]), sb("tmp", [P, NT])
        gain_loaded, ones_ready, sums_full, turned, root, step = sem("gain_loaded"), sem("ones_ready"), sem("sums_full"), sem("turned"), sem("root"), sem("step")
        y_ready, y_stored = sem("y_ready"), [sem(f"y_stored{q}") for q in range(4)]
        block = st.enter_context(nc.Block())
        RING = 3
        SUMS = m.bank[7]

        def banks(t, n):
            return m.psum[0:n, 2 * (t % RING):2 * (t % RING) + 2, :]

        def rows(x, n):
            return x.rearrange("p (a b) -> p a b", a=2)

        @block.sync
        def _(sp):
            sp.dma_start(gain[:, :], dram.final_norm.to_broadcast([P, D])).then_inc(gain_loaded, 16)
            for t in range(NT):
                sp.wait_ge(y_ready, t + 1)
                if t == 0:
                    sp.dma_start(dram.y_sample, y[0:N_SAMPLE, 0, :]).then_inc(y_stored[0], 16)
                else:
                    sp.dma_start(dram.y_prompt[P * (t - 1):P * t, :], y[:, t % 4, :]).then_inc(y_stored[t % 4], 16)
            for q in range(4):
                sp.wait_ge(y_stored[q], 16 * len(range(q, NT, 4)))

        @block.gpsimd
        def _(pool):
            pool.memset(ones[:, :], 1.0).then_inc(ones_ready, 1)

        @block.tensor
        def _(pe):
            pe.wait_ge(ones_ready, 1)
            for t in range(NT):
                c, n = tile_cols(t)
                last = pe.matmul(SUMS[0:n, t:t + 1], m.sq_sum[:, c:c + n], ones[:, :], start=True, stop=True)
            last.then_inc(sums_full, 1)
            for t in range(NT):
                c, n = tile_cols(t)
                if t >= RING:
                    pe.wait_ge(y_ready, t - RING + 1)
                for k in range(KT):
                    last = pe.transpose(m.bank[2 * (t % RING) + k // 4][0:n, P * (k % 4):P * (k % 4) + P], m.stream[:, k, c:c + n], ident[:, :])
                last.then_inc(turned, 1)

        @block.scalar
        def _(act):
            act.wait_ge(step, 2)
            act.activation(ln[:, :], mean[:, :], ACT.Ln).then_inc(root, 1)
            act.wait_ge(root, 1)
            act.activation(rms[:, :], ln[:, :], ACT.Exp, scale=-0.5).then_inc(root, 1)

        @block.vector
        def _(dve):
            dve.memset(mean[:, :], 1.0).then_inc(step, 1)
            dve.wait_ge(step, 1)
            dve.wait_ge(sums_full, 1)
            dve.tensor_scalar(mean[0:SMALL, 0:1], SUMS[0:SMALL, 0:1], 1.0 / D, EPS, ALU.mult, ALU.add)
            dve.tensor_scalar(mean[:, 1:NT], SUMS[:, 1:NT], 1.0 / D, EPS, ALU.mult, ALU.add).then_inc(step, 1)
            dve.wait_ge(root, 2)
            dve.tensor_tensor(tmp[:, :], rms[:, :], rms[:, :], ALU.mult).then_inc(step, 1)
            dve.wait_ge(step, 3)
            dve.scalar_tensor_tensor(out=tmp[:, :], in0=tmp[:, :], scalar=-0.5, in1=mean[:, :], op0=ALU.mult, op1=ALU.mult).then_inc(step, 1)
            dve.wait_ge(step, 4)
            dve.scalar_tensor_tensor(out=rms[:, :], in0=tmp[:, :], scalar=1.5, in1=rms[:, :], op0=ALU.add, op1=ALU.mult).then_inc(step, 1)
            dve.wait_ge(step, 5)
            dve.wait_ge(gain_loaded, 16)
            for t in range(NT):
                n = tile_cols(t)[1]
                dve.wait_ge(turned, t + 1)
                if t >= 4:
                    dve.wait_ge(y_stored[t % 4], 16 * (t // 4))
                dve.scalar_tensor_tensor(out=rows(y[0:n, t % 4, :], n), in0=banks(t, n), scalar=rms[0:n, t:t + 1],
                                         in1=rows(gain[0:n, :], n), op0=ALU.mult, op1=ALU.mult).then_inc(y_ready, 1)


def build(nc, a, outs):
    dram = Dram(nc, a, outs)
    with ExitStack() as whole:
        m = Memory(nc)
        m.psum = whole.enter_context(nc.psum_tensor("psum", [P, 8, 512], F32))
        m.bank = [m.psum[:, b, :] for b in range(8)]
        m.score_banks = lambda first, n: m.psum[:, first:first + n, :]
        m.ident = m.sbuf(whole, "ident", [P, P])
        with ExitStack() as st:
            m.act_hi = m.sbuf(st, "act_hi", [P, KT, T], F32R)
            m.act_lo = m.sbuf(st, "act_lo", [P, KT, T], F32R)
            m.rms_cols = m.sbuf(st, "rms_cols", [P, T])
            with ExitStack() as fox:
                m.kv_act_hi, m.kv_act_lo = m.act_hi, m.act_lo
                m.query_32 = m.sbuf(fox, "query_32", [P, T])
                m.kv_nat = m.sbuf(fox, "kv_nat", [P, NT, 2 * DH])
                m.rms_rows = m.sbuf(fox, "rms_rows", [P, NT])
                m.f_query_all = m.sbuf(fox, "f_query_all", [P, HEADS, NT])
                m.stage = m.sbuf(fox, "stage", [P, KT, 2 * DH])
                m.kv_w_hi = m.sbuf(fox, "kv_w_hi", [P, KT, 2 * DH], F32R)
                m.kv_w_lo = m.sbuf(fox, "kv_w_lo", [P, KT, 2 * DH], F32R)
                m.g_w_hi = m.sbuf(fox, "g_w_hi", [P, KT, 2 * DH], F32R)
                m.g_w_lo = m.sbuf(fox, "g_w_lo", [P, KT, 2 * DH], F32R)
                embed(nc, m, dram)
                attention(nc, m, True, dram)
            ring = ExitStack()
            m.w_in = m.sbuf(ring, "w_in", [P, 3, KT, P])
            m.w_hi = [m.sbuf(ring, f"w_hi{q}", [P, KT, P], F32R) for q in range(2)]
            m.w_lo = [m.sbuf(ring, f"w_lo{q}", [P, KT, P], F32R) for q in range(2)]
            m.q_in_gain = m.sbuf(ring, "q_in_gain", [P, KT])
            m.kv_in_gain = m.sbuf(ring, "kv_in_gain", [P, KT])
            with ExitStack() as mix:
                m.sq_sum = m.sbuf(mix, "mix_sq_sum", [P, T])
                out_projection(nc, m, dram, "mix_", dram.gated, dram.a_w_out, dram.resid, dram.resid_b, False)
            m.prefix = "b_"
            with ExitStack() as mla:
                m.c_hi = m.sbuf(mla, "c_hi", [P, KV_LORA // P, T + PAST], F32R, side="right")
                m.c_lo = m.sbuf(mla, "c_lo", [P, KV_LORA // P, T + PAST], F32R, side="right")
                m.rope_k_hi = m.sbuf(mla, "rope_k_hi", [P, T], F32R, side="right")
                m.rope_k_lo = m.sbuf(mla, "rope_k_lo", [P, T], F32R, side="right")
                m.rope_k32 = m.sbuf(mla, "rope_k32", [P, P + PAST], side="right")
                with ExitStack() as low:
                    m.ql_hi = m.sbuf(low, "ql_hi", [P, Q_LORA // P, T], F32R, side="right")
                    m.ql_lo = m.sbuf(low, "ql_lo", [P, Q_LORA // P, T], F32R, side="right")
                    m.q_factor = m.sbuf(low, "q_factor", [P, T], side="right")
                    m.cos = m.sbuf(low, "cos", [P, T], side="right")
                    m.sin = m.sbuf(low, "sin", [P, T], side="right")
                    latents(nc, m, dram)
                    ring.close()
                    m.mask_rows = m.sbuf(mla, "mask_rows", [P, 2 * P], BF16)
                    m.mask_big = m.sbuf(mla, "mask_big", [P, S9W // 2], BF16)
                    m.mask_first = m.mask_rows[:, 0:P]
                    m.mask_sample = m.mask_rows[:, 64 - N_SAMPLE:64 + N_META]
                    m.mask_meta = m.mask_rows[:, P - N_SAMPLE:P + N_META]
                    m.mask_all = m.mask_rows[:, P:2 * P]
                    m.kv_act_hi, m.kv_act_lo = m.c_hi, m.c_lo
                    m.kv_nat = m.sbuf(mla, "kv_nat", [P, NT + NC, 2 * DH])
                    m.kv_w_hi = m.sbuf(mla, "kv_w_hi", [P, KV_LORA // P, 2 * DH], F32R)
                    m.kv_w_lo = m.sbuf(mla, "kv_w_lo", [P, KV_LORA // P, 2 * DH], F32R)
                    m.g_hi_space = m.sbuf(mla, "g_hi_space", [P, QW], F32R)
                    m.g_lo_space = m.sbuf(mla, "g_lo_space", [P, QW], F32R)
                    m.stage_space = m.sbuf(mla, "stage_space", [P, T])
                    m.b_gain = m.sbuf(mla, "b_gain", [P, KT])
                    m.query_32 = m.sbuf(mla, "query_32", [P, T])
                    m.g_w_hi, m.g_w_lo, m.stage = (x[:, 0:KT * DH].rearrange("p (k n) -> p k n", n=DH)
                                                   for x in (m.g_hi_space, m.g_lo_space, m.stage_space))
                    queries(nc, m, dram)
                attention(nc, m, False, dram)
        m.stream = m.sbuf(whole, "stream", [P, KT, T])
        m.sq_sum = m.sbuf(whole, "sq_sum", [P, T])
        m.w_in = m.sbuf(whole, "w_in", [P, 2, KT, P])
        m.w_hi = [m.sbuf(whole, f"w_hi{q}", [P, KT, P], F32R) for q in range(2)]
        m.w_lo = [m.sbuf(whole, f"w_lo{q}", [P, KT, P], F32R) for q in range(2)]
        out_projection(nc, m, dram, "end_", dram.gated_b, dram.b_w_out, dram.resid_b, None, True)
        final_norm(nc, m, dram)


def constants():
    pos = np.concatenate([PAST + np.arange(N_SAMPLE), np.arange(L)]).astype(np.float32)
    half = ROPE // 2
    inv = (np.float32(10000.0) ** (-np.arange(half, dtype=np.float32) / np.float32(half))).astype(np.float32)
    ang = (inv[:, None] * pos[None, :]).astype(np.float32)
    rotate = np.zeros((P, P), np.float32)
    for r in range(half):
        for o in (0, ROPE):
            rotate[o + half + r, o + r] = -1.0
            rotate[o + r, o + half + r] = 1.0
    return {"ident": np.eye(P, dtype=np.float32), "rotate": rotate,
            "cos": np.tile(np.cos(ang).astype(np.float32), (4, 1)), "sin": np.tile(np.sin(ang).astype(np.float32), (4, 1))}


INPUTS = ["x_prompt", "x_sample", "cache_fox_k", "cache_fox_v", "cache_fox_logf", "cache_mla_ckv", "cache_mla_krope",
          "meta", "a_norm", "a_w_in", "a_b_forget", "a_w_out", "kv_norm", "w_dkv", "kv_lat_norm", "w_ukv", "b_norm",
          "b_w_in", "b_q_norm", "b_w_uq", "b_w_out", "final_norm"]
OUTPUTS = [(1, SEQ, D), (1, N_SAMPLE, D), (1, 1, L, HEADS, DH), (1, 1, L, HEADS, DH), (1, 1, L, HEADS), (1, L, KV_LORA),
           (1, L, ROPE), (1, 1, N_SAMPLE, HEADS, DH), (1, 1, N_SAMPLE, HEADS, DH), (1, 1, N_SAMPLE, HEADS),
           (1, N_SAMPLE, KV_LORA), (1, N_SAMPLE, ROPE)]


def laid_out(inputs):
    arrays = {n: np.asarray(inputs[n]) for n in INPUTS}
    for n in ("a_norm", "kv_norm", "kv_lat_norm", "b_norm", "b_q_norm"):
        arrays[n] = arrays[n].reshape(-1, P).T
    arrays["final_norm"] = arrays["final_norm"].reshape(1, D)
    arrays["a_b_forget"] = arrays["a_b_forget"].reshape(HEADS, 1)
    return {n: np.ascontiguousarray(x) for n, x in arrays.items()} | constants()


def kernel(**inputs):
    import concourse.bacc as bacc
    from concourse.bass_utils import run_bass_kernel_spmd

    nc = bacc.Bacc("TRN2", target_bir_lowering=False, num_devices=1)
    arrays = laid_out(inputs)
    a = {n: nc.dram_tensor(f"in_{n}", x.shape, F32, kind="ExternalInput").ap() for n, x in arrays.items()}
    outs = [nc.dram_tensor(f"out_{i}", s, F32, kind="ExternalOutput").ap() for i, s in enumerate(OUTPUTS)]
    build(nc, a, outs)
    r = run_bass_kernel_spmd(nc, [{f"in_{n}": x for n, x in arrays.items()}], core_ids=[0])
    return tuple(r.results[0][f"out_{i}"] for i in range(len(OUTPUTS)))
```
